# Optimizing a Trainium2 kernel written in Bass

```python
import math
import jax, jax.numpy as jnp
from jax import lax
import numpy as np
import jax
import jax.numpy as jnp

D_MODEL = 1024
BATCH = 1
SEQ = 256
DEPTH = 2

N_META = 16
BLOCK = 128
N_A_LAYERS = DEPTH // 2
N_B_LAYERS = DEPTH - N_A_LAYERS
CONV_WIDTH = 31
N_HEADS = 8
HEAD_DIM = D_MODEL // (2 * N_HEADS)
V_DIM = 2 * HEAD_DIM
ROT_DIM = HEAD_DIM // 4
ROPE_THETA = 500000.0
PEER_HEADS = 8
PEER_KEYS = 128
PEER_EXPERTS = PEER_KEYS * PEER_KEYS
PEER_HALF = 128
PEER_QDIM = 2 * PEER_HALF
PEER_TOPK = 16
PEER_CHUNK = 128
EPS = 1e-6


def rmsnorm(x, g):
    xf = x.astype(jnp.float32)
    y = xf * lax.rsqrt(jnp.mean(xf * xf, axis=-1, keepdims=True) + EPS)
    return (y * g.astype(jnp.float32)).astype(x.dtype)

def layernorm(x, g, b):
    xf = x.astype(jnp.float32)
    mu = jnp.mean(xf, axis=-1, keepdims=True)
    xc = xf - mu
    y = xc * lax.rsqrt(jnp.mean(xc * xc, axis=-1, keepdims=True) + EPS)
    return (y * g.astype(jnp.float32) + b.astype(jnp.float32)).astype(x.dtype)

def partial_rope(t, pos):
    inv = ROPE_THETA ** (-jnp.arange(0, ROT_DIM, 2, dtype=jnp.float32) / ROT_DIM)
    ang = pos.astype(jnp.float32)[:, None] * inv[None, :]
    cos = jnp.cos(ang)[None, :, None, None, :]
    sin = jnp.sin(ang)[None, :, None, None, :]
    tr = t[..., :ROT_DIM].astype(jnp.float32)
    t1, t2 = tr[..., :ROT_DIM // 2], tr[..., ROT_DIM // 2:]
    rot = jnp.concatenate([t1 * cos - t2 * sin, t1 * sin + t2 * cos], axis=-1).astype(t.dtype)
    return jnp.concatenate([rot, t[..., ROT_DIM:]], axis=-1)

def conformer_conv(h, w1, b1, dw_w, dw_b, ln_g, ln_b, w2, b2):
    u = h @ w1 + b1
    a, g = jnp.split(u, 2, axis=-1)
    u = a * jax.nn.sigmoid(g)
    u = lax.conv_general_dilated(
        u, dw_w[:, None, :], window_strides=(1,), padding=[(CONV_WIDTH - 1, 0)],
        dimension_numbers=('NWC', 'WIO', 'NWC'), feature_group_count=D_MODEL) + dw_b
    u = jax.nn.silu(layernorm(u, ln_g, ln_b))
    return u @ w2 + b2

def peer(h, wq, sk1, sk2, u_tab, v_tab):
    B, L, D = h.shape
    tok = h.reshape(-1, PEER_CHUNK, D)

    def chunk(xc):
        q = (xc @ wq).reshape(PEER_CHUNK, PEER_HEADS, 2, PEER_HALF)
        s1 = jnp.einsum('chd,kd->chk', q[:, :, 0], sk1)
        s2 = jnp.einsum('chd,kd->chk', q[:, :, 1], sk2)
        v1, i1 = lax.top_k(s1, PEER_TOPK)
        v2, i2 = lax.top_k(s2, PEER_TOPK)
        cand_s = (v1[..., :, None] + v2[..., None, :]).reshape(PEER_CHUNK, PEER_HEADS, PEER_TOPK * PEER_TOPK)
        cand_i = (i1[..., :, None] * PEER_KEYS + i2[..., None, :]).reshape(PEER_CHUNK, PEER_HEADS, PEER_TOPK * PEER_TOPK)
        top_s, top_pos = lax.top_k(cand_s, PEER_TOPK)
        expert = jnp.take_along_axis(cand_i, top_pos, axis=-1)
        gate = jax.nn.softmax(top_s.astype(jnp.float32), axis=-1).astype(xc.dtype)
        u = u_tab[expert]
        v = v_tab[expert]
        act = jax.nn.gelu(jnp.einsum('cd,chkd->chk', xc, u), approximate=False)
        return jnp.einsum('chk,chkd->cd', gate * act, v)

    return lax.map(chunk, tok).reshape(B, L, D)

def diff_attention(h, wq, k, v, lq1, lk1, lq2, lk2, subln_g, wo, lam_init, pos):
    B, L, D = h.shape
    q = (h @ wq).reshape(B, L, N_HEADS, 2, HEAD_DIM)
    q = partial_rope(q, pos) * (HEAD_DIM ** -0.5)
    lam = (jnp.exp(jnp.sum(lq1.astype(jnp.float32) * lk1.astype(jnp.float32)))
           - jnp.exp(jnp.sum(lq2.astype(jnp.float32) * lk2.astype(jnp.float32))) + lam_init)
    n_blk = L // BLOCK
    qb = q.reshape(B, n_blk, BLOCK, N_HEADS, 2, HEAD_DIM).transpose(1, 0, 2, 3, 4, 5)
    kpos = jnp.arange(L)

    def attend(args):
        qblk, bi = args
        s = jnp.einsum('bqhcd,bkhcd->bhcqk', qblk, k).astype(jnp.float32)
        qpos = bi * BLOCK + jnp.arange(BLOCK)
        mask = kpos[None, :] <= qpos[:, None]
        s = jnp.where(mask, s, -jnp.inf)
        p = jax.nn.softmax(s, axis=-1)
        a = p[:, :, 0] - lam * p[:, :, 1]
        return jnp.einsum('bhqk,bkhe->bqhe', a.astype(v.dtype), v)

    o = lax.map(attend, (qb, jnp.arange(n_blk)))
    o = o.transpose(1, 0, 2, 3, 4).reshape(B, L, N_HEADS, V_DIM)
    o = rmsnorm(o, subln_g) * (1.0 - lam_init)
    return o.reshape(B, L, N_HEADS * V_DIM) @ wo

def first_inputs(seed: int = 0) -> dict:
    key = jax.random.key(seed)
    ks = jax.random.split(key, 32)
    D = D_MODEL
    nrm = lambda k, shape, scale: jax.random.normal(k, shape, jnp.float32) * scale
    gain = lambda k, shape: 1.0 + 0.01 * jax.random.normal(k, shape, jnp.float32)
    return {
        "x": nrm(ks[0], (BATCH, SEQ, D), 1.0),
        "meta_tokens": nrm(ks[1], (N_META, D), 1.0),
        "a_norm_g": gain(ks[2], (N_A_LAYERS, D)),
        "a_pw1_w": nrm(ks[3], (N_A_LAYERS, D, 2 * D), D ** -0.5),
        "a_pw1_b": nrm(ks[4], (N_A_LAYERS, 2 * D), 0.01),
        "a_dw_w": nrm(ks[5], (N_A_LAYERS, CONV_WIDTH, D), CONV_WIDTH ** -0.5),
        "a_dw_b": nrm(ks[6], (N_A_LAYERS, D), 0.01),
        "a_ln_g": gain(ks[7], (N_A_LAYERS, D)),
        "a_ln_b": nrm(ks[8], (N_A_LAYERS, D), 0.01),
        "a_pw2_w": nrm(ks[9], (N_A_LAYERS, D, D), D ** -0.5),
        "a_pw2_b": nrm(ks[10], (N_A_LAYERS, D), 0.01),
        "kv_norm_g": gain(ks[11], (D,)),
        "w_kv": nrm(ks[12], (D, 2 * N_HEADS * HEAD_DIM + N_HEADS * V_DIM), D ** -0.5),
        "b_norm_g": gain(ks[13], (N_B_LAYERS, D)),
        "b_wq": nrm(ks[14], (N_B_LAYERS, D, 2 * N_HEADS * HEAD_DIM), D ** -0.5),
        "b_lambda_q1": nrm(ks[15], (N_B_LAYERS, HEAD_DIM), 0.1),
        "b_lambda_k1": nrm(ks[16], (N_B_LAYERS, HEAD_DIM), 0.1),
        "b_lambda_q2": nrm(ks[17], (N_B_LAYERS, HEAD_DIM), 0.1),
        "b_lambda_k2": nrm(ks[18], (N_B_LAYERS, HEAD_DIM), 0.1),
        "b_subln_g": gain(ks[19], (N_B_LAYERS, V_DIM)),
        "b_wo": nrm(ks[20], (N_B_LAYERS, N_HEADS * V_DIM, D), D ** -0.5),
        "f_norm_g": gain(ks[21], (DEPTH, D)),
        "f_wq": nrm(ks[22], (DEPTH, D, PEER_HEADS * PEER_QDIM), D ** -0.5),
        "f_subkey1": nrm(ks[23], (DEPTH, PEER_KEYS, PEER_HALF), PEER_HALF ** -0.5),
        "f_subkey2": nrm(ks[24], (DEPTH, PEER_KEYS, PEER_HALF), PEER_HALF ** -0.5),
        "f_u": nrm(ks[25], (DEPTH, PEER_EXPERTS, D), D ** -0.5),
        "f_v": nrm(ks[26], (DEPTH, PEER_EXPERTS, D), D ** -0.5),
        "final_norm_g": gain(ks[27], (D,)),
    }

def first_block(x, meta_tokens, a_norm_g, a_pw1_w, a_pw1_b, a_dw_w, a_dw_b, a_ln_g, a_ln_b,
              a_pw2_w, a_pw2_b, kv_norm_g, w_kv, b_norm_g, b_wq, b_lambda_q1, b_lambda_k1,
              b_lambda_q2, b_lambda_k2, b_subln_g, b_wo, f_norm_g, f_wq, f_subkey1, f_subkey2,
              f_u, f_v, final_norm_g):
    B, S, D = x.shape
    L = N_META + S
    Lp = -(-L // BLOCK) * BLOCK
    meta = jnp.broadcast_to(meta_tokens.astype(x.dtype)[None], (B, N_META, D))
    pad = jnp.zeros((B, Lp - L, D), x.dtype)
    h = jnp.concatenate([meta, x, pad], axis=1)
    pos = jnp.arange(Lp)
    k_shared = None
    v_shared = None
    for layer in range(DEPTH):
        if layer < N_A_LAYERS:
            i = layer
            h = h + conformer_conv(rmsnorm(h, a_norm_g[i]), a_pw1_w[i], a_pw1_b[i], a_dw_w[i],
                                   a_dw_b[i], a_ln_g[i], a_ln_b[i], a_pw2_w[i], a_pw2_b[i])
        else:
            j = layer - N_A_LAYERS
            lam_init = 0.8 - 0.6 * math.exp(-0.3 * layer)
            h = h + diff_attention(rmsnorm(h, b_norm_g[j]), b_wq[j], k_shared, v_shared,
                                   b_lambda_q1[j], b_lambda_k1[j], b_lambda_q2[j], b_lambda_k2[j],
                                   b_subln_g[j], b_wo[j], lam_init, pos)
        h = h + peer(rmsnorm(h, f_norm_g[layer]), f_wq[layer], f_subkey1[layer],
                     f_subkey2[layer], f_u[layer], f_v[layer])
        if layer == N_A_LAYERS - 1:
            kv = rmsnorm(h, kv_norm_g) @ w_kv
            k_flat, v_flat = jnp.split(kv, [2 * N_HEADS * HEAD_DIM], axis=-1)
            k_shared = partial_rope(k_flat.reshape(B, Lp, N_HEADS, 2, HEAD_DIM), pos)
            v_shared = v_flat.reshape(B, Lp, N_HEADS, V_DIM)
    out = rmsnorm(h, final_norm_g)
    return out[:, N_META:N_META + S]


N_MIXERS = 3
HEAD_DIM_2 = 64
N_HEADS_2 = D_MODEL // HEAD_DIM_2
D_FF = 4 * D_MODEL
ROPE_THETA_2 = 10000.0
NORM_EPS = 1e-6
NEG_INF = -1e30
NSA_KV_GROUPS = 4
NSA_CMP_LEN = 32
NSA_CMP_STRIDE = 16
NSA_CMP_HIDDEN = 4 * HEAD_DIM_2
NSA_SEL_LEN = 64
NSA_TOP_N = 16
NSA_WINDOW = 512
NSA_SEL_QBLOCK = 32
NSA_FORCE_BONUS = 1000.0
FOX_QBLOCK = 128
SWA_KV_HEADS = 2
SWA_WINDOW = 128
BAND_QBLOCK = 128
N_LAYERS_A = len(range(0, DEPTH, N_MIXERS))
N_LAYERS_B = len(range(1, DEPTH, N_MIXERS))
N_LAYERS_C = len(range(2, DEPTH, N_MIXERS))


def rms_norm(x, g):
    xf = x.astype(jnp.float32)
    y = xf * lax.rsqrt(jnp.mean(xf * xf, axis=-1, keepdims=True) + NORM_EPS)
    return (y * g.astype(jnp.float32)).astype(x.dtype)

def rope_tables(seq):
    inv = ROPE_THETA_2 ** (-jnp.arange(0, HEAD_DIM_2, 2, dtype=jnp.float32) / HEAD_DIM_2)
    ang = jnp.arange(seq, dtype=jnp.float32)[:, None] * inv[None, :]
    return jnp.cos(ang), jnp.sin(ang)

def apply_rope(x, cos, sin):
    xf = x.astype(jnp.float32)
    x1, x2 = jnp.split(xf, 2, axis=-1)
    c = cos[None, :, None, :]
    s = sin[None, :, None, :]
    return jnp.concatenate([x1 * c - x2 * s, x2 * c + x1 * s], axis=-1).astype(x.dtype)

def banded_attention(q, k, v, window, sinks=None):
    B, T, H, dh = q.shape
    G = k.shape[2]
    rep = H // G
    blk = BAND_QBLOCK
    nb = T // blk
    span = blk + window
    scale = dh ** -0.5
    kp = jnp.pad(k, ((0, 0), (window, 0), (0, 0), (0, 0)))
    vp = jnp.pad(v, ((0, 0), (window, 0), (0, 0), (0, 0)))
    qc = q.reshape(B, nb, blk, G, rep, dh).transpose(1, 0, 2, 3, 4, 5)
    offs_q = jnp.arange(blk)
    offs_k = jnp.arange(span) - window

    def one(args):
        i, qi = args
        start = i * blk
        kc = lax.dynamic_slice_in_dim(kp, start, span, axis=1)
        vc = lax.dynamic_slice_in_dim(vp, start, span, axis=1)
        qpos = start + offs_q
        kpos = start + offs_k
        dist = qpos[:, None] - kpos[None, :]
        valid = (kpos[None, :] >= 0) & (dist >= 0) & (dist < window)
        s = jnp.einsum('bqgrd,bkgd->bgrqk', qi, kc).astype(jnp.float32) * scale
        s = jnp.where(valid, s, NEG_INF)
        if sinks is None:
            p = jax.nn.softmax(s, axis=-1)
        else:
            sink = jnp.broadcast_to(sinks.astype(jnp.float32).reshape(G, rep)[None, :, :, None, None],
                                    (B, G, rep, blk, 1))
            p = jax.nn.softmax(jnp.concatenate([s, sink], axis=-1), axis=-1)[..., :-1]
        return jnp.einsum('bgrqk,bkgd->bqgrd', p.astype(vc.dtype), vc)

    out = lax.map(one, (jnp.arange(nb), qc))
    return out.transpose(1, 0, 2, 3, 4, 5).reshape(B, T, H, dh)

def nsa_compress(tok, pos, w1, w2):
    B, T, G, dh = tok.shape
    nc = (T - NSA_CMP_LEN) // NSA_CMP_STRIDE + 1
    idx = np.arange(nc)[:, None] * NSA_CMP_STRIDE + np.arange(NSA_CMP_LEN)[None, :]
    win = tok[:, idx] + pos[:, None, :].astype(tok.dtype)
    win = win.transpose(0, 1, 3, 2, 4).reshape(B, nc, G, NSA_CMP_LEN * dh)
    return jax.nn.silu(win @ w1) @ w2

def nsa_selected_attention(qg, k, v, sel):
    B, T, G, rep, dh = qg.shape
    ns = T // NSA_SEL_LEN
    n = sel.shape[-1]
    qb = NSA_SEL_QBLOCK
    nq = T // qb
    scale = dh ** -0.5
    kb = k.reshape(B, ns, NSA_SEL_LEN, G, dh).transpose(0, 3, 1, 2, 4)
    vb = v.reshape(B, ns, NSA_SEL_LEN, G, dh).transpose(0, 3, 1, 2, 4)
    qc = qg.reshape(B, nq, qb, G, rep, dh).transpose(1, 0, 2, 3, 4, 5)
    sc = sel.reshape(B, G, nq, qb, n).transpose(2, 0, 1, 3, 4)
    gather = jax.vmap(jax.vmap(lambda tab, ix: tab[ix]))
    offs = jnp.arange(NSA_SEL_LEN)

    def one(args):
        i, qi, si = args
        gk = gather(kb, si).reshape(B, G, qb, n * NSA_SEL_LEN, dh)
        gv = gather(vb, si).reshape(B, G, qb, n * NSA_SEL_LEN, dh)
        kpos = (si[..., None] * NSA_SEL_LEN + offs).reshape(B, G, qb, n * NSA_SEL_LEN)
        qpos = i * qb + jnp.arange(qb)
        valid = kpos <= qpos[None, None, :, None]
        s = jnp.einsum('bqgrd,bgqkd->bgrqk', qi, gk).astype(jnp.float32) * scale
        s = jnp.where(valid[:, :, None], s, NEG_INF)
        p = jax.nn.softmax(s, axis=-1)
        return jnp.einsum('bgrqk,bgqkd->bqgrd', p.astype(gv.dtype), gv)

    out = lax.map(one, (jnp.arange(nq), qc, sc))
    return out.transpose(1, 0, 2, 3, 4, 5).reshape(B, T, G * rep, dh)

def nsa_mixer(h, w_in, cmp_pos, cmp_w1, cmp_w2, w_out, cos, sin):
    B, T, _ = h.shape
    H, G, dh = N_HEADS_2, NSA_KV_GROUPS, HEAD_DIM_2
    rep = H // G
    kvw = G * dh
    scale = dh ** -0.5
    proj = h @ w_in
    sizes = [H * dh, kvw, kvw, kvw, kvw, kvw, kvw, 3 * H]
    cuts = np.cumsum(sizes)[:-1].tolist()
    q, kc_t, vc_t, ks, vs, kw, vw, gate = jnp.split(proj, cuts, axis=-1)
    q = apply_rope(q.reshape(B, T, H, dh), cos, sin)
    kc_t = apply_rope(kc_t.reshape(B, T, G, dh), cos, sin)
    ks = apply_rope(ks.reshape(B, T, G, dh), cos, sin)
    kw = apply_rope(kw.reshape(B, T, G, dh), cos, sin)
    vc_t = vc_t.reshape(B, T, G, dh)
    vs = vs.reshape(B, T, G, dh)
    vw = vw.reshape(B, T, G, dh)
    qg = q.reshape(B, T, G, rep, dh)
    tpos = jnp.arange(T)

    kcmp = nsa_compress(kc_t, cmp_pos[0], cmp_w1[0], cmp_w2[0])
    vcmp = nsa_compress(vc_t, cmp_pos[1], cmp_w1[1], cmp_w2[1])
    nc = kcmp.shape[1]
    s = jnp.einsum('btgrd,bcgd->bgrtc', qg, kcmp).astype(jnp.float32) * scale
    cend = jnp.arange(nc) * NSA_CMP_STRIDE + NSA_CMP_LEN - 1
    cvalid = cend[None, :] <= tpos[:, None]
    p_cmp = jax.nn.softmax(jnp.where(cvalid, s, NEG_INF), axis=-1)
    p_cmp = jnp.where((tpos >= NSA_CMP_LEN - 1)[:, None], p_cmp, 0.0)
    o_cmp = jnp.einsum('bgrtc,bcgd->btgrd', p_cmp.astype(vcmp.dtype), vcmp).reshape(B, T, H, dh)

    ns = T // NSA_SEL_LEN
    c_lo = np.arange(nc)[:, None] * NSA_CMP_STRIDE
    s_lo = np.arange(ns)[None, :] * NSA_SEL_LEN
    ov = np.clip(np.minimum(c_lo + NSA_CMP_LEN, s_lo + NSA_SEL_LEN) - np.maximum(c_lo, s_lo), 0, None)
    overlap = jnp.asarray(ov.astype(np.float32) / NSA_CMP_LEN)
    imp = jnp.einsum('bgrtc,cn->bgtn', p_cmp, overlap)
    tblk = tpos // NSA_SEL_LEN
    j = jnp.arange(ns)
    forced = (j[None, :] == 0) | (j[None, :] == tblk[:, None]) | (j[None, :] == tblk[:, None] - 1)
    bvalid = j[None, :] <= tblk[:, None]
    score = jnp.where(bvalid, imp + jnp.where(forced, NSA_FORCE_BONUS, 0.0), -1.0)
    n_top = min(NSA_TOP_N, ns)
    _, sel = lax.top_k(score, n_top)

    o_slc = nsa_selected_attention(qg, ks, vs, sel)
    o_win = banded_attention(q, kw, vw, NSA_WINDOW)

    g = jax.nn.sigmoid(gate.astype(jnp.float32)).reshape(B, T, H, 3)
    o = g[..., 0:1] * o_cmp + g[..., 1:2] * o_slc + g[..., 2:3] * o_win
    return o.astype(h.dtype).reshape(B, T, H * dh) @ w_out

def fox_attention(q, k, v, logf):
    B, T, H, dh = q.shape
    blk = FOX_QBLOCK
    nb = T // blk
    scale = dh ** -0.5
    c = jnp.cumsum(logf, axis=1).transpose(0, 2, 1)
    outs = []
    for i in range(nb):
        lo, hi = i * blk, (i + 1) * blk
        s = jnp.einsum('bqhd,bkhd->bhqk', q[:, lo:hi], k[:, :hi]).astype(jnp.float32) * scale
        s = s + c[:, :, lo:hi, None] - c[:, :, None, :hi]
        causal = jnp.arange(lo, hi)[:, None] >= jnp.arange(hi)[None, :]
        p = jax.nn.softmax(jnp.where(causal, s, NEG_INF), axis=-1)
        outs.append(jnp.einsum('bhqk,bkhd->bqhd', p.astype(v.dtype), v[:, :hi]))
    return jnp.concatenate(outs, axis=1)

def fox_mixer(h, w_in, b_f, w_out):
    B, T, _ = h.shape
    H, dh = N_HEADS_2, HEAD_DIM_2
    proj = h @ w_in
    q, k, v, fl = jnp.split(proj, [H * dh, 2 * H * dh, 3 * H * dh], axis=-1)
    logf = jax.nn.log_sigmoid(fl.astype(jnp.float32) + b_f.astype(jnp.float32))
    o = fox_attention(q.reshape(B, T, H, dh), k.reshape(B, T, H, dh), v.reshape(B, T, H, dh), logf)
    return o.reshape(B, T, H * dh) @ w_out

def swa_mixer(h, w_in, b_in, sinks, w_out, b_out, cos, sin):
    B, T, _ = h.shape
    H, G, dh = N_HEADS_2, SWA_KV_HEADS, HEAD_DIM_2
    proj = h @ w_in + b_in
    q, k, v = jnp.split(proj, [H * dh, H * dh + G * dh], axis=-1)
    q = apply_rope(q.reshape(B, T, H, dh), cos, sin)
    k = apply_rope(k.reshape(B, T, G, dh), cos, sin)
    o = banded_attention(q, k, v.reshape(B, T, G, dh), SWA_WINDOW, sinks)
    return o.reshape(B, T, H * dh) @ w_out + b_out

def squared_relu_mlp(h, w_up, w_down):
    return jnp.square(jax.nn.relu(h @ w_up)) @ w_down

def second_inputs(seed: int = 0) -> dict:
    key = jax.random.key(seed)
    ks = jax.random.split(key, 20)
    D, H, dh = D_MODEL, N_HEADS_2, HEAD_DIM_2
    f32 = jnp.float32
    nsa_in_w = H * dh + 6 * NSA_KV_GROUPS * dh + 3 * H
    fox_in_w = 3 * H * dh + H
    swa_in_w = H * dh + 2 * SWA_KV_HEADS * dh
    cmp_in = NSA_CMP_LEN * dh
    nrm = lambda k, shape, fan: jax.random.normal(k, shape, f32) * (fan ** -0.5)
    return {
        'x': jax.random.normal(ks[0], (BATCH, SEQ, D), f32),
        'norm_g': 1.0 + 0.02 * jax.random.normal(ks[1], (DEPTH, 4, D), f32),
        'mlp_w_up': nrm(ks[2], (DEPTH, D, D_FF), D),
        'mlp_w_down': nrm(ks[3], (DEPTH, D_FF, D), D_FF),
        'nsa_w_in': nrm(ks[4], (N_LAYERS_A, D, nsa_in_w), D),
        'nsa_cmp_pos': 0.2 * jax.random.normal(ks[5], (N_LAYERS_A, 2, NSA_CMP_LEN, dh), f32),
        'nsa_cmp_w1': nrm(ks[6], (N_LAYERS_A, 2, cmp_in, NSA_CMP_HIDDEN), cmp_in),
        'nsa_cmp_w2': nrm(ks[7], (N_LAYERS_A, 2, NSA_CMP_HIDDEN, dh), NSA_CMP_HIDDEN),
        'nsa_w_out': nrm(ks[8], (N_LAYERS_A, H * dh, D), H * dh),
        'fox_w_in': nrm(ks[9], (N_LAYERS_B, D, fox_in_w), D),
        'fox_b_f': jax.random.uniform(ks[10], (N_LAYERS_B, H), f32, 1.0, 5.0),
        'fox_w_out': nrm(ks[11], (N_LAYERS_B, H * dh, D), H * dh),
        'swa_w_in': nrm(ks[12], (N_LAYERS_C, D, swa_in_w), D),
        'swa_b_in': 0.02 * jax.random.normal(ks[13], (N_LAYERS_C, swa_in_w), f32),
        'swa_sinks': jax.random.normal(ks[14], (N_LAYERS_C, H), f32),
        'swa_w_out': nrm(ks[15], (N_LAYERS_C, H * dh, D), H * dh),
        'swa_b_out': 0.02 * jax.random.normal(ks[16], (N_LAYERS_C, D), f32),
    }

def second_block(x, norm_g, mlp_w_up, mlp_w_down, nsa_w_in, nsa_cmp_pos, nsa_cmp_w1, nsa_cmp_w2, nsa_w_out,
              fox_w_in, fox_b_f, fox_w_out, swa_w_in, swa_b_in, swa_sinks, swa_w_out, swa_b_out):
    T = x.shape[1]
    cos, sin = rope_tables(T)
    for i in range(DEPTH):
        kind = i % N_MIXERS
        slot = i // N_MIXERS
        h = rms_norm(x, norm_g[i, 0])
        if kind == 0:
            m = nsa_mixer(h, nsa_w_in[slot], nsa_cmp_pos[slot], nsa_cmp_w1[slot], nsa_cmp_w2[slot],
                          nsa_w_out[slot], cos, sin)
        elif kind == 1:
            m = fox_mixer(h, fox_w_in[slot], fox_b_f[slot], fox_w_out[slot])
        else:
            m = swa_mixer(h, swa_w_in[slot], swa_b_in[slot], swa_sinks[slot], swa_w_out[slot],
                          swa_b_out[slot], cos, sin)
        x = x + rms_norm(m, norm_g[i, 1])
        h = rms_norm(x, norm_g[i, 2])
        x = x + rms_norm(squared_relu_mlp(h, mlp_w_up[i], mlp_w_down[i]), norm_g[i, 3])
    return x


def setup_inputs(seed=0):
    out = dict(first_inputs(seed))
    for name, value in second_inputs(seed + 1).items():
        if name != "x":
            out[name + "_2"] = value
    return out


def reference(
    x, meta_tokens, a_norm_g, a_pw1_w, a_pw1_b, a_dw_w, a_dw_b, a_ln_g, a_ln_b, a_pw2_w,
    a_pw2_b, kv_norm_g, w_kv, b_norm_g, b_wq, b_lambda_q1, b_lambda_k1, b_lambda_q2,
    b_lambda_k2, b_subln_g, b_wo, f_norm_g, f_wq, f_subkey1, f_subkey2, f_u, f_v, final_norm_g,
    norm_g_2, mlp_w_up_2, mlp_w_down_2, nsa_w_in_2, nsa_cmp_pos_2, nsa_cmp_w1_2, nsa_cmp_w2_2,
    nsa_w_out_2, fox_w_in_2, fox_b_f_2, fox_w_out_2, swa_w_in_2, swa_b_in_2, swa_sinks_2,
    swa_w_out_2, swa_b_out_2,
):
    x = first_block(
        x, meta_tokens, a_norm_g, a_pw1_w, a_pw1_b, a_dw_w, a_dw_b, a_ln_g, a_ln_b, a_pw2_w,
        a_pw2_b, kv_norm_g, w_kv, b_norm_g, b_wq, b_lambda_q1, b_lambda_k1, b_lambda_q2,
        b_lambda_k2, b_subln_g, b_wo, f_norm_g, f_wq, f_subkey1, f_subkey2, f_u, f_v,
        final_norm_g,
    )
    return second_block(
        x, norm_g_2, mlp_w_up_2, mlp_w_down_2, nsa_w_in_2, nsa_cmp_pos_2, nsa_cmp_w1_2,
        nsa_cmp_w2_2, nsa_w_out_2, fox_w_in_2, fox_b_f_2, fox_w_out_2, swa_w_in_2, swa_b_in_2,
        swa_sinks_2, swa_w_out_2, swa_b_out_2,
    )


_drawn_inputs = setup_inputs


def setup_inputs(seed=0):
    import zlib

    import numpy as np

    out = dict(_drawn_inputs(seed))
    spreads = {}
    factors = {'a_norm_g': 8.0,
     'a_pw1_b': 3.706,
     'a_ln_g': 5.103,
     'a_ln_b': 3.687,
     'kv_norm_g': 6.938,
     'b_norm_g': 8.0,
     'b_lambda_k2': 3.258,
     'b_subln_g': 7.771,
     'f_norm_g': 8.0,
     'f_wq': 3.143,
     'f_subkey1': 3.248,
     'f_subkey2': 3.227,
     'f_u': 3.524,
     'f_v': 3.118,
     'final_norm_g': 5.728}
    for name, (base, spread) in spreads.items():
        noise = np.random.default_rng([zlib.crc32(name.encode()), seed]).standard_normal(out[name].shape)
        drawn = base * np.exp(spread * noise) if base else spread * noise
        out[name] = jnp.asarray(drawn.astype(out[name].dtype))
    for name, factor in factors.items():
        out[name] = (out[name] * factor).astype(out[name].dtype)
    return out
```

```python
from contextlib import ExitStack

import numpy as np

import concourse.bass as bass
from concourse import mybir

F32 = mybir.dt.float32
U32 = mybir.dt.uint32
I32 = mybir.dt.int32
ALU = mybir.AluOpType
ACT = mybir.ActivationFunctionType
AX_X = mybir.AxisListType.X

P = 128
D = 1024
NC = D // P
META = 16
SEQ = 256
T0 = META + SEQ
NT = SEQ // P
CONV_W = 31
EPS = 1e-6
HEADS = 8
TOPK = 16
KEYS = 128
LAM_INIT = float(0.8 - 0.6 * np.exp(-0.3 * 1))
NEG = -1e30
LOWEST = -3e38
CHUNK_SLOTS = 8
FFC = 4096 // P
CMP_L, CMP_STEP = 32, 16
NCMP = (SEQ - CMP_L) // CMP_STEP + 1
GROUPS = 4
SCALE = 0.125
ARENA = T0 * KEYS

CAND_ROWS = [(0, 1, 16), (1, 1, 8), (2, 1, 5), (3, 1, 4), (4, 1, 3), (5, 3, 2), (8, 8, 1)]
NCAND = sum(na * nb for _, na, nb in CAND_ROWS)

VEC_LIST = [("a_norm_g", 1), ("a_pw1_b", 2), ("a_dw_w", CONV_W), ("a_dw_b", 1), ("a_ln_g", 1), ("a_ln_b", 1),
            ("a_pw2_b", 1), ("kv_norm_g", 1), ("b_norm_g", 1), ("f_norm_g", 2), ("final_norm_g", 1), ("norm_g_2", 8)]
VEC = {}
_at = 0
for _name, _n in VEC_LIST:
    VEC[_name] = _at
    _at += NC * _n
NVEC = _at

CONST_A = [("ident", P), ("ones", P), ("iota", P), ("iota_cand", 64)]
CONST_B = [("rope_mat", P), ("rope_cos", T0), ("rope_sin", T0), ("tri", P)]
CONST_C = [("rope_mat", P), ("rope_cos", SEQ), ("rope_sin", SEQ), ("tri", P), ("cmp_mask", NT * 16), ("row_ok", 2),
           ("head_sel", 16 * SEQ)]

STAGES = [
    ("norm", dict(gain="a_norm_g", gi=0, tokens=T0)),
    ("conv_in", dict(chunks=16)),
    ("layernorm", dict()),
    ("proj_add", dict(chunks=8, src="xn", bias=True, tokens=T0)),
    ("norm", dict(gain="f_norm_g", gi=0, tokens=T0)),
    ("peer_query", dict(chunks=16, layer=0, tokens=T0)),
    ("peer_topk", dict(layer=0, tokens=T0)),
    ("peer_gates", dict(layer=0, tokens=T0)),
    ("dense", dict(chunks=2 * KEYS, what="peer", tokens=T0, n=KEYS)),
    ("norm", dict(gain="kv_norm_g", gi=0, tokens=T0)),
    ("kv_proj", dict(chunks=16)),
    ("norm", dict(gain="b_norm_g", gi=0, tokens=SEQ)),
    ("q_proj", dict(chunks=8)),
    ("diff_attn", dict()),
    ("subln", dict()),
    ("turn_out", dict()),
    ("proj_add", dict(chunks=8, src="ot", bias=False, tokens=SEQ)),
    ("norm", dict(gain="f_norm_g", gi=1, tokens=SEQ)),
    ("peer_query", dict(chunks=16, layer=1, tokens=SEQ)),
    ("peer_topk", dict(layer=1, tokens=SEQ)),
    ("peer_gates", dict(layer=1, tokens=SEQ)),
    ("dense", dict(chunks=2 * KEYS, what="peer", tokens=SEQ, n=KEYS)),
    ("norm", dict(gain="final_norm_g", gi=0, tokens=SEQ, into="h")),
    ("norm", dict(gain="norm_g_2", gi=0, tokens=SEQ)),
    ("nsa_proj", dict(chunks=20)),
    ("nsa_compress", dict(chunks=8)),
    ("nsa_attn", dict()),
    ("turn_out", dict()),
    ("proj_keep", dict(chunks=8)),
    ("norm", dict(gain="norm_g_2", gi=1, tokens=SEQ, into="add")),
    ("norm", dict(gain="norm_g_2", gi=2, tokens=SEQ)),
    ("dense", dict(chunks=2 * FFC, what="mlp", tokens=SEQ, n=FFC)),
    ("norm", dict(gain="norm_g_2", gi=3, tokens=SEQ, into="add")),
    ("norm", dict(gain="norm_g_2", gi=4, tokens=SEQ)),
    ("fox_proj", dict(chunks=24)),
    ("fox_attn", dict()),
    ("turn_out", dict()),
    ("proj_keep", dict(chunks=8)),
    ("norm", dict(gain="norm_g_2", gi=5, tokens=SEQ, into="add")),
    ("norm", dict(gain="norm_g_2", gi=6, tokens=SEQ)),
    ("dense", dict(chunks=2 * FFC, what="mlp", tokens=SEQ, n=FFC)),
    ("norm", dict(gain="norm_g_2", gi=7, tokens=SEQ, into="add")),
]


def lay_out_stages():
    out, n, seen = [], 0, {}
    bank_frees = rope_chunks = dense_steps = units = peer_tiles = gate_groups = 0
    for at, (kind, q) in enumerate(STAGES):
        s = dict(q, kind=kind, at=at, n0=n, k=seen.get(kind, 0), bf0=bank_frees, r0=rope_chunks, d0=dense_steps,
                 u0=units, pt0=peer_tiles, gg0=gate_groups)
        seen[kind] = s["k"] + 1
        n += q.get("chunks", 0)
        bank_frees += {"proj_add": 8, "proj_keep": 8, "peer_query": 16, "fox_proj": 16}.get(kind, 0)
        rope_chunks += {"kv_proj": 8, "q_proj": 8, "nsa_proj": 14}.get(kind, 0)
        dense_steps += q["n"] if kind == "dense" else 0
        units += {"diff_attn": 16, "nsa_attn": 32, "fox_attn": 16}.get(kind, 0)
        if kind == "peer_topk":
            peer_tiles += len(peer_token_tiles(q["tokens"]))
        if kind == "peer_gates":
            gate_groups += q["tokens"] // 4
        out.append(s)
    return out


def peer_token_tiles(tokens):
    meta = tokens - SEQ
    return [(meta + P * i, P) for i in range(NT)] + ([(0, meta)] if meta else [])


def build_program(nc, dram, out):
    stages = lay_out_stages()
    with ExitStack() as ctx:
        def sb(name, shape, dt=F32):
            return ctx.enter_context(nc.sbuf_tensor(name, shape, dt))

        def sem(name):
            return ctx.enter_context(nc.semaphore(name))

        h = sb("h", [P, NC, T0])
        xn = sb("xn", [P, NC, T0])
        ring = sb("ring", [P, CHUNK_SLOTS, D])
        vecs = sb("vecs", [P, NVEC])
        const_a = sb("const_a", [P, sum(n for _, n in CONST_A)])
        work = sb("work", [P, 2048])
        pick = sb("pick", [P, 3, T0])
        subkeys = sb("subkeys", [P, 4, KEYS])
        gate_w = sb("gate_w", [P, NC, 48])
        forget_w = sb("forget_w", [P, NC, 16])
        small = sb("small", [P, 96])
        arena = sb("arena", [P, ARENA])
        banks = ctx.enter_context(nc.psum_tensor("banks", [P, 8, 512], F32))

        cols = {}
        at = 0
        for name, n in CONST_A:
            cols[name] = const_a[:, at:at + n]
            at += n
        ident, ones, iota, iota_cand = cols["ident"], cols["ones"], cols["iota"], cols["iota_cand"][:, 0:NCAND]

        class Carve:

            def __init__(self, at=0):
                self.at = at

            def __call__(self, *dims, dt=None):
                n = int(np.prod(dims))
                v = arena[:, self.at:self.at + n]
                self.at += n
                assert self.at <= ARENA
                if dt is not None:
                    v = v.bitcast(dt)
                if len(dims) == 2:
                    v = v.rearrange("p (a b) -> p a b", b=dims[1])
                if len(dims) == 3:
                    v = v.rearrange("p (a b c) -> p a b c", b=dims[1], c=dims[2])
                return v

        top = Carve(ARENA - (NC * T0 + 3 * T0))
        squares = top(NC, T0)
        root, rstd, mean = top(T0), top(T0), top(T0)
        cv = Carve()
        glu_u = cv(NC, CONV_W - 1 + T0)
        conv_y = cv(NC, T0)
        conv_odd = cv(NC, T0)
        glu_sig = cv(2, T0)
        products = cv(4, T0)
        pv = Carve()
        peer_q = pv(16, T0)
        tk = dict(vals=pv(16, 16), idx=pv(16, 16, dt=U32), idxf=pv(16, 16), rest=pv(16, KEYS),
                  cand=pv(HEADS, NCAND), cand_rest=pv(HEADS, NCAND), code=pv(HEADS, NCAND), best=pv(HEADS, TOPK),
                  pos=pv(HEADS, TOPK, dt=U32), posf=pv(HEADS, TOPK), hit=pv(HEADS * TOPK, NCAND),
                  picked=pv(P), pickedi=pv(P, dt=I32), k1i=pv(P, dt=I32), k2i=pv(P, dt=I32),
                  k1=pv(P), k2=pv(P), ex=pv(HEADS, TOPK), tot=pv(HEADS), inv=pv(HEADS), gate=pv(HEADS, TOPK))
        spread = arena[:, :].rearrange("p (t k) -> p t k", k=KEYS)
        onehot1 = work[:, 0:1024].rearrange("p (a t k) -> p a t k", a=2, t=4)
        onehot2 = work[:, 1024:2048].rearrange("p (a t k) -> p a t k", a=2, t=4)
        act_out = work[:, 0:2 * T0].rearrange("p (a t) -> p a t", a=2)
        act_gated = work[:, 2 * T0:4 * T0].rearrange("p (a t) -> p a t", a=2)
        av = Carve()
        qT = av(NC, SEQ)
        kT = av(NC, T0)
        v_tok = av(3, D)
        raw = av(2, T0)
        rot = av(2, T0)
        probs = av(2, 3 * T0)
        probsT = av(2, 1024)
        o_tok = av(NT, D)
        oT = av(NC, SEQ)
        o_sq = av(NT, D)
        mo = o_sq.rearrange("p t n -> p (t n)").rearrange("p (c t) -> p c t", c=NC)
        cb_at = av.at
        const_b = av(sum(n for _, n in CONST_B))
        lam_vecs = av(4, 64)
        subln_gain = av(P)
        lam_tmp = av(2, 64)
        set_b = {}
        at = cb_at
        for name, n in CONST_B:
            set_b[name] = arena[:, at:at + n]
            at += n
        cc = Carve(cb_at)
        cc_at = cc.at
        const_c = cc(sum(n for _, n in CONST_C))
        set_c = {}
        at = cc_at
        for name, n in CONST_C:
            set_c[name] = arena[:, at:at + n]
            at += n
        head_sel = set_c["head_sel"].rearrange("p (h t) -> p h t", t=SEQ)
        cmp_w2 = cc(2, 2, 64)
        cmp_w2d = cc(2, P)
        cmp_pos = cc(2, 2, 16)
        forget_b = cc(2)
        kcT, ksT, kwT, vcT = (cc(2, SEQ) for _ in range(4))
        blocks = [cc(16, GROUPS * NCMP) for _ in range(2)]
        hid = cc(2 * 2, 64)
        kcmpT = cc(64)
        vcmp = cc(GROUPS, 64)
        gates = cc(NT, 48)
        fz = cc(6, SEQ)
        o_mix_at = cc(2 * P)
        assert cc.at <= ARENA - (NC * T0 + 3 * T0)

        eps = small[:, 0:1]
        lam_sum, lam_exp, neg_lam = small[:, 2:4], small[:, 4:6], small[:, 6:7]
        row_max = small[:, 8:16].rearrange("p (a m) -> p a m", a=2)
        neg_max = small[:, 16:24].rearrange("p (a m) -> p a m", a=2)
        row_sum = small[:, 24:36].rearrange("p (a m) -> p a m", a=3)
        coef = small[:, 36:44].rearrange("p (a m) -> p a m", a=2)
        sub_ss, sub_root, sub_rstd = (small[:, 44 + 16 * i:60 + 16 * i] for i in range(3))
        o_mix = o_mix_at.rearrange("p (a b c) -> p a b c", a=1, b=2)

        chunk_landed = [sem(f"chunk_landed{i}") for i in range(CHUNK_SLOTS)]
        chunk_used = sem("chunk_used")
        inputs_landed = sem("inputs_landed")
        consts_b_landed = sem("consts_b_landed")
        consts_c_landed = sem("consts_c_landed")
        out_stored = sem("out_stored")
        stage_done = sem("stage_done")
        set_up = sem("set_up")
        dve_step = sem("dve_step")
        pool_step = sem("pool_step")
        act_step = sem("act_step")
        squares_ready, sum_ready, root_ready, rstd_ready = (sem(n) for n in (
            "squares_ready", "sum_ready", "root_ready", "rstd_ready"))
        bank_free = sem("bank_free")
        glu_gate_ready, glu_done, taps_ready = sem("glu_gate_ready"), sem("glu_done"), sem("taps_ready")
        product_ready = sem("product_ready")
        mean_summed, centred, var_summed, ln_root_ready, ln_scaled = (sem(n) for n in (
            "mean_summed", "centred", "var_summed", "ln_root_ready", "ln_scaled"))
        raw_ready, rot_ready, cos_ready, rope_done = (sem(n) for n in ("raw_ready", "rot_ready", "cos_ready", "rope_done"))
        tile_scores, index_ready, codes_ready, tops_ready, exps_ready, tile_picks, picks_turned, picks_stored = (
            sem(n) for n in ("tile_scores", "index_ready", "codes_ready", "tops_ready", "exps_ready", "tile_picks",
                             "picks_turned", "picks_stored"))
        onehots_ready, spread_summed, spread_stored = (sem(n) for n in (
            "onehots_ready", "spread_summed", "spread_stored"))
        act_ready, gated_ready = sem("act_ready"), sem("gated_ready")
        scores_ready, max_ready, exp_done, turned, turned_stored, av_done, mixed = (sem(n) for n in (
            "scores_ready", "max_ready", "exp_done", "turned", "turned_stored", "av_done", "mixed"))
        out_turned, out_turned_stored = sem("out_turned"), sem("out_turned_stored")
        sub_squared, sub_root_ready = sem("sub_squared"), sem("sub_root_ready")
        lam_exps = sem("lam_exps")
        lam_sums = sem("lam_sums")
        gates_summed = sem("gates_summed")
        cmp_blocks_ready = [sem("cmp_keys_ready"), sem("cmp_values_ready")]
        cmp_hidden_ready, cmp_out_summed = sem("cmp_hidden_ready"), sem("cmp_out_summed")
        forget_summed, forget_parts, forget_abs = sem("forget_summed"), sem("forget_parts"), sem("forget_abs")

        block = ctx.enter_context(nc.Block())

        def vec(name, i, c):
            n = VEC[name] + NC * i + c
            return vecs[:, n:n + 1]

        def slot_of(n):
            return n % CHUNK_SLOTS

        def tok_slice(tokens):
            return slice(T0 - tokens, T0)

        class Steps:

            def __init__(self, eng, sem_):
                self.eng, self.sem, self.n = eng, sem_, 0

            def mark(self, ins):
                ins.then_inc(self.sem, 1)
                self.n += 1
                return self.n

            def join(self, n=None):
                self.eng.wait_ge(self.sem, self.n if n is None else n)

            def link(self, ins):
                self.mark(ins)
                self.join()

        def end_stage(eng, s):
            eng.drain().then_inc(stage_done, 1)
            eng.wait_ge(stage_done, 4 * (s["at"] + 1))

        def stage_at(kind, k):
            return next(s["at"] for s in stages if s["kind"] == kind and s["k"] == k)

        DVE_NORM = 5
        POOL_CONV = (1, 3, 5)
        PRODUCTS = 4

        def pool_conv_step(n):
            norm_steps = NC - DVE_NORM
            return 2 * norm_steps + n + 1 + n // (CONV_W - 2)

        def conv_taps(eng, steps, c):
            sums = (conv_y[:, c], conv_odd[:, c])
            for w in range(CONV_W):
                src, tap = glu_u[:, c, w:w + T0], vec("a_dw_w", w, c)
                o = sums[w % 2]
                if w >= 2:
                    steps.join(steps.n - 1)
                if w == 0:
                    steps.mark(eng.tensor_scalar(o, src, tap, vec("a_dw_b", 0, c), ALU.mult, ALU.add))
                elif w == 1:
                    steps.mark(eng.tensor_scalar(o, src, tap, None, ALU.mult))
                else:
                    steps.mark(eng.scalar_tensor_tensor(out=o, in0=src, scalar=tap, in1=o, op0=ALU.mult, op1=ALU.add))
            steps.join()
            steps.mark(eng.tensor_tensor(sums[0], sums[0], sums[1], ALU.add))

        def scale_rows(eng, s, c, src):
            tk_ = tok_slice(s["tokens"])
            into = s.get("into")
            dst = mo[:, c] if into == "add" else h[:, c, tk_] if into == "h" else xn[:, c, tk_]
            return eng.scalar_tensor_tensor(out=dst, in0=src, scalar=vec(s["gain"], s["gi"], c), in1=rstd[:, tk_],
                                            op0=ALU.mult, op1=ALU.mult)

        head_sel_ones = ones[0:16, 0:1].broadcast_to([16, SEQ])

        def nsa_rope_dst(m):
            return qT[:, m] if m < 8 else (kcT, ksT, kwT)[(m - 8) // 2][:, m % 2]

        def block_rows(eng, kv):
            src = (kcT, vcT)[kv]
            dst = blocks[kv].rearrange("p l (g c) -> p l g c", g=GROUPS)
            for g in range(GROUPS):
                rows = slice(64 * (g % 2), 64 * (g % 2) + 64)
                tokens = src[rows, g // 2].rearrange("p (c l f) -> p l f c", l=8, f=2)
                for par in range(2):
                    for half in range(2):
                        ins = eng.tensor_tensor(
                            dst[64 * par:64 * par + 64, 8 * half:8 * half + 8, g],
                            tokens[:, :, par, half:half + NCMP],
                            cmp_pos[rows, kv, par, 8 * half:8 * half + 8].unsqueeze(2).broadcast_to([64, 8, NCMP]), ALU.add)
            return ins

        def attention_units(kind):
            units = []

            def map_(u, i, q, k, nk, bank, col, add):
                e = probs[:, u % 2, i * T0:i * T0 + nk]
                return dict(q=q, k=k, nk=nk, bank=bank, col=col, add=add, e=e, i=i)

            if kind == "diff_attn":
                for t in range(NT):
                    for hd in range(HEADS):
                        u = len(units)
                        nk = META + P * (t + 1)
                        maps = [map_(u, c, qT[64 * c:64 * c + 64, hd, t * P:(t + 1) * P], kT[64 * c:64 * c + 64, hd, 0:nk],
                                     nk, c, 0, [(ident, set_b["tri"], nk - P, P)]) for c in range(2)]
                        turns, stores, vals = [], [], [[], []]
                        full = nk // P
                        for c in range(2):
                            for kt in range(full + 1):
                                kn = P if kt < full else META
                                bank, col = (0, (c * full + kt) * P) if kt < full else (1, c * P)
                                turns.append((maps[c]["e"][:, kt * P:kt * P + kn], kn, bank, col))
                                vals[c].append((probsT[0:kn, u % 2, 512 * bank + col:512 * bank + col + P],
                                                v_tok[0:kn, kt, hd * P:(hd + 1) * P]))
                        stores = [(P, 0, 2 * full * P), (META, 1, 2 * P)]
                        units.append(dict(kind=kind, tile=t, maps=maps, turns=turns, stores=stores, values=vals, width=P,
                                          maxes=[(banks[:, 2 * (u % 2):2 * (u % 2) + 2, 0:nk], 0, 2)],
                                          out=o_tok[:, t, hd * P:(hd + 1) * P], nmaps=2))
            elif kind == "fox_attn":
                for t in range(NT):
                    for pr in range(8):
                        u = len(units)
                        nk = P * (t + 1)
                        maps = [map_(u, b, qT[64 * b:64 * b + 64, pr, t * P:(t + 1) * P], kT[64 * b:64 * b + 64, pr, 0:nk],
                                     nk, b, 0,
                                     [(fz[0:16, 4, t * P:(t + 1) * P], head_sel[0:16, 2 * pr + b, 0:nk], 0, nk),
                                      (head_sel[0:16, 2 * pr + b, 0:P], fz[0:16, 5, 0:nk], 0, nk),
                                      (ident, set_c["tri"], nk - P, P)]) for b in range(2)]
                        turns, vals = [], [[], []]
                        for b in range(2):
                            for kt in range(t + 1):
                                col = (b * (t + 1) + kt) * P
                                turns.append((maps[b]["e"][:, kt * P:(kt + 1) * P], P, 0, col))
                                hcol = (2 * pr + b) * 64
                                vals[b].append((probsT[:, u % 2, col:col + P], v_tok[:, kt, hcol:hcol + 64]))
                        sc = banks[:, 2 * (u % 2):2 * (u % 2) + 2, 0:nk]
                        units.append(dict(kind=kind, tile=t, maps=maps, turns=turns, stores=[(P, 0, 2 * (t + 1) * P)],
                                          values=vals, width=64, maxes=[(sc, 0, 2)],
                                          out=o_tok[:, t, pr * P:(pr + 1) * P].rearrange("p (b d) -> p b d", b=2), nmaps=2))
            else:
                for t in range(NT):
                    for pair in range(2):
                        for r in range(4):
                            for b in range(2):
                                u = len(units)
                                nk = P * (t + 1)
                                g, j = 2 * pair + b, 4 * pair + r
                                rows = slice(64 * b, 64 * b + 64)
                                q = qT[rows, j, t * P:(t + 1) * P]
                                tri = (ident, set_c["tri"], nk - P, P)
                                maps = [map_(u, 0, q, kcmpT[rows, g * NCMP:(g + 1) * NCMP], NCMP, 1, 0,
                                             [(ident, set_c["cmp_mask"][:, t * 16:t * 16 + NCMP], 0, NCMP)]),
                                        map_(u, 1, q, ksT[rows, pair, 0:nk], nk, 0, 0, [tri]),
                                        map_(u, 2, q, kwT[rows, pair, 0:nk], nk, 0, SEQ, [tri])]
                                turns = [(maps[0]["e"], NCMP, 1, 0)]
                                vals = [[(probsT[0:NCMP, u % 2, 512:512 + P], vcmp[0:NCMP, g, :])], [], []]
                                for i in (1, 2):
                                    for kt in range(t + 1):
                                        col = ((i - 1) * (t + 1) + kt) * P
                                        turns.append((maps[i]["e"][:, kt * P:(kt + 1) * P], P, 0, col))
                                        vc = (i - 1) * 256 + g * 64
                                        vals[i].append((probsT[:, u % 2, col:col + P], v_tok[:, kt, vc:vc + 64]))
                                sc = banks[:, 2 * (u % 2), :].rearrange("p (m n) -> p m n", m=2)[:, :, 0:nk]
                                cmp_sc = banks[:, 2 * (u % 2) + 1, 0:NCMP].unsqueeze(1)
                                units.append(dict(kind=kind, tile=t, maps=maps, turns=turns,
                                                  stores=[(P, 0, 2 * (t + 1) * P), (NCMP, 1, P)], values=vals, width=64,
                                                  maxes=[(cmp_sc, 0, 1), (sc, 1, 2)], head=4 * g + r, nmaps=3,
                                                  out=o_tok[:, t, j * P + b * 64:j * P + b * 64 + 64]))
            return units

        @block.sync
        def _(sp):
            sp.dma_start(h[:, :, :], dram["x"]).then_inc(inputs_landed, 16)
            sp.dma_start(vecs[:, :], dram["vecs"]).then_inc(inputs_landed, 16)
            sp.dma_start(const_a[:, :], dram["const_a"]).then_inc(inputs_landed, 16)
            sp.dma_start(subkeys[:, :, :], dram["subkeys"]).then_inc(inputs_landed, 16)
            sp.dma_start(gate_w[:, :, :], dram["gate_w"]).then_inc(inputs_landed, 16)
            sp.dma_start(forget_w[:, :, :], dram["forget_w"]).then_inc(inputs_landed, 16)

            def load(n, src):
                if n >= CHUNK_SLOTS:
                    sp.wait_ge(chunk_used, n - CHUNK_SLOTS + 1)
                sp.dma_start(ring[:, slot_of(n), :], src).then_inc(chunk_landed[slot_of(n)], 16)

            def dense_stream(s, first, second):
                n0, steps = s["n0"], s["n"]
                load(n0, first(0))
                with sp.Fori(0, steps // 4 - 1) as i:
                    for j in range(4):
                        for b, src in ((1, first(i * 4 + (j + 1))), (2, second(i * 4 + j))):
                            n = n0 + 2 * j + b
                            sp.wait_ge(chunk_used, i * 8 + (n - CHUNK_SLOTS + 1))
                            sp.dma_start(ring[:, slot_of(n), :], src).then_inc(chunk_landed[slot_of(n)], 16)
                for k in range(steps - 3, steps):
                    load(n0 + 2 * k - 1, first(k))
                    load(n0 + 2 * k, second(k - 1))
                load(n0 + 2 * steps - 1, second(steps - 1))

            def row(ap, k):
                return ap[bass.ds(k, 1)].rearrange("a p n -> (a p) n")

            for s in stages:
                kind, n0, k = s["kind"], s["n0"], s["k"]
                if kind == "norm" and s["gain"] == "kv_norm_g":
                    sp.wait_ge(stage_done, 4 * s["at"])
                    sp.dma_start(const_b, dram["const_b"]).then_inc(consts_b_landed, 16)
                    sp.dma_start(lam_vecs, dram["lam_vecs"]).then_inc(consts_b_landed, 16)
                    sp.dma_start(subln_gain, dram["subln_gain"]).then_inc(consts_b_landed, 16)
                if kind == "norm" and s["gain"] == "final_norm_g":
                    sp.wait_ge(stage_done, 4 * s["at"])
                    sp.dma_start(const_c, dram["const_c"]).then_inc(consts_c_landed, 16)
                    sp.dma_start(cmp_w2, dram["cmp_w2"]).then_inc(consts_c_landed, 16)
                    sp.dma_start(cmp_w2d, dram["cmp_w2d"]).then_inc(consts_c_landed, 16)
                    sp.dma_start(cmp_pos, dram["cmp_pos"]).then_inc(consts_c_landed, 16)
                    sp.dma_start(forget_b[0:16, 0:1], dram["forget_b"]).then_inc(consts_c_landed, 16)
                if kind == "dense" and s["what"] == "peer":
                    u, v = dram["peer_u"][k], dram["peer_v"][k].rearrange("(a b) d -> b a d", b=KEYS)
                    dense_stream(s, lambda i: row(u, i), lambda i: row(v, i))
                elif kind == "dense":
                    up = dram["mlp_up"][k - 2]
                    down = dram["mlp_down"][k - 2].rearrange("(f p) d -> f p d", p=P)
                    dense_stream(s, lambda i: row(up, i), lambda i: row(down, i))
                elif s.get("chunks"):
                    src = dram[(kind, k)]
                    for m in range(s["chunks"]):
                        load(n0 + m, src[m])
            sp.wait_ge(stage_done, 4 * len(stages))
            sp.dma_start(out, h[:, :, META:T0]).then_inc(out_stored, 16)
            sp.wait_ge(out_stored, 16)

        @block.tensor
        def _(pe):
            def await_chunk(n):
                pe.wait_ge(chunk_landed[slot_of(n)], 16 * (n // CHUNK_SLOTS + 1))

            def project(n, bank, x, tokens):
                await_chunk(n)
                for c in range(NC):
                    mm = pe.matmul(banks[:, bank, 0:tokens], ring[:, slot_of(n), c * P:(c + 1) * P], x[:, c],
                                   start=c == 0, stop=c == NC - 1)
                mm.then_inc(chunk_used, 1)

            def norm(s):
                tk_ = tok_slice(s["tokens"])
                for half in range(2):
                    pe.wait_ge(squares_ready, 2 * s["k"] + half + 1)
                    for c in range(4 * half, 4 * half + 4):
                        mm = pe.matmul(banks[:, 0, 0:s["tokens"]], ones, squares[:, c, tk_], start=c == 0, stop=c == NC - 1)
                mm.then_inc(sum_ready, 1)

            def conv_in(s):
                for m in range(16):
                    if m >= 4:
                        pe.wait_ge(glu_done, m // 2 - 1)
                    project(s["n0"] + m, m % 4, xn[:, :, :], T0)

            def layernorm(s):
                for c in range(NC):
                    mm = pe.matmul(banks[:, 0, 0:T0], ones, conv_y[:, c], start=c == 0, stop=c == NC - 1)
                mm.then_inc(mean_summed, 1)
                pe.wait_ge(squares_ready, 2 * norm_runs + 1)
                for c in range(NC):
                    mm = pe.matmul(banks[:, 1, 0:T0], ones, squares[:, c], start=c == 0, stop=c == NC - 1)
                mm.then_inc(var_summed, 1)

            def proj(s, x, tokens):
                for m in range(s["chunks"]):
                    if m >= 4:
                        pe.wait_ge(bank_free, s["bf0"] + m - 3)
                    project(s["n0"] + m, m % 4, x, tokens)

            def peer_topk(s):
                lo = T0 - s["tokens"]
                tiles = peer_token_tiles(s["tokens"])

                def scores(i):
                    t0, n = tiles[i]
                    if i >= 2:
                        pe.wait_ge(picks_stored, s["pt0"] + i - 1)
                    for m in range(16):
                        b = 4 * (i % 2) + m // 4
                        mm = pe.matmul(banks[0:n, b, (m % 4) * KEYS:(m % 4 + 1) * KEYS], peer_q[:, m, lo + t0:lo + t0 + n],
                                       subkeys[:, 2 * s["layer"] + m % 2, :], start=True, stop=True)
                    mm.then_inc(tile_scores, 1)

                def turn(i):
                    t0, n = tiles[i]
                    pe.wait_ge(tile_picks, s["pt0"] + i + 1)
                    for j, src in enumerate((tk["k1"], tk["k2"], tk["gate"].rearrange("p a b -> p (a b)"))):
                        mm = pe.transpose(banks[:, 4 * (i % 2), j * P:j * P + n], src[0:n, :], ident[0:n, 0:n])
                    mm.then_inc(picks_turned, 1)

                scores(0)
                scores(1)
                for i in range(len(tiles)):
                    turn(i)
                    if i + 2 < len(tiles):
                        scores(i + 2)

            def peer_gates(s):
                def groups(i, first=False):
                    for b in range(2):
                        g = 2 * i + b if first else i * 2 + b
                        pe.wait_ge(onehots_ready, g + (s["gg0"] + 1))
                        if not first:
                            pe.wait_ge(spread_stored, g + (s["gg0"] - 1))
                        for t in range(4):
                            mm = pe.matmul(banks[:, b, t * KEYS:(t + 1) * KEYS], onehot1[:, b, t], onehot2[:, b, t],
                                           start=True, stop=True)
                        mm.then_inc(spread_summed, 1)

                groups(0, first=True)
                with pe.Fori(1, s["tokens"] // 8) as i:
                    groups(i)

            def dense(s):
                n0, d0, steps, tokens = s["n0"], s["d0"], s["n"], s["tokens"]
                meta = tokens - SEQ
                x = xn[:, :, tok_slice(tokens)]

                def up(b, n, landed, freed):
                    pe.wait_ge(chunk_landed[slot_of(n)], landed)
                    if freed is not None:
                        pe.wait_ge(act_ready, freed)
                    for c in range(NC):
                        mm = pe.matmul(banks[:, 6 + b, 0:tokens], ring[:, slot_of(n), c * P:(c + 1) * P], x[:, c],
                                       start=c == 0, stop=c == NC - 1)
                    mm.then_inc(chunk_used, 1)

                def down(b, n, landed, ready, first, last):
                    pe.wait_ge(chunk_landed[slot_of(n)], landed)
                    pe.wait_ge(gated_ready, ready)
                    for c in range(NC):
                        w = ring[:, slot_of(n), c * P:(c + 1) * P]
                        mm = pe.matmul(banks[:, c // 2, (c % 2) * SEQ:(c % 2 + 1) * SEQ], w, act_gated[:, b, meta:tokens],
                                       start=first and c % 2 == 0, stop=last, skip_group_check=True)
                        if meta:
                            mm = pe.matmul(banks[:, 4, c * META:(c + 1) * META], w, act_gated[:, b, 0:meta],
                                           start=first and c == 0, stop=last, skip_group_check=True)
                    mm.then_inc(chunk_used, 1)

                def landed(n):
                    return 16 * (n // CHUNK_SLOTS + 1)

                up(0, n0, landed(n0), None)
                for k in range(1, 5):
                    nu, nd = n0 + 2 * k - 1, n0 + 2 * k
                    up(k % 2, nu, landed(nu), d0 + k - 1 if k >= 2 else None)
                    down((k - 1) % 2, nd, landed(nd), d0 + k, k == 1, False)
                with pe.Fori(1, steps // 4 - 1) as i:
                    for j in range(4):
                        nu, nd = n0 + 2 * j + 1, n0 + 2 * j + 2
                        up((j + 1) % 2, nu, i * 16 + landed(nu), i * 4 + (d0 + j))
                        down(j % 2, nd, i * 16 + landed(nd), i * 4 + (d0 + j + 1), False, False)
                for k in range(steps - 3, steps):
                    nu, nd = n0 + 2 * k - 1, n0 + 2 * k
                    up(k % 2, nu, landed(nu), d0 + k - 1)
                    down((k - 1) % 2, nd, landed(nd), d0 + k, False, False)
                nd = n0 + 2 * steps - 1
                down((steps - 1) % 2, nd, landed(nd), d0 + steps, False, True)

            def rope_projections(s, n0, m_count, x, tokens, mat, r_at=0):
                r0 = s["r0"] + r_at

                def rotate(m):
                    pe.wait_ge(raw_ready, r0 + m + 1)
                    if m >= 2:
                        pe.wait_ge(rope_done, r0 + m - 1)
                    pe.matmul(banks[:, 4 + m % 2, 0:tokens], mat, raw[:, m % 2, 0:tokens],
                              start=True, stop=True).then_inc(rot_ready, 1)

                for m in range(m_count):
                    if m >= 4:
                        pe.wait_ge(raw_ready, r0 + m - 3)
                    project(n0 + m, m % 4, x, tokens)
                    if m >= 1:
                        rotate(m - 1)
                rotate(m_count - 1)

            def values(n0, per_chunk, width, tiles, first_bank=0):
                halves = width // 512
                for n in range(NC // per_chunk):
                    await_chunk(n0 + n)
                    for j in range(per_chunk):
                        c = n * per_chunk + j
                        for i, (t0, m) in enumerate(tiles):
                            for half in range(halves):
                                mm = pe.matmul(banks[0:m, first_bank + halves * i + half, :], xn[:, c, t0:t0 + m],
                                               ring[:, slot_of(n0 + n), j * width + half * 512:j * width + half * 512 + 512],
                                               start=c == 0, stop=c == NC - 1, skip_group_check=True)
                    mm.then_inc(chunk_used, 1)

            def kv_proj(s):
                pe.wait_ge(consts_b_landed, 48)
                rope_projections(s, s["n0"], 8, xn[:, :, :], T0, set_b["rope_mat"])
                pe.wait_ge(raw_ready, s["r0"] + 8)
                pe.wait_ge(rope_done, s["r0"] + 8)
                values(s["n0"] + 8, 1, D, [(0, P), (P, P), (2 * P, META)])

            def q_proj(s):
                rope_projections(s, s["n0"], 8, xn[:, :, META:T0], SEQ, set_b["rope_mat"])

            def nsa_proj(s):
                pe.wait_ge(consts_c_landed, 80)
                x = xn[:, :, META:T0]
                rope_projections(s, s["n0"], 14, x, SEQ, set_c["rope_mat"])
                pe.wait_ge(raw_ready, s["r0"] + 14)
                pe.wait_ge(rope_done, s["r0"] + 14)
                for m in range(2):
                    project(s["n0"] + 14 + m, m, x, SEQ)
                values(s["n0"] + 16, 2, 512, [(META + P * i, P) for i in range(NT)], first_bank=2)
                for i in range(NT):
                    for c in range(NC):
                        mm = pe.matmul(banks[:, 4 + i, 0:48], xn[:, c, META + P * i:META + P * (i + 1)], gate_w[:, c],
                                       start=c == 0, stop=c == NC - 1)
                mm.then_inc(gates_summed, 1)

            def nsa_compress(s):
                for kv in range(2):
                    pe.wait_ge(cmp_blocks_ready[kv], 1)
                    for q in range(4):
                        n = s["n0"] + 4 * kv + q
                        await_chunk(n)
                        for j in range(4):
                            lp = 4 * q + j
                            for m in range(2):
                                mm = pe.matmul(banks[:, 2 * kv + m, 0:GROUPS * NCMP],
                                               ring[:, slot_of(n), j * 256 + m * P:j * 256 + (m + 1) * P],
                                               blocks[kv][:, lp], start=lp == 0, stop=lp == 15, skip_group_check=True)
                        mm.then_inc(chunk_used, 1)
                pe.wait_ge(cmp_hidden_ready, 1)
                for m in range(2):
                    pe.matmul(banks[:, 4, 0:GROUPS * NCMP], cmp_w2d[:, m], hid[:, m, 0:GROUPS * NCMP],
                              start=m == 0, stop=m == 1)
                for g in range(GROUPS):
                    for m in range(2):
                        mm = pe.matmul(banks[0:NCMP, 5, g * 64:(g + 1) * 64], hid[:, 2 + m, g * NCMP:(g + 1) * NCMP],
                                       cmp_w2[:, 1, m], start=m == 0, stop=m == 1, skip_group_check=True)
                mm.then_inc(cmp_out_summed, 1)

            def attend(s, units):
                u0 = s["u0"]

                def scores(u):
                    if u >= 2:
                        pe.wait_ge(exp_done, u0 + u - 1)
                    for mp in units[u]["maps"]:
                        o = banks[:, 2 * (u % 2) + mp["bank"], mp["col"]:mp["col"] + mp["nk"]]
                        mm = pe.matmul(o, mp["q"], mp["k"], start=True, stop=not mp["add"], skip_group_check=True)
                        for j, (lhsT, rhs, c0, w) in enumerate(mp["add"]):
                            mm = pe.matmul(o[:, c0:c0 + w], lhsT, rhs, start=False, stop=j == len(mp["add"]) - 1,
                                           skip_group_check=True)
                    mm.then_inc(scores_ready, 1)

                def turn(u):
                    pe.wait_ge(exp_done, u0 + u + 1)
                    if u >= 1:
                        pe.wait_ge(turned_stored, u0 + u)
                    for (src, kn, bank, col) in units[u]["turns"]:
                        mm = pe.transpose(banks[0:kn, 4 + bank, col:col + P], src, ident)
                    mm.then_inc(turned, 1)

                def weigh(u):
                    pe.wait_ge(turned_stored, u0 + u + 1)
                    if u >= 2:
                        pe.wait_ge(mixed, u0 + u - 1)
                    for i, parts in enumerate(units[u]["values"]):
                        for j, (lhsT, v) in enumerate(parts):
                            w = units[u]["width"]
                            mm = pe.matmul(banks[:, 6 + u % 2, i * w:(i + 1) * w], lhsT, v, start=j == 0,
                                           stop=j == len(parts) - 1, skip_group_check=True)
                    mm.then_inc(av_done, 1)

                for u in range(len(units) + 2):
                    if u < len(units):
                        scores(u)
                    if 1 <= u <= len(units):
                        turn(u - 1)
                    if u >= 2:
                        weigh(u - 2)

            def turn_out(s):
                for i in range(NT):
                    for half in range(2):
                        for c in range(4 * half, 4 * half + 4):
                            mm = pe.transpose(banks[:, 2 * i + half, (c % 4) * P:(c % 4 + 1) * P],
                                              o_tok[:, i, c * P:(c + 1) * P], ident)
                        mm.then_inc(out_turned, 1)

            def fox_proj(s):
                x = xn[:, :, META:T0]
                for m in range(16):
                    if m >= 4:
                        pe.wait_ge(bank_free, s["bf0"] + m - 3)
                    project(s["n0"] + m, m % 4, x, SEQ)
                for c in range(NC):
                    mm = pe.matmul(banks[0:16, 4, 0:SEQ], forget_w[:, c], x[:, c], start=c == 0, stop=c == NC - 1)
                mm.then_inc(forget_summed, 1)
                pe.wait_ge(bank_free, s["bf0"] + 16)
                values(s["n0"] + 16, 1, D, [(META + P * i, P) for i in range(NT)])

            pe.wait_ge(inputs_landed, 96)
            norm_runs = 0
            for s in stages:
                kind = s["kind"]
                if kind == "norm":
                    norm(dict(s, k=norm_runs))
                    norm_runs += 1
                elif kind == "layernorm":
                    layernorm(s)
                    norm_runs += 1
                elif kind == "conv_in":
                    conv_in(s)
                elif kind == "proj_add":
                    proj(s, xn[:, :, :] if s["src"] == "xn" else oT, s["tokens"])
                elif kind == "proj_keep":
                    proj(s, oT, SEQ)
                elif kind == "peer_query":
                    proj(s, xn[:, :, tok_slice(s["tokens"])], s["tokens"])
                elif kind in ("diff_attn", "nsa_attn", "fox_attn"):
                    attend(s, attention_units(kind))
                else:
                    dict(peer_topk=peer_topk, peer_gates=peer_gates, dense=dense, kv_proj=kv_proj, q_proj=q_proj,
                         nsa_proj=nsa_proj, nsa_compress=nsa_compress, turn_out=turn_out, fox_proj=fox_proj,
                         subln=lambda s: None)[kind](s)
                end_stage(pe, s)

        @block.scalar
        def _(act):
            steps = Steps(act, act_step)
            norm_runs = 0

            def norm(s, src):
                tk_ = tok_slice(s["tokens"])
                for half in range(2):
                    act.activation(squares[:, 4 * half:4 * half + 4, tk_], src[:, 4 * half:4 * half + 4], ACT.Square)\
                       .then_inc(squares_ready, 1)
                act.wait_ge(sum_ready, s["k"] - ln_runs + 1)
                act.activation(root[:, tk_], banks[:, 0, 0:s["tokens"]], ACT.Sqrt, bias=eps, scale=1.0 / D)\
                   .then_inc(root_ready, 1)

            def weigh_taps(c, taps):
                act.wait_ge(glu_done, c + 1)
                for w in taps:
                    n = POOL_CONV.index(c) * (CONV_W - 2) + w - 2
                    dst = (conv_y[:, c], conv_odd[:, c])[w] if w < 2 else products[:, n % PRODUCTS]
                    if w >= 2 and n >= PRODUCTS:
                        act.wait_ge(pool_step, pool_conv_step(n - PRODUCTS))
                    src, tap = glu_u[:, c, w:w + T0], vec("a_dw_w", w, c)
                    if w == 0:
                        act.activation(dst, src, ACT.Identity, bias=vec("a_dw_b", 0, c), scale=tap)
                    else:
                        ins = act.activation(dst, src, ACT.Copy, scale=tap)
                        if w >= 2:
                            ins.then_inc(product_ready, 1)

            def conv_in(s):
                for p_ in range(8):
                    act.wait_ge(chunk_used, s["n0"] + 2 * p_ + 2)
                    if p_ >= 2:
                        act.wait_ge(glu_done, p_ - 1)
                    act.activation(glu_sig[:, p_ % 2], banks[:, (2 * p_ + 1) % 4, 0:T0], ACT.Sigmoid,
                                   bias=vec("a_pw1_b", 1, p_)).then_inc(glu_gate_ready, 1)
                    if p_ - 1 in POOL_CONV:
                        weigh_taps(p_ - 1, range(0, 16))
                    if p_ - 2 in POOL_CONV:
                        weigh_taps(p_ - 2, range(16, CONV_W))

            def layernorm(s):
                act.wait_ge(centred, 1)
                act.activation(squares[:, :, :], conv_y[:, :, :], ACT.Square).then_inc(squares_ready, 2)
                act.wait_ge(var_summed, 1)
                act.activation(root[:, :], banks[:, 1, 0:T0], ACT.Sqrt, bias=eps, scale=1.0 / D).then_inc(ln_root_ready, 1)
                for c in range(NC):
                    act.wait_ge(ln_scaled, c + 1)
                    act.activation(xn[:, c], squares[:, c], ACT.Silu, bias=vec("a_ln_b", 0, c), scale=vec("a_ln_g", 0, c))

            def keep(s, dst, tokens):
                for m in range(s["chunks"] if s["kind"] != "fox_proj" else 16):
                    act.wait_ge(chunk_used, s["n0"] + m + 1)
                    act.activation(dst(m), banks[:, m % 4, 0:tokens], ACT.Copy).then_inc(bank_free, 1)

            def peer_topk(s):
                for i, (t0, n) in enumerate(peer_token_tiles(s["tokens"])):
                    act.wait_ge(tops_ready, s["pt0"] + i + 1)
                    act.activation(tk["ex"][0:n], tk["ex"][0:n], ACT.Exp).then_inc(exps_ready, 1)
                    act.wait_ge(picks_turned, s["pt0"] + i + 1)
                    src = banks[:, 4 * (i % 2), 0:3 * P].rearrange("p (j t) -> p j t", j=3)[:, :, 0:n]
                    act.activation(pick[:, :, t0:t0 + n], src, ACT.Copy).then_inc(picks_stored, 1)

            def peer_gates(s):
                def groups(i):
                    for b in range(2):
                        g = i * 2 + b
                        act.wait_ge(spread_summed, g + (s["gg0"] + 1))
                        act.activation(arena[:, bass.ds(g * 512, 512)], banks[:, b, :], ACT.Copy).then_inc(spread_stored, 1)

                with act.Fori(0, s["tokens"] // 8) as i:
                    groups(i)

            def dense(s):
                n0, d0, steps_, tokens = s["n0"], s["d0"], s["n"], s["tokens"]
                func = ACT.Gelu if s["what"] == "peer" else ACT.Relu

                def one(b, used, freed):
                    act.wait_ge(chunk_used, used)
                    if freed is not None:
                        act.wait_ge(gated_ready, freed)
                    act.activation(act_out[:, b, 0:tokens], banks[:, 6 + b, 0:tokens], func).then_inc(act_ready, 1)

                one(0, n0 + 1, None)
                one(1, n0 + 2, None)
                one(0, n0 + 4, d0 + 1)
                one(1, n0 + 6, d0 + 2)
                with act.Fori(1, steps_ // 4) as i:
                    for j in range(4):
                        one(j % 2, i * 8 + (n0 + 2 * j), i * 4 + (d0 + j - 1))

            def rope(s, n0, m_count, tokens, r_at=0):
                r0 = s["r0"] + r_at
                for m in range(m_count):
                    act.wait_ge(chunk_used, n0 + m + 1)
                    if m >= 2:
                        act.wait_ge(rope_done, r0 + m - 1)
                    act.activation(raw[:, m % 2, 0:tokens], banks[:, m % 4, 0:tokens], ACT.Copy).then_inc(raw_ready, 1)

            def kv_proj(s):
                rope(s, s["n0"], 8, T0)
                act.wait_ge(chunk_used, s["n0"] + 16)
                for i, m in enumerate((P, P, META)):
                    act.activation(v_tok[0:m, i, 0:512], banks[0:m, 2 * i, :], ACT.Copy)

            def diff_lambda():
                act.wait_ge(lam_sums, 1)
                act.activation(lam_exp, lam_sum, ACT.Exp).then_inc(lam_exps, 1)

            def nsa_proj(s):
                rope(s, s["n0"], 14, SEQ)
                for m in range(2):
                    act.wait_ge(chunk_used, s["n0"] + 14 + m + 1)
                    act.activation(vcT[:, m], banks[:, m, 0:SEQ], ACT.Copy)
                act.wait_ge(gates_summed, 1)
                act.activation(gates[:, :, :], banks[:, 4:6, 0:48], ACT.Sigmoid)

            def nsa_compress(s):
                for kv in range(2):
                    act.wait_ge(chunk_used, s["n0"] + 4 * kv + 4)
                    ins = act.activation(hid[:, 2 * kv:2 * kv + 2, 0:GROUPS * NCMP],
                                         banks[:, 2 * kv:2 * kv + 2, 0:GROUPS * NCMP], ACT.Silu)
                ins.then_inc(cmp_hidden_ready, 1)
                act.wait_ge(cmp_out_summed, 1)
                act.activation(kcmpT[:, 0:GROUPS * NCMP], banks[:, 4, 0:GROUPS * NCMP], ACT.Copy)
                act.activation(vcmp[0:NCMP, :, :], banks[0:NCMP, 5, 0:256].rearrange("p (g d) -> p g d", g=GROUPS), ACT.Copy)

            def attend(s, units):
                u0 = s["u0"]

                def store(u):
                    act.wait_ge(turned, u0 + u + 1)
                    if u >= 2:
                        act.wait_ge(av_done, u0 + u - 1)
                    for rows, bank, width in units[u]["stores"]:
                        ins = act.activation(probsT[0:rows, u % 2, 512 * bank:512 * bank + width],
                                             banks[0:rows, 4 + bank, 0:width], ACT.Copy)
                    ins.then_inc(turned_stored, 1)

                for u in range(len(units) + 1):
                    if u < len(units):
                        act.wait_ge(max_ready, u0 + u + 1)
                        if u >= 2:
                            act.wait_ge(turned, u0 + u - 1)
                        if u >= 3:
                            act.wait_ge(mixed, u0 + u - 2)
                        for mp in units[u]["maps"]:
                            i = mp["i"]
                            ins = act.activation(mp["e"], banks[:, 2 * (u % 2) + mp["bank"], mp["col"]:mp["col"] + mp["nk"]],
                                                 ACT.Exp, bias=neg_max[:, u % 2, i:i + 1], scale=SCALE,
                                                 accum_out=row_sum[:, u % 3, i:i + 1])
                        ins.then_inc(exp_done, 1)
                    if u >= 1:
                        store(u - 1)

            def subln(s):
                act.wait_ge(sub_squared, 1)
                act.activation(sub_root, sub_ss, ACT.Sqrt, bias=eps, scale=1.0 / P).then_inc(sub_root_ready, 1)

            def turn_out(s):
                for i in range(NT):
                    for half in range(2):
                        act.wait_ge(out_turned, 4 * s["k"] + 2 * i + half + 1)
                        act.activation(oT[:, 4 * half:4 * half + 4, i * P:(i + 1) * P],
                                       banks[:, 2 * i + half, :].rearrange("p (c t) -> p c t", c=4), ACT.Copy)

            def fox_proj(s):
                keep(s, lambda m: qT[:, m] if m < 8 else kT[:, m - 8, 0:SEQ], SEQ)
                act.wait_ge(forget_parts, 1)
                steps.link(act.activation(fz[0:16, 1], fz[0:16, 0], ACT.Abs))
                steps.link(act.activation(fz[0:16, 1], fz[0:16, 1], ACT.Exp, scale=-1.0))
                act.activation(fz[0:16, 2], fz[0:16, 1], ACT.Ln, bias=1.0).then_inc(forget_abs, 1)
                act.wait_ge(chunk_used, s["n0"] + 24)
                for i in range(NT):
                    act.activation(v_tok[:, i, 0:512], banks[:, 2 * i, :], ACT.Copy)

            act.wait_ge(inputs_landed, 96)
            act.wait_ge(set_up, 2)
            ln_runs = 0
            for s in stages:
                kind = s["kind"]
                if kind == "norm":
                    norm(dict(s, k=norm_runs), mo if s.get("into") == "add" else h[:, :, tok_slice(s["tokens"])])
                    norm_runs += 1
                elif kind == "layernorm":
                    layernorm(s)
                    norm_runs += 1
                    ln_runs += 1
                elif kind == "proj_keep":
                    keep(s, lambda m: mo[:, m], SEQ)
                elif kind == "peer_query":
                    keep(s, lambda m, s=s: peer_q[:, m, tok_slice(s["tokens"])], s["tokens"])
                elif kind == "q_proj":
                    rope(s, s["n0"], 8, SEQ)
                    diff_lambda()
                elif kind in ("diff_attn", "nsa_attn", "fox_attn"):
                    attend(s, attention_units(kind))
                else:
                    dict(conv_in=conv_in, peer_topk=peer_topk, peer_gates=peer_gates, dense=dense, kv_proj=kv_proj,
                         nsa_proj=nsa_proj, nsa_compress=nsa_compress, turn_out=turn_out, fox_proj=fox_proj,
                         subln=subln, proj_add=lambda s: None)[kind](s)
                end_stage(act, s)

        @block.vector
        def _(dve):
            steps = Steps(dve, dve_step)

            def norm(s):
                tk_ = tok_slice(s["tokens"])
                dve.wait_ge(root_ready, s["k"] + 1)
                dve.reciprocal(rstd[:, tk_], root[:, tk_]).then_inc(rstd_ready, 1)
                dve.wait_ge(rstd_ready, s["k"] + 1)
                for c in range(DVE_NORM):
                    steps.mark(scale_rows(dve, s, c, mo[:, c] if s.get("into") == "add" else h[:, c, tk_]))
                if s.get("into") == "add":
                    steps.join()
                    dve.tensor_tensor(h[:, 0:DVE_NORM, tk_], h[:, 0:DVE_NORM, tk_], mo[:, 0:DVE_NORM], ALU.add)

            def conv_in(s):
                dve.wait_ge(taps_ready, 1)
                for p_ in range(8):
                    dve.wait_ge(glu_gate_ready, p_ + 1)
                    dve.scalar_tensor_tensor(out=glu_u[:, p_, CONV_W - 1:], in0=banks[:, (2 * p_) % 4, 0:T0],
                                             scalar=vec("a_pw1_b", 0, p_), in1=glu_sig[:, p_ % 2],
                                             op0=ALU.add, op1=ALU.mult).then_inc(glu_done, 1)
                    if p_ not in POOL_CONV:
                        dve.wait_ge(glu_done, p_ + 1)
                        conv_taps(dve, steps, p_)

            def layernorm(s):
                dve.wait_ge(mean_summed, 1)
                steps.link(dve.tensor_scalar(mean[:, :], banks[:, 0, 0:T0], 1.0 / D, None, ALU.mult))
                dve.tensor_tensor(conv_y[:, :, :], conv_y[:, :, :], mean.unsqueeze(1).broadcast_to([P, NC, T0]),
                                  ALU.subtract).then_inc(centred, 1)
                dve.wait_ge(ln_root_ready, 1)
                steps.link(dve.reciprocal(rstd[:, :], root[:, :]))
                for c in range(NC):
                    dve.tensor_tensor(squares[:, c], conv_y[:, c], rstd[:, :], ALU.mult).then_inc(ln_scaled, 1)

            def proj_add(s):
                tk_ = tok_slice(s["tokens"])
                for m in range(8):
                    dve.wait_ge(chunk_used, s["n0"] + m + 1)
                    src, dst = banks[:, m % 4, 0:s["tokens"]], h[:, m, tk_]
                    if s["bias"]:
                        ins = dve.scalar_tensor_tensor(out=dst, in0=src, scalar=vec("a_pw2_b", 0, m), in1=dst,
                                                       op0=ALU.add, op1=ALU.add)
                    else:
                        ins = dve.tensor_tensor(dst, src, dst, ALU.add)
                    ins.then_inc(bank_free, 1)

            def top16(n, src, vals, idx, rest, count):
                for m in range(count):
                    steps.mark(dve.max(vals[0:n, m, 0:8], src(m)))
                steps.join()
                for m in range(count):
                    steps.mark(dve.max_index(idx[0:n, m, 0:8], vals[0:n, m, 0:8], src(m)))
                    steps.mark(dve.match_replace(rest[0:n, m], vals[0:n, m, 0:8], src(m), LOWEST))
                steps.join()
                for m in range(count):
                    steps.mark(dve.max(vals[0:n, m, 8:16], rest[0:n, m]))
                steps.join()
                for m in range(count):
                    last = dve.max_index(idx[0:n, m, 8:16], vals[0:n, m, 8:16], rest[0:n, m])
                    if m < count - 1:
                        steps.mark(last)
                return last

            def peer_topk(s):
                for i, (t0, n) in enumerate(peer_token_tiles(s["tokens"])):
                    k = s["pt0"] + i
                    dve.wait_ge(tile_scores, k + 1)
                    src = lambda m: banks[0:n, 4 * (i % 2) + m // 4, (m % 4) * KEYS:(m % 4 + 1) * KEYS]
                    if i:
                        dve.wait_ge(codes_ready, k)
                    top16(n, src, tk["vals"], tk["idx"], tk["rest"], 16).then_inc(index_ready, 1)
                    at = 0
                    v = tk["vals"][0:n].rearrange("p (h f) r -> p h f r", f=2)
                    for a, na, nb in CAND_ROWS:
                        o = tk["cand"][0:n, :, at:at + na * nb].rearrange("p h (a b) -> p h a b", b=nb)
                        steps.mark(dve.tensor_tensor(o, v[:, :, 0, a:a + na].unsqueeze(3).broadcast_to([n, HEADS, na, nb]),
                                                     v[:, :, 1, 0:nb].unsqueeze(2).broadcast_to([n, HEADS, na, nb]), ALU.add))
                        at += na * nb
                    steps.join()
                    steps.link(top16(n, lambda m: tk["cand"][0:n, m], tk["best"], tk["pos"], tk["cand_rest"], HEADS))
                    best = tk["best"][0:n]
                    dve.tensor_tensor(tk["ex"][0:n], best, best[:, :, 0:1].broadcast_to([n, HEADS, TOPK]), ALU.subtract)\
                       .then_inc(tops_ready, 1)
                    steps.link(dve.tensor_copy(tk["posf"][0:n], tk["pos"][0:n]))
                    hit = tk["hit"][0:n]
                    flat = tk["posf"][0:n].rearrange("p h j -> p (h j)")
                    steps.link(dve.tensor_tensor(hit, iota_cand[0:n].unsqueeze(1).broadcast_to([n, P, NCAND]),
                                                 flat.unsqueeze(2).broadcast_to([n, P, NCAND]), ALU.is_equal))
                    dve.wait_ge(codes_ready, k + 1)
                    hit4 = hit.rearrange("p (h j) c -> p h j c", h=HEADS)
                    steps.link(dve.tensor_tensor(hit4, hit4, tk["code"][0:n].unsqueeze(2).broadcast_to([n, HEADS, TOPK, NCAND]),
                                                 ALU.mult))
                    steps.link(dve.reduce_sum(tk["picked"][0:n], hit, AX_X))
                    steps.link(dve.tensor_copy(tk["pickedi"][0:n], tk["picked"][0:n]))
                    if i:
                        dve.wait_ge(picks_turned, k)
                    steps.mark(dve.tensor_scalar(tk["k1i"][0:n], tk["pickedi"][0:n], 7, None, ALU.logical_shift_right))
                    steps.link(dve.tensor_scalar(tk["k2i"][0:n], tk["pickedi"][0:n], 127, None, ALU.bitwise_and))
                    steps.mark(dve.tensor_copy(tk["k1"][0:n], tk["k1i"][0:n]))
                    steps.mark(dve.tensor_copy(tk["k2"][0:n], tk["k2i"][0:n]))
                    dve.wait_ge(exps_ready, k + 1)
                    steps.link(dve.reduce_sum(tk["tot"][0:n], tk["ex"][0:n], AX_X))
                    steps.link(dve.reciprocal(tk["inv"][0:n], tk["tot"][0:n]))
                    dve.tensor_tensor(tk["gate"][0:n], tk["ex"][0:n],
                                      tk["inv"][0:n].unsqueeze(2).broadcast_to([n, HEADS, TOPK]), ALU.mult)\
                       .then_inc(tile_picks, 1)

            def peer_gates(s):
                def groups(i, first=False):
                    for b in range(2):
                        if not first:
                            dve.wait_ge(spread_summed, i * 2 + (b + s["gg0"] - 1))
                        for t in range(4):
                            at = i * 8 + (4 * b + t)
                            dve.tensor_scalar(onehot1[:, b, t], iota, pick[:, 0, bass.ds(at, 1)], None, ALU.is_equal)
                            ins = dve.tensor_scalar(onehot2[:, b, t], iota, pick[:, 1, bass.ds(at, 1)],
                                                    pick[:, 2, bass.ds(at, 1)], ALU.is_equal, ALU.mult)
                        ins.then_inc(onehots_ready, 1)

                groups(0, first=True)
                with dve.Fori(1, s["tokens"] // 8) as i:
                    groups(i)

            def dense(s):
                d0, n, tokens = s["d0"], s["n"], s["tokens"]
                meta = tokens - SEQ

                def one(b, ready, k):
                    dve.wait_ge(act_ready, ready)
                    a = act_out[:, b, 0:tokens]
                    g = spread[:, 0:tokens, bass.ds(k, 1)].rearrange("p t k -> p (t k)") if s["what"] == "peer" else a
                    dve.tensor_tensor(act_gated[:, b, 0:tokens], a, g, ALU.mult).then_inc(gated_ready, 1)

                with dve.Fori(0, n // 4) as i:
                    for j in range(4):
                        one(j % 2, i * 4 + (d0 + j + 1), i * 4 + j)
                dve.wait_ge(chunk_used, s["n0"] + 2 * n)
                dst = h[:, :, META:T0] if s["what"] == "peer" else mo
                for b in range(4):
                    src = banks[:, b, :].rearrange("p (c t) -> p c t", c=2)
                    if s["what"] == "peer":
                        dve.tensor_tensor(dst[:, 2 * b:2 * b + 2], dst[:, 2 * b:2 * b + 2], src, ALU.add)
                    else:
                        dve.tensor_copy(dst[:, 2 * b:2 * b + 2], src)
                if meta:
                    dve.tensor_tensor(h[:, :, 0:META], h[:, :, 0:META],
                                      banks[:, 4, 0:NC * META].rearrange("p (c t) -> p c t", c=NC), ALU.add)

            def rope(s, m_count, tokens, dst, sin):
                for m in range(m_count):
                    dve.wait_ge(rot_ready, s["r0"] + m + 1)
                    steps.link(dve.tensor_tensor(rot[:, m % 2, 0:tokens], banks[:, 4 + m % 2, 0:tokens], sin, ALU.mult))
                    dve.wait_ge(cos_ready, s["r0"] + m + 1)
                    dve.tensor_tensor(dst(m), dst(m), rot[:, m % 2, 0:tokens], ALU.add).then_inc(rope_done, 1)

            def kv_proj(s):
                dve.wait_ge(consts_b_landed, 48)
                rope(s, 8, T0, lambda m: kT[:, m], set_b["rope_sin"])
                dve.wait_ge(chunk_used, s["n0"] + 16)
                for i, m in enumerate((P, P, META)):
                    dve.tensor_copy(v_tok[0:m, i, 512:1024], banks[0:m, 2 * i + 1, :])

            def q_proj(s):
                for j in range(2):
                    steps.link(dve.tensor_tensor(lam_tmp[:, j], lam_vecs[:, 2 * j], lam_vecs[:, 2 * j + 1], ALU.mult))
                dve.reduce_sum(lam_sum, lam_tmp, AX_X).then_inc(lam_sums, 1)
                rope(s, 8, SEQ, lambda m: qT[:, m], set_b["rope_sin"][:, META:T0])
                dve.wait_ge(lam_exps, 1)
                steps.link(dve.tensor_tensor(neg_lam, lam_exp[:, 1:2], lam_exp[:, 0:1], ALU.subtract))
                steps.link(dve.tensor_scalar(neg_lam, neg_lam, -LAM_INIT, None, ALU.add))

            def nsa_proj(s):
                dve.wait_ge(consts_c_landed, 80)
                rope(s, 14, SEQ, nsa_rope_dst, set_c["rope_sin"])
                dve.wait_ge(chunk_used, s["n0"] + 20)
                for i in range(NT):
                    dve.tensor_copy(v_tok[:, i, 0:512], banks[:, 2 + i, :])

            def nsa_compress(s):
                steps.link(dve.tensor_scalar(gates[:, 0, :].rearrange("p (h i) -> p h i", i=3)[:, :, 0],
                                             gates[:, 0, :].rearrange("p (h i) -> p h i", i=3)[:, :, 0],
                                             set_c["row_ok"][:, 0:1], None, ALU.mult))
                block_rows(dve, 0).then_inc(cmp_blocks_ready[0], 1)

            def attend(s, units):
                u0 = s["u0"]

                def mix(u):
                    un = units[u]
                    n, w = un["nmaps"], un["width"]
                    part = lambda i: banks[:, 6 + u % 2, i * w:(i + 1) * w]
                    cf, sums = coef[:, u % 2, 0:n], row_sum[:, u % 3, 0:n]
                    dve.wait_ge(av_done, u0 + u + 1)
                    steps.link(dve.reciprocal(cf, sums))
                    if un["kind"] == "fox_attn":
                        for i in range(2):
                            ins = dve.tensor_scalar(un["out"][:, i], part(i), cf[:, i:i + 1], None, ALU.mult)
                    elif un["kind"] == "diff_attn":
                        steps.link(dve.tensor_tensor(cf[:, 1:2], cf[:, 1:2], neg_lam, ALU.mult))
                        steps.link(dve.tensor_scalar(o_mix[:, 0, 0], part(1), cf[:, 1:2], None, ALU.mult))
                        ins = dve.scalar_tensor_tensor(out=un["out"], in0=part(0), scalar=cf[:, 0:1], in1=o_mix[:, 0, 0],
                                                       op0=ALU.mult, op1=ALU.add)
                    else:
                        hd = un["head"]
                        steps.link(dve.tensor_tensor(cf, cf, gates[:, un["tile"], 3 * hd:3 * hd + 3], ALU.mult))
                        steps.link(dve.tensor_scalar(o_mix[:, 0, 0, 0:w], part(0), cf[:, 0:1], None, ALU.mult))
                        steps.link(dve.scalar_tensor_tensor(out=o_mix[:, 0, 1, 0:w], in0=part(1), scalar=cf[:, 1:2],
                                                            in1=o_mix[:, 0, 0, 0:w], op0=ALU.mult, op1=ALU.add))
                        ins = dve.scalar_tensor_tensor(out=un["out"], in0=part(2), scalar=cf[:, 2:3],
                                                       in1=o_mix[:, 0, 1, 0:w], op0=ALU.mult, op1=ALU.add)
                    ins.then_inc(mixed, 1)

                for u in range(len(units) + 2):
                    if u < len(units):
                        un = units[u]
                        dve.wait_ge(scores_ready, u0 + u + 1)
                        if u >= 2:
                            dve.wait_ge(exp_done, u0 + u - 1)
                        for src, c0, n in un["maxes"]:
                            steps.mark(dve.reduce_max(row_max[:, u % 2, c0:c0 + n], src, AX_X))
                        steps.join()
                        n = un["nmaps"]
                        dve.tensor_scalar(neg_max[:, u % 2, 0:n], row_max[:, u % 2, 0:n], -SCALE, None, ALU.mult)\
                           .then_inc(max_ready, 1)
                    if u >= 2:
                        mix(u - 2)

            def subln(s):
                o3 = o_tok.rearrange("p t (h e) -> p (t h) e", h=HEADS)
                sq3 = o_sq.rearrange("p t (h e) -> p (t h) e", h=HEADS)
                full = [P, NT * HEADS, P]
                steps.link(dve.tensor_tensor(sq3, o3, o3, ALU.mult))
                dve.reduce_sum(sub_ss, sq3, AX_X).then_inc(sub_squared, 1)
                dve.wait_ge(sub_root_ready, 1)
                steps.link(dve.reciprocal(sub_rstd, sub_root))
                steps.link(dve.tensor_scalar(lam_tmp.rearrange("p a b -> p (a b)"), subln_gain, 1.0 - LAM_INIT, None, ALU.mult))
                steps.link(dve.tensor_tensor(o3, o3, sub_rstd.unsqueeze(2).broadcast_to(full), ALU.mult))
                steps.link(dve.tensor_tensor(o3, o3, lam_tmp.rearrange("p a b -> p (a b)").unsqueeze(1).broadcast_to(full), ALU.mult))

            def fox_proj(s):
                dve.wait_ge(forget_summed, 1)
                steps.link(dve.tensor_scalar(fz[0:16, 0], banks[0:16, 4, 0:SEQ], forget_b[0:16, 0:1], None, ALU.add))
                dve.tensor_scalar(fz[0:16, 3], fz[0:16, 0], 0.0, None, ALU.min).then_inc(forget_parts, 1)
                dve.wait_ge(forget_abs, 1)
                steps.link(dve.tensor_tensor(fz[0:16, 3], fz[0:16, 3], fz[0:16, 2], ALU.subtract))
                steps.link(dve.tensor_tensor_scan(fz[0:16, 2], head_sel_ones, fz[0:16, 3], 0.0, ALU.mult, ALU.add))
                steps.mark(dve.tensor_scalar(fz[0:16, 4], fz[0:16, 2], 1.0 / SCALE, None, ALU.mult))
                steps.mark(dve.tensor_scalar(fz[0:16, 5], fz[0:16, 2], -1.0 / SCALE, None, ALU.mult))
                dve.wait_ge(chunk_used, s["n0"] + 24)
                for i in range(NT):
                    dve.tensor_copy(v_tok[:, i, 512:1024], banks[:, 2 * i + 1, :])

            dve.memset(eps, EPS).then_inc(set_up, 1)
            dve.memset(small[:, 95:96], 0.0).then_inc(set_up, 1)
            dve.wait_ge(inputs_landed, 96)
            norm_runs = 0
            for s in stages:
                kind = s["kind"]
                if kind == "norm":
                    norm(dict(s, k=norm_runs))
                    norm_runs += 1
                elif kind in ("diff_attn", "nsa_attn", "fox_attn"):
                    attend(s, attention_units(kind))
                else:
                    dict(conv_in=conv_in, layernorm=layernorm, peer_topk=peer_topk, peer_gates=peer_gates, dense=dense,
                         kv_proj=kv_proj, q_proj=q_proj, nsa_proj=nsa_proj, nsa_compress=nsa_compress,
                         fox_proj=fox_proj, subln=subln, proj_add=proj_add, proj_keep=lambda s: None,
                         peer_query=lambda s: None, turn_out=lambda s: None)[kind](s)
                end_stage(dve, s)

        @block.gpsimd
        def _(pool):
            steps = Steps(pool, pool_step)

            def norm(s):
                tk_ = tok_slice(s["tokens"])
                into = s.get("into")
                src = mo if into == "add" else h[:, :, tk_]
                dst = src if into else xn[:, :, tk_]
                if into:
                    pool.wait_ge(rstd_ready, s["k"] + 1)
                for c in range(DVE_NORM, NC):
                    steps.mark(pool.tensor_scalar(dst[:, c], src[:, c], vec(s["gain"], s["gi"], c), None, ALU.mult))
                if not into:
                    pool.wait_ge(rstd_ready, s["k"] + 1)
                steps.join()
                for c in range(DVE_NORM, NC):
                    steps.mark(pool.tensor_tensor(dst[:, c], dst[:, c], rstd[:, tk_], ALU.mult))
                if s.get("into") == "add":
                    steps.join()
                    pool.tensor_tensor(h[:, DVE_NORM:, tk_], h[:, DVE_NORM:, tk_], mo[:, DVE_NORM:], ALU.add)

            def conv_in(s):
                pool.memset(glu_u[:, :, 0:CONV_W - 1], 0.0).then_inc(taps_ready, 1)
                pool.wait_ge(taps_ready, 1)
                for i, c in enumerate(POOL_CONV):
                    sums = (conv_y[:, c], conv_odd[:, c])
                    for w in range(2, CONV_W):
                        n = i * (CONV_W - 2) + w - 2
                        pool.wait_ge(product_ready, n + 1)
                        if w >= 4:
                            steps.join(steps.n - 1)
                        ins = pool.tensor_tensor(sums[w % 2], sums[w % 2], products[:, n % PRODUCTS], ALU.add)
                        steps.mark(ins)
                    steps.join()
                    steps.mark(pool.tensor_tensor(sums[0], sums[0], sums[1], ALU.add))

            def peer_topk(s):
                for i, (t0, n) in enumerate(peer_token_tiles(s["tokens"])):
                    k = s["pt0"] + i
                    pool.wait_ge(index_ready, k + 1)
                    steps.link(pool.tensor_copy(tk["idxf"][0:n], tk["idx"][0:n]))
                    f = tk["idxf"][0:n].rearrange("p (h f) r -> p h f r", f=2)
                    steps.link(pool.tensor_scalar(f[:, :, 0], f[:, :, 0], float(KEYS), None, ALU.mult))
                    if i:
                        pool.wait_ge(tile_picks, k)
                    at = 0
                    for a, na, nb in CAND_ROWS:
                        o = tk["code"][0:n, :, at:at + na * nb].rearrange("p h (a b) -> p h a b", b=nb)
                        ins = pool.tensor_tensor(o, f[:, :, 0, a:a + na].unsqueeze(3).broadcast_to([n, HEADS, na, nb]),
                                                 f[:, :, 1, 0:nb].unsqueeze(2).broadcast_to([n, HEADS, na, nb]), ALU.add)
                        at += na * nb
                    ins.then_inc(codes_ready, 1)

            def rope(s, m_count, tokens, dst, cos):
                for m in range(m_count):
                    pool.wait_ge(raw_ready, s["r0"] + m + 1)
                    pool.tensor_tensor(dst(m), raw[:, m % 2, 0:tokens], cos, ALU.mult).then_inc(cos_ready, 1)

            pool.wait_ge(inputs_landed, 96)
            norm_runs = 0
            for s in stages:
                kind = s["kind"]
                if kind == "norm":
                    norm(dict(s, k=norm_runs))
                    norm_runs += 1
                elif kind == "conv_in":
                    conv_in(s)
                elif kind == "peer_topk":
                    peer_topk(s)
                elif kind == "kv_proj":
                    pool.wait_ge(consts_b_landed, 48)
                    rope(s, 8, T0, lambda m: kT[:, m], set_b["rope_cos"])
                elif kind == "q_proj":
                    rope(s, 8, SEQ, lambda m: qT[:, m], set_b["rope_cos"][:, META:T0])
                elif kind == "nsa_proj":
                    pool.wait_ge(consts_c_landed, 80)
                    rope(s, 14, SEQ, nsa_rope_dst, set_c["rope_cos"])
                elif kind == "nsa_compress":
                    block_rows(pool, 1).then_inc(cmp_blocks_ready[1], 1)
                end_stage(pool, s)



def rope_constants(rotated, half, theta, n_tokens, first=0):
    inv = np.float32(theta) ** (-np.arange(0, rotated, 2, dtype=np.float32) / np.float32(rotated))
    ang = np.arange(n_tokens, dtype=np.float32)[:, None] * inv.astype(np.float32)[None, :]
    cos = np.ones((P, n_tokens), np.float32)
    sin = np.zeros((P, n_tokens), np.float32)
    mat = np.zeros((P, P), np.float32)
    for base in (0, 64):
        for f in range(half):
            for p in (base + f, base + half + f):
                cos[p], sin[p] = np.cos(ang[:, f]), np.sin(ang[:, f])
            mat[base + half + f, base + f] = -1.0
            mat[base + f, base + half + f] = 1.0
    return mat, cos, sin


def shape_constants():
    ident = np.eye(P, dtype=np.float32)
    iota = np.broadcast_to(np.arange(P, dtype=np.float32), (P, P))
    iota_c = np.broadcast_to(np.arange(64, dtype=np.float32), (P, 64))
    q = np.arange(P)
    tri = np.where(q[None, :] <= q[:, None], 0.0, NEG).astype(np.float32)
    a = np.concatenate([ident, np.ones((P, P), np.float32), iota, iota_c], axis=1)
    m, c, s = rope_constants(16, 8, 500000.0, T0)
    b = np.concatenate([m, c, s, tri], axis=1)
    m, c, s = rope_constants(64, 32, 10000.0, SEQ)
    ends = np.arange(16) * CMP_STEP + CMP_L - 1
    cmp_mask = np.concatenate([np.where(ends[None, :] <= (t * P + q)[:, None], 0.0, NEG) for t in range(NT)], axis=1)
    row_ok = np.repeat((q >= CMP_L - 1).astype(np.float32)[:, None], 2, axis=1)
    sel = np.zeros((P, 16, SEQ), np.float32)
    for i in range(16):
        sel[i, i] = 1.0
    cc = np.concatenate([m, c, s, tri, cmp_mask.astype(np.float32), row_ok, sel.reshape(P, -1)], axis=1)
    return tuple(np.ascontiguousarray(x, dtype=np.float32) for x in (a, b, cc))


def kernel(**inputs):
    import concourse.bacc as _bacc
    from concourse.bass_utils import run_bass_kernel_spmd as _run

    g = {k: np.asarray(v) for k, v in inputs.items()}

    def by_chunk(w):
        m = w.shape[1] // P
        return w.reshape(NC, P, m, P).transpose(2, 1, 0, 3).reshape(m, P, D)

    def feature_major(x):
        return x.T.reshape(NC, P, -1).transpose(1, 0, 2)

    def head_order():
        return [4 * (2 * pair + b) + r for pair in range(2) for r in range(4) for b in range(2)]

    arrays = {}
    arrays["x"] = feature_major(np.concatenate([g["meta_tokens"], g["x"][0]], axis=0))
    arrays["vecs"] = np.concatenate([g[n].reshape(k * NC, P) for n, k in VEC_LIST], axis=0).T
    arrays["const_a"], arrays["const_b"], arrays["const_c"] = shape_constants()
    arrays["subkeys"] = np.stack([g["f_subkey1"], g["f_subkey2"]], axis=1).reshape(4, KEYS, P).transpose(2, 0, 1)
    nsa, fox = g["nsa_w_in_2"][0], g["fox_w_in_2"][0]
    arrays["gate_w"] = nsa[:, 2560:2608].reshape(NC, P, 48).transpose(1, 0, 2)
    arrays["forget_w"] = fox[:, 3072:3088].reshape(NC, P, 16).transpose(1, 0, 2)
    arrays["forget_b"] = g["fox_b_f_2"].reshape(16, 1)
    lam = np.stack([g[f"b_lambda_{n}"][0] for n in ("q1", "k1", "q2", "k2")])
    arrays["lam_vecs"] = np.repeat(lam[None], P, axis=0)
    arrays["subln_gain"] = np.repeat(g["b_subln_g"], P, axis=0)
    w2 = g["nsa_cmp_w2_2"][0].reshape(2, 2, P, 64)
    arrays["cmp_w2"] = w2.transpose(2, 0, 1, 3)
    arrays["cmp_w2d"] = np.concatenate([w2[0], w2[0]], axis=2).transpose(1, 0, 2)
    pos = g["nsa_cmp_pos_2"][0].reshape(2, 16, 2, 64).transpose(3, 0, 2, 1)
    arrays["cmp_pos"] = np.concatenate([pos, pos], axis=0)
    arrays["peer_u"] = g["f_u"].reshape(2, KEYS, KEYS, NC, P).transpose(0, 2, 4, 3, 1).reshape(2, KEYS, P, D)
    arrays["peer_v"] = g["f_v"]
    arrays["mlp_up"] = np.stack([by_chunk(w) for w in g["mlp_w_up_2"]])
    arrays["mlp_down"] = g["mlp_w_down_2"]

    order = head_order()
    heads = nsa[:, 0:1024].reshape(D, 16, 64)[:, order].reshape(D, D)
    kc, vc, ks, vs, kw, vw = (nsa[:, 1024 + 256 * i:1280 + 256 * i] for i in range(6))
    pw1 = by_chunk(g["a_pw1_w"][0])
    streams = {
        ("conv_in", 0): pw1.reshape(2, NC, P, D).transpose(1, 0, 2, 3).reshape(16, P, D),
        ("proj_add", 0): by_chunk(g["a_pw2_w"][0]),
        ("peer_query", 0): by_chunk(g["f_wq"][0]),
        ("kv_proj", 0): np.concatenate([by_chunk(g["w_kv"][:, 0:D]), g["w_kv"][:, D:].reshape(NC, P, D)]),
        ("q_proj", 0): by_chunk(g["b_wq"][0]),
        ("proj_add", 1): by_chunk(g["b_wo"][0]),
        ("peer_query", 1): by_chunk(g["f_wq"][1]),
        ("nsa_proj", 0): np.concatenate([
            by_chunk(np.concatenate([heads, kc, ks, kw, vc], axis=1)),
            np.concatenate([vs, vw], axis=1).reshape(4, 2, P, 512).transpose(0, 2, 1, 3).reshape(4, P, D)]),
        ("nsa_compress", 0): g["nsa_cmp_w1_2"][0].reshape(2, 4, 4, P, 256).transpose(0, 1, 3, 2, 4).reshape(8, P, D),
        ("proj_keep", 0): by_chunk(g["nsa_w_out_2"][0].reshape(16, 64, D)[order].reshape(D, D)),
        ("fox_proj", 0): np.concatenate([by_chunk(fox[:, 0:2048]), fox[:, 2048:3072].reshape(NC, P, D)]),
        ("proj_keep", 1): by_chunk(g["fox_w_out_2"][0]),
    }

    nc = _bacc.Bacc("TRN2", target_bir_lowering=False, num_devices=1)
    dram, feeds = {}, {}

    def declare(key, name, a):
        a = np.ascontiguousarray(a)
        feeds[name] = a
        dram[key] = nc.dram_tensor(name, a.shape, mybir.dt.from_np(a.dtype), kind="ExternalInput").ap()

    for name, a in arrays.items():
        declare(name, f"in_{name}", a)
    for (kind, k), a in streams.items():
        declare((kind, k), f"w_{kind}_{k}", a)
    out = nc.dram_tensor("out_features", [P, NC, SEQ], F32, kind="ExternalOutput").ap()
    build_program(nc, dram, out)
    r = _run(nc, [feeds], core_ids=[0])
    y = r.results[0]["out_features"]
    return np.ascontiguousarray(y.transpose(2, 1, 0).reshape(1, SEQ, D))
```

```python
from contextlib import ExitStack

import numpy as np

import concourse.bass as bass
from concourse import mybir

F32 = mybir.dt.float32
F32R = mybir.dt.float32r
U32 = mybir.dt.uint32
I32 = mybir.dt.int32
ALU = mybir.AluOpType
ACT = mybir.ActivationFunctionType
AX_X = mybir.AxisListType.X

P = 128
D = 1024
NC = D // P
META = 16
SEQ = 256
T0 = META + SEQ
NT = SEQ // P
CONV_W = 31
EPS = 1e-6
HEADS = 8
TOPK = 16
KEYS = 128
LAM_INIT = float(0.8 - 0.6 * np.exp(-0.3 * 1))
NEG = -1e30
LOWEST = -3e38
CHUNK_SLOTS = 4
HALF = D // 2
SPLITS = 4
FFC = 4096 // P
CMP_L, CMP_STEP = 32, 16
NCMP = (SEQ - CMP_L) // CMP_STEP + 1
GROUPS = 4
SCALE = 0.125
ARENA = T0 * KEYS

CAND_ROWS = [(0, 1, 16), (1, 1, 8), (2, 1, 5), (3, 1, 4), (4, 1, 3), (5, 3, 2), (8, 8, 1)]
NCAND = sum(na * nb for _, na, nb in CAND_ROWS)

VEC_LIST = [("a_norm_g", 1), ("a_pw1_b", 2), ("a_dw_b", 1), ("a_ln_g", 1), ("a_ln_b", 1),
            ("a_pw2_b", 1), ("kv_norm_g", 1), ("b_norm_g", 1), ("f_norm_g", 2), ("final_norm_g", 1), ("norm_g_2", 8)]
VEC = {}
_at = 0
for _name, _n in VEC_LIST:
    VEC[_name] = _at
    _at += NC * _n
NVEC = _at

CONST_A = [("ident", P), ("ones", P), ("iota", P)]
CONST_B = [("rope_mat", P), ("rope_cos", T0), ("rope_sin", T0), ("tri", P)]
CONST_C = [("rope_mat", P), ("rope_cos", SEQ), ("rope_sin", SEQ), ("tri", P), ("cmp_mask", NT * 16), ("row_ok", 2),
           ("head_sel", 16 * SEQ), ("gate_w", NC * 48), ("forget_w", NC * 16)]

STAGES = [
    ("norm", dict(gain="a_norm_g", gi=0, tokens=T0)),
    ("conv_in", dict(chunks=16)),
    ("conv_taps", dict()),
    ("layernorm", dict()),
    ("proj_add", dict(chunks=8, src="xn", bias=True, tokens=T0)),
    ("norm", dict(gain="f_norm_g", gi=0, tokens=T0)),
    ("peer_query", dict(chunks=16, layer=0, tokens=T0)),
    ("peer_topk", dict(layer=0, tokens=T0)),
    ("peer_gates", dict(layer=0, tokens=T0)),
    ("dense", dict(chunks=2 * KEYS, what="peer", tokens=T0, n=KEYS)),
    ("norm", dict(gain="kv_norm_g", gi=0, tokens=T0)),
    ("kv_proj", dict(chunks=16)),
    ("norm", dict(gain="b_norm_g", gi=0, tokens=SEQ)),
    ("q_proj", dict(chunks=8)),
    ("diff_attn", dict()),
    ("subln", dict()),
    ("turn_out", dict()),
    ("proj_add", dict(chunks=8, src="ot", bias=False, tokens=SEQ)),
    ("norm", dict(gain="f_norm_g", gi=1, tokens=SEQ)),
    ("peer_query", dict(chunks=16, layer=1, tokens=SEQ)),
    ("peer_topk", dict(layer=1, tokens=SEQ)),
    ("peer_gates", dict(layer=1, tokens=SEQ)),
    ("dense", dict(chunks=2 * KEYS, what="peer", tokens=SEQ, n=KEYS)),
    ("norm", dict(gain="final_norm_g", gi=0, tokens=SEQ, into="h")),
    ("norm", dict(gain="norm_g_2", gi=0, tokens=SEQ)),
    ("nsa_proj", dict(chunks=20)),
    ("nsa_compress", dict(chunks=8)),
    ("nsa_attn", dict()),
    ("turn_out", dict()),
    ("proj_keep", dict(chunks=8)),
    ("norm", dict(gain="norm_g_2", gi=1, tokens=SEQ, into="add")),
    ("norm", dict(gain="norm_g_2", gi=2, tokens=SEQ)),
    ("dense", dict(chunks=2 * FFC, what="mlp", tokens=SEQ, n=FFC)),
    ("norm", dict(gain="norm_g_2", gi=3, tokens=SEQ, into="add")),
    ("norm", dict(gain="norm_g_2", gi=4, tokens=SEQ)),
    ("fox_proj", dict(chunks=24)),
    ("fox_attn", dict()),
    ("turn_out", dict()),
    ("proj_keep", dict(chunks=8)),
    ("norm", dict(gain="norm_g_2", gi=5, tokens=SEQ, into="add")),
    ("norm", dict(gain="norm_g_2", gi=6, tokens=SEQ)),
    ("dense", dict(chunks=2 * FFC, what="mlp", tokens=SEQ, n=FFC)),
    ("norm", dict(gain="norm_g_2", gi=7, tokens=SEQ, into="add")),
]


def lay_out_stages():
    out, n, seen = [], 0, {}
    bank_frees = rope_chunks = dense_steps = units = peer_tiles = gate_groups = 0
    for at, (kind, q) in enumerate(STAGES):
        s = dict(q, kind=kind, at=at, n0=n, k=seen.get(kind, 0), bf0=bank_frees, r0=rope_chunks, d0=dense_steps,
                 u0=units, pt0=peer_tiles, gg0=gate_groups)
        seen[kind] = s["k"] + 1
        n += q.get("chunks", 0)
        bank_frees += {"proj_add": 8, "proj_keep": 8, "peer_query": 16, "fox_proj": 16}.get(kind, 0)
        rope_chunks += {"kv_proj": 8, "q_proj": 8, "nsa_proj": 14}.get(kind, 0)
        dense_steps += q["n"] if kind == "dense" else 0
        units += {"diff_attn": 16, "nsa_attn": 32, "fox_attn": 16}.get(kind, 0)
        if kind == "peer_topk":
            peer_tiles += len(peer_token_tiles(q["tokens"]))
        if kind == "peer_gates":
            gate_groups += q["tokens"] // 2
        out.append(s)
    return out


N_CHUNKS = sum(q.get("chunks", 0) for _, q in STAGES)


def peer_token_tiles(tokens):
    meta = tokens - SEQ
    return [(meta + P * i, P) for i in range(NT)] + ([(0, meta)] if meta else [])


def build_program(nc, dram, out):
    stages = lay_out_stages()
    with ExitStack() as ctx:
        def sb(name, shape, dt=F32):
            return ctx.enter_context(nc.sbuf_tensor(name, shape, dt))

        def sem(name):
            return ctx.enter_context(nc.semaphore(name))

        h = sb("h", [P, NC, T0])
        x_hi = sb("x_hi", [P, NC, T0], F32R)
        x_lo = sb("x_lo", [P, NC, T0], F32R)
        ring = sb("ring", [P, CHUNK_SLOTS, D])
        vecs = sb("vecs", [P, NVEC])
        const_a = sb("const_a", [P, sum(n for _, n in CONST_A)])
        w_hi = sb("w_hi", [P, SPLITS, HALF], F32R)
        w_lo = sb("w_lo", [P, SPLITS, HALF], F32R)
        gated_hi = sb("gated_hi", [P, 2, T0], F32R)
        gated_lo = sb("gated_lo", [P, 2, T0], F32R)
        work = sb("work", [P, 1024])
        pick = sb("pick", [P, 3, T0])
        small = sb("small", [P, 96])
        arena = sb("arena", [P, ARENA])
        banks = ctx.enter_context(nc.psum_tensor("banks", [P, 8, 512], F32))

        cols = {}
        at = 0
        for name, n in CONST_A:
            cols[name] = const_a[:, at:at + n]
            at += n
        ident, ones, iota = cols["ident"], cols["ones"], cols["iota"]
        iota_cand = iota[:, 0:NCAND]

        class Carve:

            def __init__(self, at=0):
                self.at = at

            def __call__(self, *dims, dt=None):
                n = int(np.prod(dims))
                v = arena[:, self.at:self.at + n]
                self.at += n
                assert self.at <= ARENA
                if dt is not None:
                    v = v.bitcast(dt)
                if len(dims) == 2:
                    v = v.rearrange("p (a b) -> p a b", b=dims[1])
                if len(dims) == 3:
                    v = v.rearrange("p (a b c) -> p a b c", b=dims[1], c=dims[2])
                return v

        top = Carve(ARENA - (NC * T0 + 3 * T0))
        squares = top(NC, T0)
        root, rstd, mean = top(T0), top(T0), top(T0)
        cv = Carve()
        glu_u = cv(NC, CONV_W - 1 + T0)
        conv_y = cv(NC, T0)
        conv_odd = cv(NC, T0)
        glu_sig = cv(2, T0)
        products = cv(4, T0)
        taps = cv(CONV_W * NC)
        pv = Carve()
        peer_q = pv(16, T0)
        subkeys = pv(2, KEYS)
        tk = dict(vals=pv(16, 16), idx=pv(16, 16, dt=U32), idxf=pv(16, 16), rest=pv(16, KEYS),
                  cand=pv(HEADS, NCAND), cand_rest=pv(HEADS, NCAND), code=pv(HEADS, NCAND), best=pv(HEADS, TOPK),
                  pos=pv(HEADS, TOPK, dt=U32), posf=pv(HEADS, TOPK), hit=pv(HEADS * TOPK, NCAND),
                  picked=pv(P), pickedi=pv(P, dt=I32), k1i=pv(P, dt=I32), k2i=pv(P, dt=I32),
                  k1=pv(P), k2=pv(P), ex=pv(HEADS, TOPK), tot=pv(HEADS), inv=pv(HEADS), gate=pv(HEADS, TOPK))
        spread = arena[:, :].rearrange("p (t k) -> p t k", k=KEYS)
        onehot1 = work[:, 0:512].rearrange("p (a t k) -> p a t k", a=2, t=2)
        onehot2 = work[:, 512:1024].rearrange("p (a t k) -> p a t k", a=2, t=2)
        act_out = work[:, 0:2 * T0].rearrange("p (a t) -> p a t", a=2)
        act_gated = work[:, 2 * T0:3 * T0]
        meta_rows = arena[:, 0:D]
        av = Carve()
        qT = av(NC, SEQ)
        kT = av(NC, T0)
        v_tok = av(3, D)
        raw = av(2, T0)
        rot = av(2, T0)
        probs = av(2, 3 * T0)
        probsT = av(2, 1024)
        o_tok = av(NT, D)
        o_sq = av(NT, D)
        mo = o_sq.rearrange("p t n -> p (t n)").rearrange("p (c t) -> p c t", c=NC)
        cb_at = av.at
        const_b = av(sum(n for _, n in CONST_B))
        lam_vecs = av(4, 64)
        subln_gain = av(P)
        lam_tmp = av(2, 64)
        set_b = {}
        at = cb_at
        for name, n in CONST_B:
            set_b[name] = arena[:, at:at + n]
            at += n
        cc = Carve(cb_at)
        cc_at = cc.at
        const_c = cc(sum(n for _, n in CONST_C))
        set_c = {}
        at = cc_at
        for name, n in CONST_C:
            set_c[name] = arena[:, at:at + n]
            at += n
        head_sel = set_c["head_sel"].rearrange("p (h t) -> p h t", t=SEQ)
        gate_w = set_c["gate_w"].rearrange("p (c n) -> p c n", c=NC)
        forget_w = set_c["forget_w"].rearrange("p (c n) -> p c n", c=NC)
        cmp_w2 = cc(2, 2, 64)
        cmp_w2d = cc(2, P)
        cmp_pos = cc(2, 2, 16)
        forget_b = cc(2)
        kcT, ksT, kwT, vcT = (cc(2, SEQ) for _ in range(4))
        blocks = [cc(16, GROUPS * NCMP) for _ in range(2)]
        blocks_hi, blocks_lo = ([x[:, 4 * kv:4 * kv + 4].rearrange("p c t -> p (c t)")[:, 0:16 * GROUPS * NCMP]
                                 .rearrange("p (l n) -> p l n", l=16) for kv in range(2)] for x in (x_hi, x_lo))
        hid = cc(2 * 2, 64)
        kcmpT = cc(64)
        vcmp = cc(GROUPS, 64)
        gates = cc(NT, 48)
        fz = cc(6, SEQ)
        o_mix_at = cc(2 * P)
        assert cc.at <= ARENA - (NC * T0 + 3 * T0)

        eps = small[:, 0:1]
        lam_sum, lam_exp, neg_lam = small[:, 2:4], small[:, 4:6], small[:, 6:7]
        row_max = small[:, 8:16].rearrange("p (a m) -> p a m", a=2)
        neg_max = small[:, 16:24].rearrange("p (a m) -> p a m", a=2)
        row_sum = small[:, 24:36].rearrange("p (a m) -> p a m", a=3)
        coef = small[:, 36:44].rearrange("p (a m) -> p a m", a=2)
        sub_ss, sub_root, sub_rstd = (small[:, 44 + 16 * i:60 + 16 * i] for i in range(3))
        o_mix = o_mix_at.rearrange("p (a b c) -> p a b c", a=1, b=2)

        chunk_landed = [sem(f"chunk_landed{i}") for i in range(CHUNK_SLOTS)]
        hi_ready, lo_ready = sem("hi_ready"), sem("lo_ready")
        half_used = sem("half_used")
        x_scaled, x_hi_ready = sem("x_scaled"), sem("x_hi_ready")
        subkeys_landed = sem("subkeys_landed")
        meta_rows_ready, meta_turned = sem("meta_rows_ready"), sem("meta_turned")
        gated_hi_ready = sem("gated_hi_ready")
        gated_f32_ready = sem("gated_f32_ready")
        blocks_hi_ready, blocks_split = sem("blocks_hi_ready"), sem("blocks_split")
        inputs_landed = sem("inputs_landed")
        consts_b_landed = sem("consts_b_landed")
        consts_c_landed = sem("consts_c_landed")
        out_stored = sem("out_stored")
        stage_done = sem("stage_done")
        set_up = sem("set_up")
        dve_step = sem("dve_step")
        pool_step = sem("pool_step")
        act_step = sem("act_step")
        squares_ready, sum_ready, root_ready, rstd_ready = (sem(n) for n in (
            "squares_ready", "sum_ready", "root_ready", "rstd_ready"))
        bank_free = sem("bank_free")
        glu_gate_ready, glu_done = sem("glu_gate_ready"), sem("glu_done")
        product_ready = sem("product_ready")
        mean_summed, centred, var_summed, ln_root_ready, ln_scaled = (sem(n) for n in (
            "mean_summed", "centred", "var_summed", "ln_root_ready", "ln_scaled"))
        raw_ready, rot_ready, cos_ready, rope_done = (sem(n) for n in ("raw_ready", "rot_ready", "cos_ready", "rope_done"))
        tile_scores, index_ready, codes_ready, tops_ready, exps_ready, tile_picks, picks_turned, picks_stored = (
            sem(n) for n in ("tile_scores", "index_ready", "codes_ready", "tops_ready", "exps_ready", "tile_picks",
                             "picks_turned", "picks_stored"))
        onehots_ready, spread_summed, spread_stored = (sem(n) for n in (
            "onehots_ready", "spread_summed", "spread_stored"))
        act_ready, gated_ready = sem("act_ready"), sem("gated_ready")
        scores_ready, max_ready, exp_done, turned, turned_stored, av_done, mixed = (sem(n) for n in (
            "scores_ready", "max_ready", "exp_done", "turned", "turned_stored", "av_done", "mixed"))
        out_turned, out_hi_ready = sem("out_turned"), sem("out_hi_ready")
        sub_squared, sub_root_ready = sem("sub_squared"), sem("sub_root_ready")
        lam_exps = sem("lam_exps")
        lam_sums = sem("lam_sums")
        gates_summed = sem("gates_summed")
        cmp_blocks_ready = [sem("cmp_keys_ready"), sem("cmp_values_ready")]
        cmp_hidden_ready, cmp_out_summed = sem("cmp_hidden_ready"), sem("cmp_out_summed")
        forget_summed, forget_parts, forget_abs = sem("forget_summed"), sem("forget_parts"), sem("forget_abs")

        block = ctx.enter_context(nc.Block())

        def vec(name, i, c):
            n = VEC[name] + NC * i + c
            return vecs[:, n:n + 1]

        def slot_of(n):
            return n % CHUNK_SLOTS

        def half_of(n, half):
            return (2 * n + half) % SPLITS

        def raw_half(hn):
            return ring[:, slot_of(hn // 2), (hn % 2) * HALF:(hn % 2 + 1) * HALF]

        def plus(base, i, per):
            return base if i is None else i * per + base

        def split_hi(act, hn, i=None):
            if hn >= 2 * N_CHUNKS:
                return
            n = hn // 2
            act.wait_ge(chunk_landed[slot_of(n)], plus(16 * (n // CHUNK_SLOTS + 1), i, 16 * 8 // CHUNK_SLOTS))
            if hn >= SPLITS:
                act.wait_ge(half_used, plus(hn - SPLITS + 1, i, 16))
            act.activation(w_hi[:, hn % SPLITS], raw_half(hn), ACT.Copy).then_inc(hi_ready, 1)

        def split_lo(dve, hn, i=None):
            if hn >= 2 * N_CHUNKS:
                return
            dve.wait_ge(hi_ready, plus(hn + 1, i, 16))
            dve.tensor_tensor(w_lo[:, hn % SPLITS], raw_half(hn), w_hi[:, hn % SPLITS].bitcast(F32), ALU.subtract)\
               .then_inc(lo_ready, 1)

        def follow(split, eng, n, i=None):
            for half in range(2):
                split(eng, 2 * n + half + SPLITS, i)

        def tok_slice(tokens):
            return slice(T0 - tokens, T0)

        class Steps:

            def __init__(self, eng, sem_):
                self.eng, self.sem, self.n = eng, sem_, 0

            def mark(self, ins):
                ins.then_inc(self.sem, 1)
                self.n += 1
                return self.n

            def join(self, n=None):
                self.eng.wait_ge(self.sem, self.n if n is None else n)

            def link(self, ins):
                self.mark(ins)
                self.join()

        def end_stage(eng, s):
            eng.drain().then_inc(stage_done, 1)
            eng.wait_ge(stage_done, 4 * (s["at"] + 1))

        def stage_at(kind, k):
            return next(s["at"] for s in stages if s["kind"] == kind and s["k"] == k)

        DVE_NORM = 5
        POOL_CONV = (1, 3, 5)
        PRODUCTS = 4

        def pool_conv_step(n):
            return n + 1 + n // (CONV_W - 2)

        def conv_taps(eng, steps, c):
            sums = (conv_y[:, c], conv_odd[:, c])
            for w in range(CONV_W):
                src, tap = glu_u[:, c, w:w + T0], taps[:, w * NC + c:w * NC + c + 1]
                o = sums[w % 2]
                if w >= 2:
                    steps.join(steps.n - 1)
                if w == 0:
                    steps.mark(eng.tensor_scalar(o, src, tap, vec("a_dw_b", 0, c), ALU.mult, ALU.add))
                elif w == 1:
                    steps.mark(eng.tensor_scalar(o, src, tap, None, ALU.mult))
                else:
                    steps.mark(eng.scalar_tensor_tensor(out=o, in0=src, scalar=tap, in1=o, op0=ALU.mult, op1=ALU.add))
            steps.join()
            steps.mark(eng.tensor_tensor(sums[0], sums[0], sums[1], ALU.add))

        def scale_rows(eng, s, c, src):
            tk_ = tok_slice(s["tokens"])
            into = s.get("into")
            dst = mo[:, c] if into == "add" else h[:, c, tk_] if into == "h" else squares[:, c, tk_]
            return eng.scalar_tensor_tensor(out=dst, in0=src, scalar=vec(s["gain"], s["gi"], c), in1=rstd[:, tk_],
                                            op0=ALU.mult, op1=ALU.mult)

        head_sel_ones = ones[0:16, 0:1].broadcast_to([16, SEQ])

        def nsa_rope_dst(m):
            return qT[:, m] if m < 8 else (kcT, ksT, kwT)[(m - 8) // 2][:, m % 2]

        def block_rows(eng, kv):
            src = (kcT, vcT)[kv]
            dst = blocks[kv].rearrange("p l (g c) -> p l g c", g=GROUPS)
            for g in range(GROUPS):
                rows = slice(64 * (g % 2), 64 * (g % 2) + 64)
                tokens = src[rows, g // 2].rearrange("p (c l f) -> p l f c", l=8, f=2)
                for par in range(2):
                    for half in range(2):
                        ins = eng.tensor_tensor(
                            dst[64 * par:64 * par + 64, 8 * half:8 * half + 8, g],
                            tokens[:, :, par, half:half + NCMP],
                            cmp_pos[rows, kv, par, 8 * half:8 * half + 8].unsqueeze(2).broadcast_to([64, 8, NCMP]), ALU.add)
            return ins

        def attention_units(kind):
            units = []

            def map_(u, i, q, k, nk, bank, col, add):
                e = probs[:, u % 2, i * T0:i * T0 + nk]
                return dict(q=q, k=k, nk=nk, bank=bank, col=col, add=add, e=e, i=i)

            if kind == "diff_attn":
                for t in range(NT):
                    for hd in range(HEADS):
                        u = len(units)
                        nk = META + P * (t + 1)
                        maps = [map_(u, c, qT[64 * c:64 * c + 64, hd, t * P:(t + 1) * P], kT[64 * c:64 * c + 64, hd, 0:nk],
                                     nk, c, 0, [(ident, set_b["tri"], nk - P, P)]) for c in range(2)]
                        turns, stores, vals = [], [], [[], []]
                        full = nk // P
                        for c in range(2):
                            for kt in range(full + 1):
                                kn = P if kt < full else META
                                bank, col = (0, (c * full + kt) * P) if kt < full else (1, c * P)
                                turns.append((maps[c]["e"][:, kt * P:kt * P + kn], kn, bank, col))
                                vals[c].append((probsT[0:kn, u % 2, 512 * bank + col:512 * bank + col + P],
                                                v_tok[0:kn, kt, hd * P:(hd + 1) * P]))
                        stores = [(P, 0, 2 * full * P), (META, 1, 2 * P)]
                        units.append(dict(kind=kind, tile=t, maps=maps, turns=turns, stores=stores, values=vals, width=P,
                                          maxes=[(banks[:, 2 * (u % 2):2 * (u % 2) + 2, 0:nk], 0, 2)],
                                          out=o_tok[:, t, hd * P:(hd + 1) * P], nmaps=2))
            elif kind == "fox_attn":
                for t in range(NT):
                    for pr in range(8):
                        u = len(units)
                        nk = P * (t + 1)
                        maps = [map_(u, b, qT[64 * b:64 * b + 64, pr, t * P:(t + 1) * P], kT[64 * b:64 * b + 64, pr, 0:nk],
                                     nk, b, 0,
                                     [(fz[0:16, 4, t * P:(t + 1) * P], head_sel[0:16, 2 * pr + b, 0:nk], 0, nk),
                                      (head_sel[0:16, 2 * pr + b, 0:P], fz[0:16, 5, 0:nk], 0, nk),
                                      (ident, set_c["tri"], nk - P, P)]) for b in range(2)]
                        turns, vals = [], [[], []]
                        for b in range(2):
                            for kt in range(t + 1):
                                col = (b * (t + 1) + kt) * P
                                turns.append((maps[b]["e"][:, kt * P:(kt + 1) * P], P, 0, col))
                                hcol = (2 * pr + b) * 64
                                vals[b].append((probsT[:, u % 2, col:col + P], v_tok[:, kt, hcol:hcol + 64]))
                        sc = banks[:, 2 * (u % 2):2 * (u % 2) + 2, 0:nk]
                        units.append(dict(kind=kind, tile=t, maps=maps, turns=turns, stores=[(P, 0, 2 * (t + 1) * P)],
                                          values=vals, width=64, maxes=[(sc, 0, 2)],
                                          out=o_tok[:, t, pr * P:(pr + 1) * P].rearrange("p (b d) -> p b d", b=2), nmaps=2))
            else:
                for t in range(NT):
                    for pair in range(2):
                        for r in range(4):
                            for b in range(2):
                                u = len(units)
                                nk = P * (t + 1)
                                g, j = 2 * pair + b, 4 * pair + r
                                rows = slice(64 * b, 64 * b + 64)
                                q = qT[rows, j, t * P:(t + 1) * P]
                                tri = (ident, set_c["tri"], nk - P, P)
                                maps = [map_(u, 0, q, kcmpT[rows, g * NCMP:(g + 1) * NCMP], NCMP, 1, 0,
                                             [(ident, set_c["cmp_mask"][:, t * 16:t * 16 + NCMP], 0, NCMP)]),
                                        map_(u, 1, q, ksT[rows, pair, 0:nk], nk, 0, 0, [tri]),
                                        map_(u, 2, q, kwT[rows, pair, 0:nk], nk, 0, SEQ, [tri])]
                                turns = [(maps[0]["e"], NCMP, 1, 0)]
                                vals = [[(probsT[0:NCMP, u % 2, 512:512 + P], vcmp[0:NCMP, g, :])], [], []]
                                for i in (1, 2):
                                    for kt in range(t + 1):
                                        col = ((i - 1) * (t + 1) + kt) * P
                                        turns.append((maps[i]["e"][:, kt * P:(kt + 1) * P], P, 0, col))
                                        vc = (i - 1) * 256 + g * 64
                                        vals[i].append((probsT[:, u % 2, col:col + P], v_tok[:, kt, vc:vc + 64]))
                                sc = banks[:, 2 * (u % 2), :].rearrange("p (m n) -> p m n", m=2)[:, :, 0:nk]
                                cmp_sc = banks[:, 2 * (u % 2) + 1, 0:NCMP].unsqueeze(1)
                                units.append(dict(kind=kind, tile=t, maps=maps, turns=turns,
                                                  stores=[(P, 0, 2 * (t + 1) * P), (NCMP, 1, P)], values=vals, width=64,
                                                  maxes=[(cmp_sc, 0, 1), (sc, 1, 2)], head=4 * g + r, nmaps=3,
                                                  out=o_tok[:, t, j * P + b * 64:j * P + b * 64 + 64]))
            return units

        @block.sync
        def _(sp):
            sp.dma_start(h[:, :, :], dram["x"]).then_inc(inputs_landed, 16)
            sp.dma_start(vecs[:, :], dram["vecs"]).then_inc(inputs_landed, 16)
            sp.dma_start(const_a[:, :], dram["const_a"]).then_inc(inputs_landed, 16)
            sp.dma_start(taps, dram["taps"]).then_inc(inputs_landed, 16)

            def load(n, src):
                if n >= CHUNK_SLOTS:
                    sp.wait_ge(lo_ready, 2 * (n - CHUNK_SLOTS + 1))
                sp.dma_start(ring[:, slot_of(n), :], src).then_inc(chunk_landed[slot_of(n)], 16)

            def dense_stream(s, first, second):
                n0, steps = s["n0"], s["n"]
                load(n0, first(0))
                with sp.Fori(0, steps // 4 - 1) as i:
                    for j in range(4):
                        for b, src in ((1, first(i * 4 + (j + 1))), (2, second(i * 4 + j))):
                            n = n0 + 2 * j + b
                            sp.wait_ge(lo_ready, i * 16 + 2 * (n - CHUNK_SLOTS + 1))
                            sp.dma_start(ring[:, slot_of(n), :], src).then_inc(chunk_landed[slot_of(n)], 16)
                for k in range(steps - 3, steps):
                    load(n0 + 2 * k - 1, first(k))
                    load(n0 + 2 * k, second(k - 1))
                load(n0 + 2 * steps - 1, second(steps - 1))

            def row(ap, k):
                return ap[bass.ds(k, 1)].rearrange("a p n -> (a p) n")

            for s in stages:
                kind, n0, k = s["kind"], s["n0"], s["k"]
                if kind == "dense" and s["what"] == "peer":
                    u, v = dram["peer_u"][k], dram["peer_v"][k].rearrange("(a b) d -> b a d", b=KEYS)
                    dense_stream(s, lambda i: row(u, i), lambda i: row(v, i))
                elif kind == "dense":
                    up = dram["mlp_up"][k - 2]
                    down = dram["mlp_down"][k - 2].rearrange("(f p) d -> f p d", p=P)
                    dense_stream(s, lambda i: row(up, i), lambda i: row(down, i))
                elif s.get("chunks"):
                    src = dram[(kind, k)]
                    for m in range(s["chunks"]):
                        load(n0 + m, src[m])
            sp.wait_ge(stage_done, 4 * len(stages))
            sp.dma_start(out, h[:, :, META:T0]).then_inc(out_stored, 16)
            sp.wait_ge(out_stored, 16)

        @block.tensor
        def _(pe):
            def three(out, w_at, xh, xl, start, stop):
                for j, (w, x) in enumerate(((w_hi, xh), (w_hi, xl), (w_lo, xh))):
                    mm = pe.matmul(out, w_at(w), x, start=start and j == 0, stop=stop and j == 2, skip_group_check=True)
                return mm

            def project(n, bank, tokens, i=None):
                tk_ = tok_slice(tokens)
                for half in range(2):
                    pe.wait_ge(lo_ready, plus(2 * n + half + 1, i, 16))
                    for c in range(4):
                        cc_ = 4 * half + c
                        mm = three(banks[:, bank, 0:tokens], lambda w: w[:, half_of(n, half), c * P:(c + 1) * P],
                                   x_hi[:, cc_, tk_], x_lo[:, cc_, tk_], cc_ == 0, cc_ == NC - 1)
                    mm.then_inc(half_used, 1)

            def norm(s):
                tk_ = tok_slice(s["tokens"])
                for half in range(2):
                    pe.wait_ge(squares_ready, 2 * s["k"] + half + 1)
                    for c in range(4 * half, 4 * half + 4):
                        mm = pe.matmul(banks[:, 0, 0:s["tokens"]], ones, squares[:, c, tk_], start=c == 0, stop=c == NC - 1)
                mm.then_inc(sum_ready, 1)

            def conv_in(s):
                for m in range(16):
                    if m >= 4:
                        pe.wait_ge(glu_done, m // 2 - 1)
                    project(s["n0"] + m, m % 4, T0)

            def layernorm(s):
                for c in range(NC):
                    mm = pe.matmul(banks[:, 0, 0:T0], ones, conv_y[:, c], start=c == 0, stop=c == NC - 1)
                mm.then_inc(mean_summed, 1)
                pe.wait_ge(squares_ready, 2 * norm_runs + 1)
                for c in range(NC):
                    mm = pe.matmul(banks[:, 1, 0:T0], ones, squares[:, c], start=c == 0, stop=c == NC - 1)
                mm.then_inc(var_summed, 1)

            def proj(s, tokens):
                for m in range(s["chunks"]):
                    if m >= 4:
                        pe.wait_ge(bank_free, s["bf0"] + m - 3)
                    project(s["n0"] + m, m % 4, tokens)

            def peer_topk(s):
                pe.wait_ge(subkeys_landed, 16 * (s["layer"] + 1))
                lo = T0 - s["tokens"]
                tiles = peer_token_tiles(s["tokens"])

                def scores(i):
                    t0, n = tiles[i]
                    if i >= 2:
                        pe.wait_ge(picks_stored, s["pt0"] + i - 1)
                    for m in range(16):
                        b = 4 * (i % 2) + m // 4
                        mm = pe.matmul(banks[0:n, b, (m % 4) * KEYS:(m % 4 + 1) * KEYS], peer_q[:, m, lo + t0:lo + t0 + n],
                                       subkeys[:, m % 2, :], start=True, stop=True)
                    mm.then_inc(tile_scores, 1)

                def turn(i):
                    t0, n = tiles[i]
                    pe.wait_ge(tile_picks, s["pt0"] + i + 1)
                    for j, src in enumerate((tk["k1"], tk["k2"], tk["gate"].rearrange("p a b -> p (a b)"))):
                        mm = pe.transpose(banks[:, 4 * (i % 2), j * P:j * P + n], src[0:n, :], ident[0:n, 0:n])
                    mm.then_inc(picks_turned, 1)

                scores(0)
                scores(1)
                for i in range(len(tiles)):
                    turn(i)
                    if i + 2 < len(tiles):
                        scores(i + 2)

            def peer_gates(s):
                def groups(i, first=False):
                    for b in range(2):
                        g = 2 * i + b if first else i * 2 + b
                        pe.wait_ge(onehots_ready, g + (s["gg0"] + 1))
                        if not first:
                            pe.wait_ge(spread_stored, g + (s["gg0"] - 1))
                        for t in range(2):
                            mm = pe.matmul(banks[:, b, t * KEYS:(t + 1) * KEYS], onehot1[:, b, t], onehot2[:, b, t],
                                           start=True, stop=True)
                        mm.then_inc(spread_summed, 1)

                groups(0, first=True)
                with pe.Fori(1, s["tokens"] // 4) as i:
                    groups(i)

            def dense(s):
                n0, d0, steps, tokens = s["n0"], s["d0"], s["n"], s["tokens"]
                meta = tokens - SEQ

                def up(b, n, freed, i=None):
                    if freed is not None:
                        pe.wait_ge(act_ready, plus(freed, i, 4))
                    project(n, 6 + b, tokens, i)

                def down(b, n, ready, first, last, i=None):
                    pe.wait_ge(gated_ready, plus(ready, i, 4))
                    for half in range(2):
                        pe.wait_ge(lo_ready, plus(2 * n + half + 1, i, 16))
                        for c4 in range(4):
                            c = 4 * half + c4
                            at_ = lambda w: w[:, half_of(n, half), c4 * P:(c4 + 1) * P]
                            mm = three(banks[:, c // 2, (c % 2) * SEQ:(c % 2 + 1) * SEQ], at_, gated_hi[:, b, meta:tokens],
                                       gated_lo[:, b, meta:tokens], first and c % 2 == 0, last)
                        if meta:
                            for j, (x, w) in enumerate(((gated_hi, w_hi), (gated_lo, w_hi), (gated_hi, w_lo))):
                                mm = pe.matmul(banks[0:meta, 4 + half, :], x[:, b, 0:meta], w[:, half_of(n, half)],
                                               start=first and j == 0, stop=last and j == 2, skip_group_check=True)
                        mm.then_inc(half_used, 1)

                up(0, n0, None)
                for k in range(1, 5):
                    up(k % 2, n0 + 2 * k - 1, d0 + k - 1 if k >= 2 else None)
                    down((k - 1) % 2, n0 + 2 * k, d0 + k, k == 1, False)
                with pe.Fori(1, steps // 4 - 1) as i:
                    for j in range(4):
                        up((j + 1) % 2, n0 + 2 * j + 1, d0 + j, i)
                        down(j % 2, n0 + 2 * j + 2, d0 + j + 1, False, False, i)
                for k in range(steps - 3, steps):
                    up(k % 2, n0 + 2 * k - 1, d0 + k - 1)
                    down((k - 1) % 2, n0 + 2 * k, d0 + k, False, False)
                down((steps - 1) % 2, n0 + 2 * steps - 1, d0 + steps, False, True)
                if meta:
                    pe.wait_ge(meta_rows_ready, 1)
                    for c in range(NC):
                        mm = pe.transpose(banks[:, 6, c * META:(c + 1) * META], meta_rows[0:META, c * P:(c + 1) * P],
                                          ident[0:META, 0:META])
                    mm.then_inc(meta_turned, 1)

            def rope_projections(s, n0, m_count, tokens, mat, r_at=0):
                r0 = s["r0"] + r_at

                def rotate(m):
                    pe.wait_ge(raw_ready, r0 + m + 1)
                    if m >= 2:
                        pe.wait_ge(rope_done, r0 + m - 1)
                    pe.matmul(banks[:, 4 + m % 2, 0:tokens], mat, raw[:, m % 2, 0:tokens],
                              start=True, stop=True).then_inc(rot_ready, 1)

                for m in range(m_count):
                    if m >= 4:
                        pe.wait_ge(raw_ready, r0 + m - 3)
                    project(n0 + m, m % 4, tokens)
                    if m >= 1:
                        rotate(m - 1)
                rotate(m_count - 1)

            def values(n0, per_chunk, width, tiles, first_bank=0):
                halves = width // 512
                for n in range(NC // per_chunk):
                    for half in range(2):
                        pe.wait_ge(lo_ready, 2 * (n0 + n) + half + 1)
                        c = n * per_chunk + (half if per_chunk == 2 else 0)
                        at_ = half_of(n0 + n, half)
                        for i, (t0, m) in enumerate(tiles):
                            o = banks[0:m, first_bank + halves * i + (half if halves == 2 else 0), :]
                            for j, (x, w) in enumerate(((x_hi, w_hi), (x_lo, w_hi), (x_hi, w_lo))):
                                mm = pe.matmul(o, x[:, c, t0:t0 + m], w[:, at_], start=c == 0 and j == 0,
                                               stop=c == NC - 1 and j == 2, skip_group_check=True)
                        mm.then_inc(half_used, 1)

            def kv_proj(s):
                pe.wait_ge(consts_b_landed, 48)
                rope_projections(s, s["n0"], 8, T0, set_b["rope_mat"])
                pe.wait_ge(raw_ready, s["r0"] + 8)
                pe.wait_ge(rope_done, s["r0"] + 8)
                values(s["n0"] + 8, 1, D, [(0, P), (P, P), (2 * P, META)])

            def q_proj(s):
                rope_projections(s, s["n0"], 8, SEQ, set_b["rope_mat"])

            def nsa_proj(s):
                pe.wait_ge(consts_c_landed, 80)
                rope_projections(s, s["n0"], 14, SEQ, set_c["rope_mat"])
                pe.wait_ge(raw_ready, s["r0"] + 14)
                pe.wait_ge(rope_done, s["r0"] + 14)
                for m in range(2):
                    project(s["n0"] + 14 + m, m, SEQ)
                values(s["n0"] + 16, 2, 512, [(META + P * i, P) for i in range(NT)], first_bank=2)
                for i in range(NT):
                    for c in range(NC):
                        mm = pe.matmul(banks[:, 4 + i, 0:48], squares[:, c, META + P * i:META + P * (i + 1)], gate_w[:, c],
                                       start=c == 0, stop=c == NC - 1)
                mm.then_inc(gates_summed, 1)

            def nsa_compress(s):
                for kv in range(2):
                    pe.wait_ge(blocks_split, kv + 1)
                    for q in range(8):
                        n, half = s["n0"] + 4 * kv + q // 2, q % 2
                        pe.wait_ge(lo_ready, 2 * n + half + 1)
                        for j in range(2):
                            lp = 2 * q + j
                            for m in range(2):
                                mm = three(banks[:, 2 * kv + m, 0:GROUPS * NCMP],
                                           lambda w: w[:, half_of(n, half), j * 256 + m * P:j * 256 + (m + 1) * P],
                                           blocks_hi[kv][:, lp], blocks_lo[kv][:, lp], lp == 0, lp == 15)
                        mm.then_inc(half_used, 1)
                pe.wait_ge(cmp_hidden_ready, 1)
                for m in range(2):
                    pe.matmul(banks[:, 4, 0:GROUPS * NCMP], cmp_w2d[:, m], hid[:, m, 0:GROUPS * NCMP],
                              start=m == 0, stop=m == 1)
                for g in range(GROUPS):
                    for m in range(2):
                        mm = pe.matmul(banks[0:NCMP, 5, g * 64:(g + 1) * 64], hid[:, 2 + m, g * NCMP:(g + 1) * NCMP],
                                       cmp_w2[:, 1, m], start=m == 0, stop=m == 1, skip_group_check=True)
                mm.then_inc(cmp_out_summed, 1)

            def attend(s, units):
                u0 = s["u0"]

                def scores(u):
                    if u >= 2:
                        pe.wait_ge(exp_done, u0 + u - 1)
                    for mp in units[u]["maps"]:
                        o = banks[:, 2 * (u % 2) + mp["bank"], mp["col"]:mp["col"] + mp["nk"]]
                        mm = pe.matmul(o, mp["q"], mp["k"], start=True, stop=not mp["add"], skip_group_check=True)
                        for j, (lhsT, rhs, c0, w) in enumerate(mp["add"]):
                            mm = pe.matmul(o[:, c0:c0 + w], lhsT, rhs, start=False, stop=j == len(mp["add"]) - 1,
                                           skip_group_check=True)
                    mm.then_inc(scores_ready, 1)

                def turn(u):
                    pe.wait_ge(exp_done, u0 + u + 1)
                    if u >= 1:
                        pe.wait_ge(turned_stored, u0 + u)
                    for (src, kn, bank, col) in units[u]["turns"]:
                        mm = pe.transpose(banks[0:kn, 4 + bank, col:col + P], src, ident)
                    mm.then_inc(turned, 1)

                def weigh(u):
                    pe.wait_ge(turned_stored, u0 + u + 1)
                    if u >= 2:
                        pe.wait_ge(mixed, u0 + u - 1)
                    for i, parts in enumerate(units[u]["values"]):
                        for j, (lhsT, v) in enumerate(parts):
                            w = units[u]["width"]
                            mm = pe.matmul(banks[:, 6 + u % 2, i * w:(i + 1) * w], lhsT, v, start=j == 0,
                                           stop=j == len(parts) - 1, skip_group_check=True)
                    mm.then_inc(av_done, 1)

                for u in range(len(units) + 2):
                    if u < len(units):
                        scores(u)
                    if 1 <= u <= len(units):
                        turn(u - 1)
                    if u >= 2:
                        weigh(u - 2)

            def turn_out(s):
                for i in range(NT):
                    for half in range(2):
                        for c in range(4 * half, 4 * half + 4):
                            mm = pe.transpose(banks[:, 2 * i + half, (c % 4) * P:(c % 4 + 1) * P],
                                              o_tok[:, i, c * P:(c + 1) * P], ident)
                        mm.then_inc(out_turned, 1)

            def fox_proj(s):
                for m in range(16):
                    if m >= 4:
                        pe.wait_ge(bank_free, s["bf0"] + m - 3)
                    project(s["n0"] + m, m % 4, SEQ)
                for c in range(NC):
                    mm = pe.matmul(banks[0:16, 4, 0:SEQ], forget_w[:, c], squares[:, c, META:T0], start=c == 0, stop=c == NC - 1)
                mm.then_inc(forget_summed, 1)
                pe.wait_ge(bank_free, s["bf0"] + 16)
                values(s["n0"] + 16, 1, D, [(META + P * i, P) for i in range(NT)])

            pe.wait_ge(inputs_landed, 64)
            norm_runs = 0
            for s in stages:
                kind = s["kind"]
                if kind == "norm":
                    norm(dict(s, k=norm_runs))
                    norm_runs += 1
                elif kind == "layernorm":
                    layernorm(s)
                    norm_runs += 1
                elif kind == "conv_in":
                    conv_in(s)
                elif kind == "proj_add":
                    proj(s, s["tokens"])
                elif kind == "proj_keep":
                    proj(s, SEQ)
                elif kind == "peer_query":
                    proj(s, s["tokens"])
                elif kind in ("diff_attn", "nsa_attn", "fox_attn"):
                    attend(s, attention_units(kind))
                else:
                    dict(peer_topk=peer_topk, peer_gates=peer_gates, dense=dense, kv_proj=kv_proj, q_proj=q_proj,
                         nsa_proj=nsa_proj, nsa_compress=nsa_compress, turn_out=turn_out, fox_proj=fox_proj,
                         subln=lambda s: None, conv_taps=lambda s: None)[kind](s)
                end_stage(pe, s)

        @block.scalar
        def _(act):
            steps = Steps(act, act_step)
            norm_runs = 0

            def norm(s, src):
                tk_ = tok_slice(s["tokens"])
                for half in range(2):
                    act.activation(squares[:, 4 * half:4 * half + 4, tk_], src[:, 4 * half:4 * half + 4], ACT.Square)\
                       .then_inc(squares_ready, 1)
                act.wait_ge(sum_ready, s["k"] - ln_runs + 1)
                act.activation(root[:, tk_], banks[:, 0, 0:s["tokens"]], ACT.Sqrt, bias=eps, scale=1.0 / D)\
                   .then_inc(root_ready, 1)
                if not s.get("into"):
                    for c in range(NC):
                        act.wait_ge(x_scaled, 8 * s["xk"] + c + 1)
                        act.activation(x_hi[:, c, tk_], squares[:, c, tk_], ACT.Copy).then_inc(x_hi_ready, 1)

            def weigh_taps(c, taps_):
                for w in taps_:
                    n = POOL_CONV.index(c) * (CONV_W - 2) + w - 2
                    dst = (conv_y[:, c], conv_odd[:, c])[w] if w < 2 else products[:, n % PRODUCTS]
                    if w >= 2 and n >= PRODUCTS:
                        act.wait_ge(pool_step, pool_conv_step(n - PRODUCTS))
                    src, tap = glu_u[:, c, w:w + T0], taps[:, w * NC + c:w * NC + c + 1]
                    if w == 0:
                        act.activation(dst, src, ACT.Identity, bias=vec("a_dw_b", 0, c), scale=tap)
                    else:
                        ins = act.activation(dst, src, ACT.Copy, scale=tap)
                        if w >= 2:
                            ins.then_inc(product_ready, 1)

            def conv_in(s):
                for p_ in range(8):
                    follow(split_hi, act, s["n0"] + 2 * p_)
                    follow(split_hi, act, s["n0"] + 2 * p_ + 1)
                    act.wait_ge(half_used, 2 * (s["n0"] + 2 * p_ + 2))
                    if p_ >= 2:
                        act.wait_ge(glu_done, p_ - 1)
                    act.activation(glu_sig[:, p_ % 2], banks[:, (2 * p_ + 1) % 4, 0:T0], ACT.Sigmoid,
                                   bias=vec("a_pw1_b", 1, p_)).then_inc(glu_gate_ready, 1)

            def conv_taps_(s):
                for c in POOL_CONV:
                    weigh_taps(c, range(CONV_W))

            def layernorm(s):
                act.wait_ge(centred, 1)
                act.activation(squares[:, :, :], conv_y[:, :, :], ACT.Square).then_inc(squares_ready, 2)
                act.wait_ge(var_summed, 1)
                act.activation(root[:, :], banks[:, 1, 0:T0], ACT.Sqrt, bias=eps, scale=1.0 / D).then_inc(ln_root_ready, 1)
                for c in range(NC):
                    act.wait_ge(ln_scaled, c + 1)
                    steps.mark(act.activation(squares[:, c], squares[:, c], ACT.Silu, bias=vec("a_ln_b", 0, c),
                                              scale=vec("a_ln_g", 0, c)))
                steps.join()
                for c in range(NC):
                    act.activation(x_hi[:, c], squares[:, c], ACT.Copy).then_inc(x_hi_ready, 1)

            def keep(s, dst, tokens):
                for m in range(s["chunks"] if s["kind"] != "fox_proj" else 16):
                    follow(split_hi, act, s["n0"] + m)
                    act.wait_ge(half_used, 2 * (s["n0"] + m + 1))
                    act.activation(dst(m), banks[:, m % 4, 0:tokens], ACT.Copy).then_inc(bank_free, 1)

            def peer_topk(s):
                for i, (t0, n) in enumerate(peer_token_tiles(s["tokens"])):
                    act.wait_ge(tops_ready, s["pt0"] + i + 1)
                    act.activation(tk["ex"][0:n], tk["ex"][0:n], ACT.Exp).then_inc(exps_ready, 1)
                    act.wait_ge(picks_turned, s["pt0"] + i + 1)
                    src = banks[:, 4 * (i % 2), 0:3 * P].rearrange("p (j t) -> p j t", j=3)[:, :, 0:n]
                    act.activation(pick[:, :, t0:t0 + n], src, ACT.Copy).then_inc(picks_stored, 1)

            def peer_gates(s):
                def groups(i):
                    for b in range(2):
                        g = i * 2 + b
                        act.wait_ge(spread_summed, g + (s["gg0"] + 1))
                        act.activation(arena[:, bass.ds(g * 256, 256)], banks[:, b, 0:256], ACT.Copy).then_inc(spread_stored, 1)

                with act.Fori(0, s["tokens"] // 4) as i:
                    groups(i)

            def dense(s):
                n0, d0, steps_, tokens = s["n0"], s["d0"], s["n"], s["tokens"]
                func = ACT.Gelu if s["what"] == "peer" else ACT.Relu

                def one(b, k, n, freed, i=None):
                    if n > n0 or i is not None:
                        follow(split_hi, act, n, i)
                    act.wait_ge(half_used, plus(2 * n + 2, i, 16))
                    if freed is not None:
                        act.wait_ge(gated_f32_ready, plus(freed, i, 4))
                    act.activation(act_out[:, b, 0:tokens], banks[:, 6 + b, 0:tokens], func).then_inc(act_ready, 1)
                    if n > n0 or i is not None:
                        split_hi(act, 2 * (n + 1) + SPLITS, i)
                    act.wait_ge(gated_f32_ready, plus(d0 + k + 1, i, 4))
                    act.activation(gated_hi[:, b, 0:tokens], act_gated[:, 0:tokens], ACT.Copy).then_inc(gated_hi_ready, 1)
                    if n > n0 or i is not None:
                        split_hi(act, 2 * (n + 1) + 1 + SPLITS, i)

                follow(split_hi, act, n0)
                one(0, 0, n0, None)
                for k in range(1, 5):
                    one(k % 2, k, n0 + 2 * k - 1, d0 + k - 1 if k >= 2 else None)
                with act.Fori(1, steps_ // 4 - 1) as i:
                    for k in range(1, 5):
                        one(k % 2, k, n0 + 2 * k - 1, d0 + k - 1, i)
                for k in range(steps_ - 3, steps_):
                    one(k % 2, k, n0 + 2 * k - 1, d0 + k - 1)
                follow(split_hi, act, n0 + 2 * steps_ - 1)

            def rope(s, n0, m_count, tokens, r_at=0):
                r0 = s["r0"] + r_at
                for m in range(m_count):
                    follow(split_hi, act, n0 + m)
                    act.wait_ge(half_used, 2 * (n0 + m + 1))
                    if m >= 2:
                        act.wait_ge(rope_done, r0 + m - 1)
                    act.activation(raw[:, m % 2, 0:tokens], banks[:, m % 4, 0:tokens], ACT.Copy).then_inc(raw_ready, 1)

            def kv_proj(s):
                rope(s, s["n0"], 8, T0)
                for m in range(8, 16):
                    follow(split_hi, act, s["n0"] + m)
                act.wait_ge(half_used, 2 * (s["n0"] + 16))
                for i, m in enumerate((P, P, META)):
                    act.activation(v_tok[0:m, i, 0:512], banks[0:m, 2 * i, :], ACT.Copy)

            def diff_lambda():
                act.wait_ge(lam_sums, 1)
                act.activation(lam_exp, lam_sum, ACT.Exp).then_inc(lam_exps, 1)

            def nsa_proj(s):
                rope(s, s["n0"], 14, SEQ)
                for m in range(2):
                    follow(split_hi, act, s["n0"] + 14 + m)
                    act.wait_ge(half_used, 2 * (s["n0"] + 14 + m + 1))
                    act.activation(vcT[:, m], banks[:, m, 0:SEQ], ACT.Copy)
                for m in range(16, 20):
                    follow(split_hi, act, s["n0"] + m)
                act.wait_ge(gates_summed, 1)
                act.activation(gates[:, :, :], banks[:, 4:6, 0:48], ACT.Sigmoid)

            def nsa_compress(s):
                for kv in range(2):
                    act.wait_ge(cmp_blocks_ready[kv], 1)
                    act.activation(blocks_hi[kv], blocks[kv], ACT.Copy).then_inc(blocks_hi_ready, 1)
                for kv in range(2):
                    for m in range(4):
                        follow(split_hi, act, s["n0"] + 4 * kv + m)
                    act.wait_ge(half_used, 2 * (s["n0"] + 4 * kv + 4))
                    ins = act.activation(hid[:, 2 * kv:2 * kv + 2, 0:GROUPS * NCMP],
                                         banks[:, 2 * kv:2 * kv + 2, 0:GROUPS * NCMP], ACT.Silu)
                ins.then_inc(cmp_hidden_ready, 1)
                act.wait_ge(cmp_out_summed, 1)
                act.activation(kcmpT[:, 0:GROUPS * NCMP], banks[:, 4, 0:GROUPS * NCMP], ACT.Copy)
                act.activation(vcmp[0:NCMP, :, :], banks[0:NCMP, 5, 0:256].rearrange("p (g d) -> p g d", g=GROUPS), ACT.Copy)

            def attend(s, units):
                u0 = s["u0"]

                def store(u):
                    act.wait_ge(turned, u0 + u + 1)
                    if u >= 2:
                        act.wait_ge(av_done, u0 + u - 1)
                    for rows, bank, width in units[u]["stores"]:
                        ins = act.activation(probsT[0:rows, u % 2, 512 * bank:512 * bank + width],
                                             banks[0:rows, 4 + bank, 0:width], ACT.Copy)
                    ins.then_inc(turned_stored, 1)

                for u in range(len(units) + 1):
                    if u < len(units):
                        act.wait_ge(max_ready, u0 + u + 1)
                        if u >= 2:
                            act.wait_ge(turned, u0 + u - 1)
                        if u >= 3:
                            act.wait_ge(mixed, u0 + u - 2)
                        for mp in units[u]["maps"]:
                            i = mp["i"]
                            ins = act.activation(mp["e"], banks[:, 2 * (u % 2) + mp["bank"], mp["col"]:mp["col"] + mp["nk"]],
                                                 ACT.Exp, bias=neg_max[:, u % 2, i:i + 1], scale=SCALE,
                                                 accum_out=row_sum[:, u % 3, i:i + 1])
                        ins.then_inc(exp_done, 1)
                    if u >= 1:
                        store(u - 1)

            def subln(s):
                act.wait_ge(sub_squared, 1)
                act.activation(sub_root, sub_ss, ACT.Sqrt, bias=eps, scale=1.0 / P).then_inc(sub_root_ready, 1)

            def turn_out(s):
                for i in range(NT):
                    for half in range(2):
                        act.wait_ge(out_turned, 4 * s["k"] + 2 * i + half + 1)
                        act.activation(x_hi[:, 4 * half:4 * half + 4, META + i * P:META + (i + 1) * P],
                                       banks[:, 2 * i + half, :].rearrange("p (c t) -> p c t", c=4), ACT.Copy)\
                           .then_inc(out_hi_ready, 1)

            def fox_proj(s):
                keep(s, lambda m: qT[:, m] if m < 8 else kT[:, m - 8, 0:SEQ], SEQ)
                act.wait_ge(forget_parts, 1)
                steps.link(act.activation(fz[0:16, 1], fz[0:16, 0], ACT.Abs))
                steps.link(act.activation(fz[0:16, 1], fz[0:16, 1], ACT.Exp, scale=-1.0))
                act.activation(fz[0:16, 2], fz[0:16, 1], ACT.Ln, bias=1.0).then_inc(forget_abs, 1)
                for m in range(16, 24):
                    follow(split_hi, act, s["n0"] + m)
                act.wait_ge(half_used, 2 * (s["n0"] + 24))
                for i in range(NT):
                    act.activation(v_tok[:, i, 0:512], banks[:, 2 * i, :], ACT.Copy)

            act.wait_ge(inputs_landed, 64)
            act.wait_ge(set_up, 2)
            ln_runs = x_runs = 0
            for hn in range(SPLITS):
                split_hi(act, hn)
            for s in stages:
                kind = s["kind"]
                if kind == "norm":
                    norm(dict(s, k=norm_runs, xk=x_runs), mo if s.get("into") == "add" else h[:, :, tok_slice(s["tokens"])])
                    norm_runs += 1
                    x_runs += not s.get("into")
                elif kind == "layernorm":
                    layernorm(s)
                    norm_runs += 1
                    ln_runs += 1
                elif kind == "proj_add":
                    for m in range(s["chunks"]):
                        follow(split_hi, act, s["n0"] + m)
                elif kind == "proj_keep":
                    keep(s, lambda m: mo[:, m], SEQ)
                elif kind == "peer_query":
                    keep(s, lambda m, s=s: peer_q[:, m, tok_slice(s["tokens"])], s["tokens"])
                elif kind == "q_proj":
                    rope(s, s["n0"], 8, SEQ)
                    diff_lambda()
                elif kind in ("diff_attn", "nsa_attn", "fox_attn"):
                    attend(s, attention_units(kind))
                else:
                    dict(conv_in=conv_in, peer_topk=peer_topk, peer_gates=peer_gates, dense=dense, kv_proj=kv_proj,
                         nsa_proj=nsa_proj, nsa_compress=nsa_compress, turn_out=turn_out, fox_proj=fox_proj,
                         subln=subln, conv_taps=conv_taps_)[kind](s)
                end_stage(act, s)

        @block.vector
        def _(dve):
            steps = Steps(dve, dve_step)

            def norm(s):
                tk_ = tok_slice(s["tokens"])
                dve.wait_ge(root_ready, s["k"] + 1)
                dve.reciprocal(rstd[:, tk_], root[:, tk_]).then_inc(rstd_ready, 1)
                dve.wait_ge(rstd_ready, s["k"] + 1)
                if not s.get("into"):
                    for c in range(NC):
                        scale_rows(dve, s, c, h[:, c, tk_]).then_inc(x_scaled, 1)
                    return
                for c in range(DVE_NORM):
                    steps.mark(scale_rows(dve, s, c, mo[:, c] if s.get("into") == "add" else h[:, c, tk_]))
                if s.get("into") == "add":
                    steps.join()
                    dve.tensor_tensor(h[:, 0:DVE_NORM, tk_], h[:, 0:DVE_NORM, tk_], mo[:, 0:DVE_NORM], ALU.add)

            def conv_in(s):
                for p_ in range(8):
                    follow(split_lo, dve, s["n0"] + 2 * p_)
                    follow(split_lo, dve, s["n0"] + 2 * p_ + 1)
                    dve.wait_ge(glu_gate_ready, p_ + 1)
                    dve.scalar_tensor_tensor(out=glu_u[:, p_, CONV_W - 1:], in0=banks[:, (2 * p_) % 4, 0:T0],
                                             scalar=vec("a_pw1_b", 0, p_), in1=glu_sig[:, p_ % 2],
                                             op0=ALU.add, op1=ALU.mult).then_inc(glu_done, 1)

            def layernorm(s):
                dve.wait_ge(mean_summed, 1)
                steps.link(dve.tensor_scalar(mean[:, :], banks[:, 0, 0:T0], 1.0 / D, None, ALU.mult))
                dve.tensor_tensor(conv_y[:, :, :], conv_y[:, :, :], mean.unsqueeze(1).broadcast_to([P, NC, T0]),
                                  ALU.subtract).then_inc(centred, 1)
                dve.wait_ge(ln_root_ready, 1)
                steps.link(dve.reciprocal(rstd[:, :], root[:, :]))
                for c in range(NC):
                    dve.tensor_tensor(squares[:, c], conv_y[:, c], rstd[:, :], ALU.mult).then_inc(ln_scaled, 1)

            def proj_add(s):
                tk_ = tok_slice(s["tokens"])
                for m in range(8):
                    follow(split_lo, dve, s["n0"] + m)
                    dve.wait_ge(half_used, 2 * (s["n0"] + m + 1))
                    src, dst = banks[:, m % 4, 0:s["tokens"]], h[:, m, tk_]
                    if s["bias"]:
                        ins = dve.scalar_tensor_tensor(out=dst, in0=src, scalar=vec("a_pw2_b", 0, m), in1=dst,
                                                       op0=ALU.add, op1=ALU.add)
                    else:
                        ins = dve.tensor_tensor(dst, src, dst, ALU.add)
                    ins.then_inc(bank_free, 1)

            def top16(n, src, vals, idx, rest, count):
                for m in range(count):
                    steps.mark(dve.max(vals[0:n, m, 0:8], src(m)))
                steps.join()
                for m in range(count):
                    steps.mark(dve.max_index(idx[0:n, m, 0:8], vals[0:n, m, 0:8], src(m)))
                    steps.mark(dve.match_replace(rest[0:n, m], vals[0:n, m, 0:8], src(m), LOWEST))
                steps.join()
                for m in range(count):
                    steps.mark(dve.max(vals[0:n, m, 8:16], rest[0:n, m]))
                steps.join()
                for m in range(count):
                    last = dve.max_index(idx[0:n, m, 8:16], vals[0:n, m, 8:16], rest[0:n, m])
                    if m < count - 1:
                        steps.mark(last)
                return last

            def peer_topk(s):
                for i, (t0, n) in enumerate(peer_token_tiles(s["tokens"])):
                    k = s["pt0"] + i
                    dve.wait_ge(tile_scores, k + 1)
                    src = lambda m: banks[0:n, 4 * (i % 2) + m // 4, (m % 4) * KEYS:(m % 4 + 1) * KEYS]
                    if i:
                        dve.wait_ge(codes_ready, k)
                    top16(n, src, tk["vals"], tk["idx"], tk["rest"], 16).then_inc(index_ready, 1)
                    at = 0
                    v = tk["vals"][0:n].rearrange("p (h f) r -> p h f r", f=2)
                    for a, na, nb in CAND_ROWS:
                        o = tk["cand"][0:n, :, at:at + na * nb].rearrange("p h (a b) -> p h a b", b=nb)
                        steps.mark(dve.tensor_tensor(o, v[:, :, 0, a:a + na].unsqueeze(3).broadcast_to([n, HEADS, na, nb]),
                                                     v[:, :, 1, 0:nb].unsqueeze(2).broadcast_to([n, HEADS, na, nb]), ALU.add))
                        at += na * nb
                    steps.join()
                    steps.link(top16(n, lambda m: tk["cand"][0:n, m], tk["best"], tk["pos"], tk["cand_rest"], HEADS))
                    best = tk["best"][0:n]
                    dve.tensor_tensor(tk["ex"][0:n], best, best[:, :, 0:1].broadcast_to([n, HEADS, TOPK]), ALU.subtract)\
                       .then_inc(tops_ready, 1)
                    steps.link(dve.tensor_copy(tk["posf"][0:n], tk["pos"][0:n]))
                    hit = tk["hit"][0:n]
                    flat = tk["posf"][0:n].rearrange("p h j -> p (h j)")
                    steps.link(dve.tensor_tensor(hit, iota_cand[0:n].unsqueeze(1).broadcast_to([n, P, NCAND]),
                                                 flat.unsqueeze(2).broadcast_to([n, P, NCAND]), ALU.is_equal))
                    dve.wait_ge(codes_ready, k + 1)
                    hit4 = hit.rearrange("p (h j) c -> p h j c", h=HEADS)
                    steps.link(dve.tensor_tensor(hit4, hit4, tk["code"][0:n].unsqueeze(2).broadcast_to([n, HEADS, TOPK, NCAND]),
                                                 ALU.mult))
                    steps.link(dve.reduce_sum(tk["picked"][0:n], hit, AX_X))
                    steps.link(dve.tensor_copy(tk["pickedi"][0:n], tk["picked"][0:n]))
                    if i:
                        dve.wait_ge(picks_turned, k)
                    steps.mark(dve.tensor_scalar(tk["k1i"][0:n], tk["pickedi"][0:n], 7, None, ALU.logical_shift_right))
                    steps.link(dve.tensor_scalar(tk["k2i"][0:n], tk["pickedi"][0:n], 127, None, ALU.bitwise_and))
                    steps.mark(dve.tensor_copy(tk["k1"][0:n], tk["k1i"][0:n]))
                    steps.mark(dve.tensor_copy(tk["k2"][0:n], tk["k2i"][0:n]))
                    dve.wait_ge(exps_ready, k + 1)
                    steps.link(dve.reduce_sum(tk["tot"][0:n], tk["ex"][0:n], AX_X))
                    steps.link(dve.reciprocal(tk["inv"][0:n], tk["tot"][0:n]))
                    dve.tensor_tensor(tk["gate"][0:n], tk["ex"][0:n],
                                      tk["inv"][0:n].unsqueeze(2).broadcast_to([n, HEADS, TOPK]), ALU.mult)\
                       .then_inc(tile_picks, 1)

            def peer_gates(s):
                def groups(i, first=False):
                    for b in range(2):
                        if not first:
                            dve.wait_ge(spread_summed, i * 2 + (b + s["gg0"] - 1))
                        for t in range(2):
                            at = i * 4 + (2 * b + t)
                            dve.tensor_scalar(onehot1[:, b, t], iota, pick[:, 0, bass.ds(at, 1)], None, ALU.is_equal)
                            ins = dve.tensor_scalar(onehot2[:, b, t], iota, pick[:, 1, bass.ds(at, 1)],
                                                    pick[:, 2, bass.ds(at, 1)], ALU.is_equal, ALU.mult)
                        ins.then_inc(onehots_ready, 1)

                groups(0, first=True)
                with dve.Fori(1, s["tokens"] // 4) as i:
                    groups(i)

            def dense(s):
                d0, n, tokens = s["d0"], s["n"], s["tokens"]
                meta = tokens - SEQ

                def one(b, k, n, i=None):
                    n0_ = s["n0"]
                    if n > n0_ or i is not None:
                        follow(split_lo, dve, n, i)
                    dve.wait_ge(act_ready, plus(d0 + k + 1, i, 4))
                    a, o = act_out[:, b, 0:tokens], act_gated[:, 0:tokens]
                    if k >= 1:
                        dve.wait_ge(gated_ready, plus(d0 + k, i, 4))
                    step = k if i is None else i * 4 + k
                    g = spread[:, 0:tokens, bass.ds(step, 1)].rearrange("p t k -> p (t k)") if s["what"] == "peer" else a
                    dve.tensor_tensor(o, a, g, ALU.mult).then_inc(gated_f32_ready, 1)
                    if n > n0_ or i is not None:
                        split_lo(dve, 2 * (n + 1) + SPLITS, i)
                    dve.wait_ge(gated_hi_ready, plus(d0 + k + 1, i, 4))
                    dve.tensor_tensor(gated_lo[:, b, 0:tokens], o, gated_hi[:, b, 0:tokens].bitcast(F32), ALU.subtract)\
                       .then_inc(gated_ready, 1)
                    if n > n0_ or i is not None:
                        split_lo(dve, 2 * (n + 1) + 1 + SPLITS, i)

                follow(split_lo, dve, s["n0"])
                one(0, 0, s["n0"])
                for k in range(1, 5):
                    one(k % 2, k, s["n0"] + 2 * k - 1)
                with dve.Fori(1, n // 4 - 1) as i:
                    for k in range(1, 5):
                        one(k % 2, k, s["n0"] + 2 * k - 1, i)
                for k in range(n - 3, n):
                    one(k % 2, k, s["n0"] + 2 * k - 1)
                follow(split_lo, dve, s["n0"] + 2 * n - 1)
                dve.wait_ge(half_used, 2 * (s["n0"] + 2 * n))
                if meta:
                    dve.tensor_copy(meta_rows[0:META, :].rearrange("p (a n) -> p a n", a=2), banks[0:META, 4:6, :])\
                       .then_inc(meta_rows_ready, 1)
                dst = h[:, :, META:T0] if s["what"] == "peer" else mo
                for b in range(4):
                    src = banks[:, b, :].rearrange("p (c t) -> p c t", c=2)
                    if s["what"] == "peer":
                        dve.tensor_tensor(dst[:, 2 * b:2 * b + 2], dst[:, 2 * b:2 * b + 2], src, ALU.add)
                    else:
                        dve.tensor_copy(dst[:, 2 * b:2 * b + 2], src)
                if meta:
                    dve.wait_ge(meta_turned, 1)
                    dve.tensor_tensor(h[:, :, 0:META], h[:, :, 0:META],
                                      banks[:, 6, 0:NC * META].rearrange("p (c t) -> p c t", c=NC), ALU.add)

            def rope(s, m_count, tokens, dst, sin):
                for m in range(m_count):
                    follow(split_lo, dve, s["n0"] + m)
                    dve.wait_ge(rot_ready, s["r0"] + m + 1)
                    steps.link(dve.tensor_tensor(rot[:, m % 2, 0:tokens], banks[:, 4 + m % 2, 0:tokens], sin, ALU.mult))
                    dve.wait_ge(cos_ready, s["r0"] + m + 1)
                    dve.tensor_tensor(dst(m), dst(m), rot[:, m % 2, 0:tokens], ALU.add).then_inc(rope_done, 1)

            def kv_proj(s):
                dve.wait_ge(consts_b_landed, 48)
                rope(s, 8, T0, lambda m: kT[:, m], set_b["rope_sin"])
                for m in range(8, 16):
                    follow(split_lo, dve, s["n0"] + m)
                dve.wait_ge(half_used, 2 * (s["n0"] + 16))
                for i, m in enumerate((P, P, META)):
                    dve.tensor_copy(v_tok[0:m, i, 512:1024], banks[0:m, 2 * i + 1, :])

            def q_proj(s):
                for j in range(2):
                    steps.link(dve.tensor_tensor(lam_tmp[:, j], lam_vecs[:, 2 * j], lam_vecs[:, 2 * j + 1], ALU.mult))
                dve.reduce_sum(lam_sum, lam_tmp, AX_X).then_inc(lam_sums, 1)
                rope(s, 8, SEQ, lambda m: qT[:, m], set_b["rope_sin"][:, META:T0])
                dve.wait_ge(lam_exps, 1)
                steps.link(dve.tensor_tensor(neg_lam, lam_exp[:, 1:2], lam_exp[:, 0:1], ALU.subtract))
                steps.link(dve.tensor_scalar(neg_lam, neg_lam, -LAM_INIT, None, ALU.add))

            def nsa_proj(s):
                dve.wait_ge(consts_c_landed, 80)
                rope(s, 14, SEQ, nsa_rope_dst, set_c["rope_sin"])
                for m in range(14, 20):
                    follow(split_lo, dve, s["n0"] + m)
                dve.wait_ge(half_used, 2 * (s["n0"] + 20))
                for i in range(NT):
                    dve.tensor_copy(v_tok[:, i, 0:512], banks[:, 2 + i, :])

            def nsa_compress(s):
                steps.link(dve.tensor_scalar(gates[:, 0, :].rearrange("p (h i) -> p h i", i=3)[:, :, 0],
                                             gates[:, 0, :].rearrange("p (h i) -> p h i", i=3)[:, :, 0],
                                             set_c["row_ok"][:, 0:1], None, ALU.mult))
                block_rows(dve, 0).then_inc(cmp_blocks_ready[0], 1)
                for kv in range(2):
                    dve.wait_ge(blocks_hi_ready, kv + 1)
                    dve.tensor_tensor(blocks_lo[kv], blocks[kv], blocks_hi[kv].bitcast(F32), ALU.subtract)\
                       .then_inc(blocks_split, 1)
                for m in range(8):
                    follow(split_lo, dve, s["n0"] + m)

            def attend(s, units):
                u0 = s["u0"]

                def mix(u):
                    un = units[u]
                    n, w = un["nmaps"], un["width"]
                    part = lambda i: banks[:, 6 + u % 2, i * w:(i + 1) * w]
                    cf, sums = coef[:, u % 2, 0:n], row_sum[:, u % 3, 0:n]
                    dve.wait_ge(av_done, u0 + u + 1)
                    steps.link(dve.reciprocal(cf, sums))
                    if un["kind"] == "fox_attn":
                        for i in range(2):
                            ins = dve.tensor_scalar(un["out"][:, i], part(i), cf[:, i:i + 1], None, ALU.mult)
                    elif un["kind"] == "diff_attn":
                        steps.link(dve.tensor_tensor(cf[:, 1:2], cf[:, 1:2], neg_lam, ALU.mult))
                        steps.link(dve.tensor_scalar(o_mix[:, 0, 0], part(1), cf[:, 1:2], None, ALU.mult))
                        ins = dve.scalar_tensor_tensor(out=un["out"], in0=part(0), scalar=cf[:, 0:1], in1=o_mix[:, 0, 0],
                                                       op0=ALU.mult, op1=ALU.add)
                    else:
                        hd = un["head"]
                        steps.link(dve.tensor_tensor(cf, cf, gates[:, un["tile"], 3 * hd:3 * hd + 3], ALU.mult))
                        steps.link(dve.tensor_scalar(o_mix[:, 0, 0, 0:w], part(0), cf[:, 0:1], None, ALU.mult))
                        steps.link(dve.scalar_tensor_tensor(out=o_mix[:, 0, 1, 0:w], in0=part(1), scalar=cf[:, 1:2],
                                                            in1=o_mix[:, 0, 0, 0:w], op0=ALU.mult, op1=ALU.add))
                        ins = dve.scalar_tensor_tensor(out=un["out"], in0=part(2), scalar=cf[:, 2:3],
                                                       in1=o_mix[:, 0, 1, 0:w], op0=ALU.mult, op1=ALU.add)
                    ins.then_inc(mixed, 1)

                for u in range(len(units) + 2):
                    if u < len(units):
                        un = units[u]
                        dve.wait_ge(scores_ready, u0 + u + 1)
                        if u >= 2:
                            dve.wait_ge(exp_done, u0 + u - 1)
                        for src, c0, n in un["maxes"]:
                            steps.mark(dve.reduce_max(row_max[:, u % 2, c0:c0 + n], src, AX_X))
                        steps.join()
                        n = un["nmaps"]
                        dve.tensor_scalar(neg_max[:, u % 2, 0:n], row_max[:, u % 2, 0:n], -SCALE, None, ALU.mult)\
                           .then_inc(max_ready, 1)
                    if u >= 2:
                        mix(u - 2)

            def subln(s):
                o3 = o_tok.rearrange("p t (h e) -> p (t h) e", h=HEADS)
                sq3 = o_sq.rearrange("p t (h e) -> p (t h) e", h=HEADS)
                full = [P, NT * HEADS, P]
                steps.link(dve.tensor_tensor(sq3, o3, o3, ALU.mult))
                dve.reduce_sum(sub_ss, sq3, AX_X).then_inc(sub_squared, 1)
                dve.wait_ge(sub_root_ready, 1)
                steps.link(dve.reciprocal(sub_rstd, sub_root))
                steps.link(dve.tensor_scalar(lam_tmp.rearrange("p a b -> p (a b)"), subln_gain, 1.0 - LAM_INIT, None, ALU.mult))
                steps.link(dve.tensor_tensor(o3, o3, sub_rstd.unsqueeze(2).broadcast_to(full), ALU.mult))
                steps.link(dve.tensor_tensor(o3, o3, lam_tmp.rearrange("p a b -> p (a b)").unsqueeze(1).broadcast_to(full), ALU.mult))

            def turn_out(s):
                for i in range(NT):
                    for half in range(2):
                        cs, ts = slice(4 * half, 4 * half + 4), slice(META + i * P, META + (i + 1) * P)
                        dve.wait_ge(out_hi_ready, 4 * s["k"] + 2 * i + half + 1)
                        dve.tensor_tensor(x_lo[:, cs, ts], banks[:, 2 * i + half, :].rearrange("p (c t) -> p c t", c=4),
                                          x_hi[:, cs, ts].bitcast(F32), ALU.subtract)

            def fox_proj(s):
                for m in range(16):
                    follow(split_lo, dve, s["n0"] + m)
                dve.wait_ge(forget_summed, 1)
                steps.link(dve.tensor_scalar(fz[0:16, 0], banks[0:16, 4, 0:SEQ], forget_b[0:16, 0:1], None, ALU.add))
                dve.tensor_scalar(fz[0:16, 3], fz[0:16, 0], 0.0, None, ALU.min).then_inc(forget_parts, 1)
                dve.wait_ge(forget_abs, 1)
                steps.link(dve.tensor_tensor(fz[0:16, 3], fz[0:16, 3], fz[0:16, 2], ALU.subtract))
                steps.link(dve.tensor_tensor_scan(fz[0:16, 2], head_sel_ones, fz[0:16, 3], 0.0, ALU.mult, ALU.add))
                steps.mark(dve.tensor_scalar(fz[0:16, 4], fz[0:16, 2], 1.0 / SCALE, None, ALU.mult))
                steps.mark(dve.tensor_scalar(fz[0:16, 5], fz[0:16, 2], -1.0 / SCALE, None, ALU.mult))
                for m in range(16, 24):
                    follow(split_lo, dve, s["n0"] + m)
                dve.wait_ge(half_used, 2 * (s["n0"] + 24))
                for i in range(NT):
                    dve.tensor_copy(v_tok[:, i, 512:1024], banks[:, 2 * i + 1, :])

            dve.memset(eps, EPS).then_inc(set_up, 1)
            dve.memset(small[:, 95:96], 0.0).then_inc(set_up, 1)
            dve.wait_ge(inputs_landed, 64)
            norm_runs = 0
            for hn in range(SPLITS):
                split_lo(dve, hn)
            for s in stages:
                kind = s["kind"]
                if kind == "norm":
                    norm(dict(s, k=norm_runs))
                    norm_runs += 1
                elif kind in ("diff_attn", "nsa_attn", "fox_attn"):
                    attend(s, attention_units(kind))
                elif kind in ("proj_keep", "peer_query"):
                    for m in range(s["chunks"]):
                        follow(split_lo, dve, s["n0"] + m)
                elif kind == "conv_taps":
                    for c in range(NC):
                        if c not in POOL_CONV:
                            conv_taps(dve, steps, c)
                else:
                    dict(conv_in=conv_in, layernorm=layernorm, peer_topk=peer_topk, peer_gates=peer_gates, dense=dense,
                         kv_proj=kv_proj, q_proj=q_proj, nsa_proj=nsa_proj, nsa_compress=nsa_compress,
                         fox_proj=fox_proj, subln=subln, proj_add=proj_add, turn_out=turn_out)[kind](s)
                end_stage(dve, s)

        @block.gpsimd
        def _(pool):
            steps = Steps(pool, pool_step)

            def remainder(tk_, k):
                for c in range(NC):
                    pool.wait_ge(x_hi_ready, 8 * k + c + 1)
                    pool.tensor_tensor(x_lo[:, c, tk_], squares[:, c, tk_], x_hi[:, c, tk_].bitcast(F32), ALU.subtract)

            def norm(s):
                tk_ = tok_slice(s["tokens"])
                into = s.get("into")
                if not into:
                    remainder(tk_, s["xk"])
                    return
                dst = src = mo if into == "add" else h[:, :, tk_]
                pool.wait_ge(rstd_ready, s["k"] + 1)
                for c in range(DVE_NORM, NC):
                    steps.mark(pool.tensor_scalar(dst[:, c], src[:, c], vec(s["gain"], s["gi"], c), None, ALU.mult))
                steps.join()
                for c in range(DVE_NORM, NC):
                    steps.mark(pool.tensor_tensor(dst[:, c], dst[:, c], rstd[:, tk_], ALU.mult))
                if s.get("into") == "add":
                    steps.join()
                    pool.tensor_tensor(h[:, DVE_NORM:, tk_], h[:, DVE_NORM:, tk_], mo[:, DVE_NORM:], ALU.add)

            def conv_in(s):
                pool.memset(glu_u[:, :, 0:CONV_W - 1], 0.0)

            def conv_taps_(s):
                for i, c in enumerate(POOL_CONV):
                    sums = (conv_y[:, c], conv_odd[:, c])
                    for w in range(2, CONV_W):
                        n = i * (CONV_W - 2) + w - 2
                        pool.wait_ge(product_ready, n + 1)
                        if w >= 4:
                            steps.join(steps.n - 1)
                        ins = pool.tensor_tensor(sums[w % 2], sums[w % 2], products[:, n % PRODUCTS], ALU.add)
                        steps.mark(ins)
                    steps.join()
                    steps.mark(pool.tensor_tensor(sums[0], sums[0], sums[1], ALU.add))

            def peer_topk(s):
                for i, (t0, n) in enumerate(peer_token_tiles(s["tokens"])):
                    k = s["pt0"] + i
                    pool.wait_ge(index_ready, k + 1)
                    steps.link(pool.tensor_copy(tk["idxf"][0:n], tk["idx"][0:n]))
                    f = tk["idxf"][0:n].rearrange("p (h f) r -> p h f r", f=2)
                    steps.link(pool.tensor_scalar(f[:, :, 0], f[:, :, 0], float(KEYS), None, ALU.mult))
                    if i:
                        pool.wait_ge(tile_picks, k)
                    at = 0
                    for a, na, nb in CAND_ROWS:
                        o = tk["code"][0:n, :, at:at + na * nb].rearrange("p h (a b) -> p h a b", b=nb)
                        ins = pool.tensor_tensor(o, f[:, :, 0, a:a + na].unsqueeze(3).broadcast_to([n, HEADS, na, nb]),
                                                 f[:, :, 1, 0:nb].unsqueeze(2).broadcast_to([n, HEADS, na, nb]), ALU.add)
                        at += na * nb
                    ins.then_inc(codes_ready, 1)

            def rope(s, m_count, tokens, dst, cos):
                for m in range(m_count):
                    pool.wait_ge(raw_ready, s["r0"] + m + 1)
                    pool.tensor_tensor(dst(m), raw[:, m % 2, 0:tokens], cos, ALU.mult).then_inc(cos_ready, 1)

            pool.wait_ge(inputs_landed, 64)
            norm_runs = x_runs = 0
            for s in stages:
                kind = s["kind"]
                if kind == "norm" and s["gain"] == "kv_norm_g":
                    pool.dma_start(const_b, dram["const_b"]).then_inc(consts_b_landed, 16)
                    pool.dma_start(lam_vecs, dram["lam_vecs"]).then_inc(consts_b_landed, 16)
                    pool.dma_start(subln_gain, dram["subln_gain"]).then_inc(consts_b_landed, 16)
                if kind == "norm" and s["gain"] == "final_norm_g":
                    pool.dma_start(const_c, dram["const_c"]).then_inc(consts_c_landed, 16)
                    pool.dma_start(cmp_w2, dram["cmp_w2"]).then_inc(consts_c_landed, 16)
                    pool.dma_start(cmp_w2d, dram["cmp_w2d"]).then_inc(consts_c_landed, 16)
                    pool.dma_start(cmp_pos, dram["cmp_pos"]).then_inc(consts_c_landed, 16)
                    pool.dma_start(forget_b[0:16, 0:1], dram["forget_b"]).then_inc(consts_c_landed, 16)
                if kind == "peer_query":
                    pool.dma_start(subkeys, dram["subkeys"][:, 2 * s["layer"]:2 * s["layer"] + 2])\
                        .then_inc(subkeys_landed, 16)
                if kind == "norm":
                    norm(dict(s, k=norm_runs, xk=x_runs))
                    norm_runs += 1
                    x_runs += not s.get("into")
                elif kind == "layernorm":
                    remainder(slice(0, T0), x_runs)
                    x_runs += 1
                elif kind == "conv_taps":
                    conv_taps_(s)
                elif kind == "conv_in":
                    conv_in(s)
                elif kind == "peer_topk":
                    peer_topk(s)
                elif kind == "kv_proj":
                    pool.wait_ge(consts_b_landed, 48)
                    rope(s, 8, T0, lambda m: kT[:, m], set_b["rope_cos"])
                elif kind == "q_proj":
                    rope(s, 8, SEQ, lambda m: qT[:, m], set_b["rope_cos"][:, META:T0])
                elif kind == "nsa_proj":
                    pool.wait_ge(consts_c_landed, 80)
                    rope(s, 14, SEQ, nsa_rope_dst, set_c["rope_cos"])
                elif kind == "nsa_compress":
                    block_rows(pool, 1).then_inc(cmp_blocks_ready[1], 1)
                end_stage(pool, s)



def rope_constants(rotated, half, theta, n_tokens, first=0):
    inv = np.float32(theta) ** (-np.arange(0, rotated, 2, dtype=np.float32) / np.float32(rotated))
    ang = np.arange(n_tokens, dtype=np.float32)[:, None] * inv.astype(np.float32)[None, :]
    cos = np.ones((P, n_tokens), np.float32)
    sin = np.zeros((P, n_tokens), np.float32)
    mat = np.zeros((P, P), np.float32)
    for base in (0, 64):
        for f in range(half):
            for p in (base + f, base + half + f):
                cos[p], sin[p] = np.cos(ang[:, f]), np.sin(ang[:, f])
            mat[base + half + f, base + f] = -1.0
            mat[base + f, base + half + f] = 1.0
    return mat, cos, sin


def shape_constants():
    ident = np.eye(P, dtype=np.float32)
    iota = np.broadcast_to(np.arange(P, dtype=np.float32), (P, P))
    q = np.arange(P)
    tri = np.where(q[None, :] <= q[:, None], 0.0, NEG).astype(np.float32)
    a = np.concatenate([ident, np.ones((P, P), np.float32), iota], axis=1)
    m, c, s = rope_constants(16, 8, 500000.0, T0)
    b = np.concatenate([m, c, s, tri], axis=1)
    m, c, s = rope_constants(64, 32, 10000.0, SEQ)
    ends = np.arange(16) * CMP_STEP + CMP_L - 1
    cmp_mask = np.concatenate([np.where(ends[None, :] <= (t * P + q)[:, None], 0.0, NEG) for t in range(NT)], axis=1)
    row_ok = np.repeat((q >= CMP_L - 1).astype(np.float32)[:, None], 2, axis=1)
    sel = np.zeros((P, 16, SEQ), np.float32)
    for i in range(16):
        sel[i, i] = 1.0
    cc = np.concatenate([m, c, s, tri, cmp_mask.astype(np.float32), row_ok, sel.reshape(P, -1)], axis=1)
    return tuple(np.ascontiguousarray(x, dtype=np.float32) for x in (a, b, cc))


def kernel(**inputs):
    import concourse.bacc as _bacc
    from concourse.bass_utils import run_bass_kernel_spmd as _run

    g = {k: np.asarray(v) for k, v in inputs.items()}

    def by_chunk(w):
        m = w.shape[1] // P
        return w.reshape(NC, P, m, P).transpose(2, 1, 0, 3).reshape(m, P, D)

    def feature_major(x):
        return x.T.reshape(NC, P, -1).transpose(1, 0, 2)

    def head_order():
        return [4 * (2 * pair + b) + r for pair in range(2) for r in range(4) for b in range(2)]

    arrays = {}
    arrays["x"] = feature_major(np.concatenate([g["meta_tokens"], g["x"][0]], axis=0))
    arrays["vecs"] = np.concatenate([g[n].reshape(k * NC, P) for n, k in VEC_LIST], axis=0).T
    arrays["taps"] = g["a_dw_w"].reshape(CONV_W * NC, P).T
    arrays["const_a"], arrays["const_b"], arrays["const_c"] = shape_constants()
    arrays["subkeys"] = np.stack([g["f_subkey1"], g["f_subkey2"]], axis=1).reshape(4, KEYS, P).transpose(2, 0, 1)
    nsa, fox = g["nsa_w_in_2"][0], g["fox_w_in_2"][0]
    arrays["const_c"] = np.concatenate([
        arrays["const_c"], nsa[:, 2560:2608].reshape(NC, P, 48).transpose(1, 0, 2).reshape(P, -1),
        fox[:, 3072:3088].reshape(NC, P, 16).transpose(1, 0, 2).reshape(P, -1)], axis=1)
    arrays["forget_b"] = g["fox_b_f_2"].reshape(16, 1)
    lam = np.stack([g[f"b_lambda_{n}"][0] for n in ("q1", "k1", "q2", "k2")])
    arrays["lam_vecs"] = np.repeat(lam[None], P, axis=0)
    arrays["subln_gain"] = np.repeat(g["b_subln_g"], P, axis=0)
    w2 = g["nsa_cmp_w2_2"][0].reshape(2, 2, P, 64)
    arrays["cmp_w2"] = w2.transpose(2, 0, 1, 3)
    arrays["cmp_w2d"] = np.concatenate([w2[0], w2[0]], axis=2).transpose(1, 0, 2)
    pos = g["nsa_cmp_pos_2"][0].reshape(2, 16, 2, 64).transpose(3, 0, 2, 1)
    arrays["cmp_pos"] = np.concatenate([pos, pos], axis=0)
    arrays["peer_u"] = g["f_u"].reshape(2, KEYS, KEYS, NC, P).transpose(0, 2, 4, 3, 1).reshape(2, KEYS, P, D)
    arrays["peer_v"] = g["f_v"]
    arrays["mlp_up"] = np.stack([by_chunk(w) for w in g["mlp_w_up_2"]])
    arrays["mlp_down"] = g["mlp_w_down_2"]

    order = head_order()
    heads = nsa[:, 0:1024].reshape(D, 16, 64)[:, order].reshape(D, D)
    kc, vc, ks, vs, kw, vw = (nsa[:, 1024 + 256 * i:1280 + 256 * i] for i in range(6))
    pw1 = by_chunk(g["a_pw1_w"][0])
    streams = {
        ("conv_in", 0): pw1.reshape(2, NC, P, D).transpose(1, 0, 2, 3).reshape(16, P, D),
        ("proj_add", 0): by_chunk(g["a_pw2_w"][0]),
        ("peer_query", 0): by_chunk(g["f_wq"][0]),
        ("kv_proj", 0): np.concatenate([by_chunk(g["w_kv"][:, 0:D]), g["w_kv"][:, D:].reshape(NC, P, D)]),
        ("q_proj", 0): by_chunk(g["b_wq"][0]),
        ("proj_add", 1): by_chunk(g["b_wo"][0]),
        ("peer_query", 1): by_chunk(g["f_wq"][1]),
        ("nsa_proj", 0): np.concatenate([
            by_chunk(np.concatenate([heads, kc, ks, kw, vc], axis=1)),
            np.concatenate([vs, vw], axis=1).reshape(4, 2, P, 512).transpose(0, 2, 1, 3).reshape(4, P, D)]),
        ("nsa_compress", 0): g["nsa_cmp_w1_2"][0].reshape(2, 4, 4, P, 256).transpose(0, 1, 3, 2, 4).reshape(8, P, D),
        ("proj_keep", 0): by_chunk(g["nsa_w_out_2"][0].reshape(16, 64, D)[order].reshape(D, D)),
        ("fox_proj", 0): np.concatenate([by_chunk(fox[:, 0:2048]), fox[:, 2048:3072].reshape(NC, P, D)]),
        ("proj_keep", 1): by_chunk(g["fox_w_out_2"][0]),
    }

    nc = _bacc.Bacc("TRN2", target_bir_lowering=False, num_devices=1)
    dram, feeds = {}, {}

    def declare(key, name, a):
        a = np.ascontiguousarray(a)
        feeds[name] = a
        dram[key] = nc.dram_tensor(name, a.shape, mybir.dt.from_np(a.dtype), kind="ExternalInput").ap()

    for name, a in arrays.items():
        declare(name, f"in_{name}", a)
    for (kind, k), a in streams.items():
        declare((kind, k), f"w_{kind}_{k}", a)
    out = nc.dram_tensor("out_features", [P, NC, SEQ], F32, kind="ExternalOutput").ap()
    build_program(nc, dram, out)
    r = _run(nc, [feeds], core_ids=[0])
    y = r.results[0]["out_features"]
    return np.ascontiguousarray(y.transpose(2, 1, 0).reshape(1, SEQ, D))
```

```python
from contextlib import ExitStack

import numpy as np

import concourse.bass as bass
from concourse import mybir

F32 = mybir.dt.float32
F32R = mybir.dt.float32r
U32 = mybir.dt.uint32
I32 = mybir.dt.int32
ALU = mybir.AluOpType
ACT = mybir.ActivationFunctionType
AX_X = mybir.AxisListType.X

P = 128
D = 1024
NC = D // P
META = 16
SEQ = 256
T0 = META + SEQ
NT = SEQ // P
CONV_W = 31
EPS = 1e-6
HEADS = 8
TOPK = 16
KEYS = 128
LAM_INIT = float(0.8 - 0.6 * np.exp(-0.3 * 1))
NEG = -1e30
LOWEST = -3e38
CHUNK_SLOTS = 4
HALF = D // 2
SPLITS = 4
FFC = 4096 // P
CMP_L, CMP_STEP = 32, 16
NCMP = (SEQ - CMP_L) // CMP_STEP + 1
GROUPS = 4
SCALE = 0.125
ARENA = T0 * KEYS

CAND_ROWS = [(0, 1, 16), (1, 1, 8), (2, 1, 5), (3, 1, 4), (4, 1, 3), (5, 3, 2), (8, 8, 1)]
NCAND = sum(na * nb for _, na, nb in CAND_ROWS)

VEC_LIST = [("a_norm_g", 1), ("a_pw1_b", 2), ("a_dw_b", 1), ("a_ln_g", 1), ("a_ln_b", 1),
            ("a_pw2_b", 1), ("kv_norm_g", 1), ("b_norm_g", 1), ("f_norm_g", 2), ("final_norm_g", 1), ("norm_g_2", 8)]
VEC = {}
_at = 0
for _name, _n in VEC_LIST:
    VEC[_name] = _at
    _at += NC * _n
NVEC = _at

CONST_A = [("ident", P), ("ones", P), ("iota", P)]
CONST_B = [("rope_mat", P), ("rope_cos", T0), ("rope_sin", T0), ("tri", P)]
CONST_C = [("rope_mat", P), ("rope_cos", SEQ), ("rope_sin", SEQ), ("tri", P), ("cmp_mask", NT * 16), ("row_ok", 2),
           ("head_sel", 16 * SEQ), ("gate_w", NC * 48), ("forget_w", NC * 16)]

EARLY_PARTS = ((12, 8, 8), (12, 8))
GATE_LOOPS = 3
EARLY = tuple(sum(parts) + 4 * GATE_LOOPS for parts in EARLY_PARTS)

STAGES = [
    ("norm", dict(gain="a_norm_g", gi=0, tokens=T0)),
    ("conv_in", dict(chunks=16)),
    ("conv_taps", dict()),
    ("layernorm", dict()),
    ("proj_add", dict(chunks=8, src="xn", bias=True, tokens=T0)),
    ("norm", dict(gain="f_norm_g", gi=0, tokens=T0)),
    ("peer_query", dict(chunks=16, layer=0, tokens=T0)),
    ("peer_select", dict(layer=0, tokens=T0, early_parts=EARLY_PARTS[0])),
    ("dense", dict(chunks=2 * KEYS - EARLY[0], what="peer", tokens=T0, n=KEYS, early=EARLY[0], layer=0)),
    ("norm", dict(gain="kv_norm_g", gi=0, tokens=T0)),
    ("kv_proj", dict(chunks=16)),
    ("norm", dict(gain="b_norm_g", gi=0, tokens=SEQ)),
    ("q_proj", dict(chunks=8)),
    ("diff_attn", dict()),
    ("subln", dict()),
    ("turn_out", dict()),
    ("proj_add", dict(chunks=8, src="ot", bias=False, tokens=SEQ)),
    ("norm", dict(gain="f_norm_g", gi=1, tokens=SEQ)),
    ("peer_query", dict(chunks=16, layer=1, tokens=SEQ)),
    ("peer_select", dict(layer=1, tokens=SEQ, early_parts=EARLY_PARTS[1])),
    ("dense", dict(chunks=2 * KEYS - EARLY[1], what="peer", tokens=SEQ, n=KEYS, early=EARLY[1], layer=1)),
    ("norm", dict(gain="final_norm_g", gi=0, tokens=SEQ, into="h")),
    ("norm", dict(gain="norm_g_2", gi=0, tokens=SEQ)),
    ("nsa_proj", dict(chunks=20)),
    ("nsa_compress", dict(chunks=8)),
    ("nsa_attn", dict()),
    ("turn_out", dict()),
    ("proj_keep", dict(chunks=8)),
    ("norm", dict(gain="norm_g_2", gi=1, tokens=SEQ, into="add")),
    ("norm", dict(gain="norm_g_2", gi=2, tokens=SEQ)),
    ("dense", dict(chunks=2 * FFC, what="mlp", tokens=SEQ, n=FFC, early=0, layer=0)),
    ("norm", dict(gain="norm_g_2", gi=3, tokens=SEQ, into="add")),
    ("norm", dict(gain="norm_g_2", gi=4, tokens=SEQ)),
    ("fox_proj", dict(chunks=24)),
    ("fox_attn", dict()),
    ("turn_out", dict()),
    ("proj_keep", dict(chunks=8)),
    ("norm", dict(gain="norm_g_2", gi=5, tokens=SEQ, into="add")),
    ("norm", dict(gain="norm_g_2", gi=6, tokens=SEQ)),
    ("dense", dict(chunks=2 * FFC, what="mlp", tokens=SEQ, n=FFC, early=0, layer=0)),
    ("norm", dict(gain="norm_g_2", gi=7, tokens=SEQ, into="add")),
]


def lay_out_stages():
    out, n, seen = [], 0, {}
    bank_frees = rope_chunks = dense_steps = fused_steps = units = peer_tiles = gate_groups = early = 0
    for at, (kind, q) in enumerate(STAGES):
        s = dict(q, kind=kind, at=at, n0=n, k=seen.get(kind, 0), bf0=bank_frees, r0=rope_chunks, d0=dense_steps, a0=fused_steps, e0=early,
                 u0=units, pt0=peer_tiles, gg0=gate_groups)
        seen[kind] = s["k"] + 1
        n += q.get("chunks", 0)
        bank_frees += {"proj_add": 8, "proj_keep": 8, "peer_query": 16, "fox_proj": 16}.get(kind, 0)
        rope_chunks += {"kv_proj": 8, "q_proj": 8, "nsa_proj": 14}.get(kind, 0)
        if kind == "dense":
            dense_steps += q["n"]
            fused_steps += q["n"] - q["early"]
            early += q["early"]
        units += {"diff_attn": 16, "nsa_attn": 32, "fox_attn": 16}.get(kind, 0)
        if kind == "peer_select":
            peer_tiles += len(peer_token_tiles(q["tokens"]))
            gate_groups += q["tokens"] // 2
        out.append(s)
    return out


N_CHUNKS = sum(q.get("chunks", 0) for _, q in STAGES)


def peer_token_tiles(tokens):
    meta = tokens - SEQ
    return [(meta + P * i, P) for i in range(NT)] + ([(0, meta)] if meta else [])


def build_program(nc, dram, spill, out):
    stages = lay_out_stages()
    with ExitStack() as ctx:
        def sb(name, shape, dt=F32):
            return ctx.enter_context(nc.sbuf_tensor(name, shape, dt))

        def sem(name):
            return ctx.enter_context(nc.semaphore(name))

        h = sb("h", [P, NC, T0])
        x_hi = sb("x_hi", [P, NC, T0], F32R)
        x_lo = sb("x_lo", [P, NC, T0], F32R)
        ring = sb("ring", [P, CHUNK_SLOTS, D])
        vecs = sb("vecs", [P, NVEC])
        const_a = sb("const_a", [P, sum(n for _, n in CONST_A)])
        w_hi = sb("w_hi", [P, SPLITS, HALF], F32R)
        w_lo = sb("w_lo", [P, SPLITS, HALF], F32R)
        gated_hi = sb("gated_hi", [P, 2, T0], F32R)
        gated_lo = sb("gated_lo", [P, 2, T0], F32R)
        work = sb("work", [P, 1024])
        pick = sb("pick", [P, 3, T0])
        small = sb("small", [P, 96])
        arena = sb("arena", [P, ARENA])
        banks = ctx.enter_context(nc.psum_tensor("banks", [P, 8, 512], F32))

        cols = {}
        at = 0
        for name, n in CONST_A:
            cols[name] = const_a[:, at:at + n]
            at += n
        ident, ones, iota = cols["ident"], cols["ones"], cols["iota"]
        iota_cand = iota[:, 0:NCAND]

        class Carve:

            def __init__(self, at=0):
                self.at = at

            def __call__(self, *dims, dt=None):
                n = int(np.prod(dims))
                v = arena[:, self.at:self.at + n]
                self.at += n
                assert self.at <= ARENA
                if dt is not None:
                    v = v.bitcast(dt)
                if len(dims) == 2:
                    v = v.rearrange("p (a b) -> p a b", b=dims[1])
                if len(dims) == 3:
                    v = v.rearrange("p (a b c) -> p a b c", b=dims[1], c=dims[2])
                return v

        top = Carve(ARENA - (NC * T0 + 3 * T0))
        squares = top(NC, T0)
        root, rstd, mean = top(T0), top(T0), top(T0)
        cv = Carve()
        glu_u = cv(NC, CONV_W - 1 + T0)
        conv_y = cv(NC, T0)
        conv_odd = cv(NC, T0)
        glu_sig = cv(2, T0)
        products = cv(4, T0)
        taps = cv(CONV_W * NC)
        pv = Carve()
        peer_q = pv(16, T0)
        subkeys = pv(2, KEYS)
        tk = dict(vals=pv(16, 16), idx=pv(16, 16, dt=U32), idxf=pv(16, 16), rest=pv(16, KEYS),
                  cand=pv(HEADS, NCAND), cand_rest=pv(HEADS, NCAND), code=pv(HEADS, NCAND), best=pv(HEADS, TOPK),
                  pos=pv(HEADS, TOPK, dt=U32), posf=pv(HEADS, TOPK), hit=pv(HEADS * TOPK, NCAND),
                  picked=pv(P), pickedi=pv(P, dt=I32), k1i=pv(P, dt=I32), k2i=pv(P, dt=I32),
                  k1=pv(P), k2=pv(P), ex=pv(HEADS, TOPK), tot=pv(HEADS), inv=pv(HEADS), gate=pv(HEADS, TOPK))
        tile_scores_sb = [pv(16, KEYS) for _ in range(3)]
        ev = Carve(ARENA - (NC * T0 + 3 * T0) - 4 * D - 4 * T0)
        assert pv.at <= ev.at and ev.at >= 64 * GATE_LOOPS * KEYS
        early_ring = ev(4, D)
        early_act = ev(4, T0)
        spread = arena[:, :].rearrange("p (t k) -> p t k", k=KEYS)
        onehot1 = work[:, 0:512].rearrange("p (a t k) -> p a t k", a=2, t=2)
        onehot2 = work[:, 512:1024].rearrange("p (a t k) -> p a t k", a=2, t=2)
        act_out = work[:, 0:2 * T0].rearrange("p (a t) -> p a t", a=2)
        act_gated = work[:, 2 * T0:3 * T0]
        meta_rows = arena[:, 0:D]
        av = Carve()
        qT = av(NC, SEQ)
        kT = av(NC, T0)
        v_tok = av(3, D)
        raw = av(2, T0)
        rot = av(2, T0)
        probs = av(2, 3 * T0)
        probsT = av(2, 1024)
        o_tok = av(NT, D)
        o_sq = av(NT, D)
        mo = o_sq.rearrange("p t n -> p (t n)").rearrange("p (c t) -> p c t", c=NC)
        cb_at = av.at
        const_b = av(sum(n for _, n in CONST_B))
        lam_vecs = av(4, 64)
        subln_gain = av(P)
        lam_tmp = av(2, 64)
        set_b = {}
        at = cb_at
        for name, n in CONST_B:
            set_b[name] = arena[:, at:at + n]
            at += n
        cc = Carve(cb_at)
        cc_at = cc.at
        const_c = cc(sum(n for _, n in CONST_C))
        set_c = {}
        at = cc_at
        for name, n in CONST_C:
            set_c[name] = arena[:, at:at + n]
            at += n
        head_sel = set_c["head_sel"].rearrange("p (h t) -> p h t", t=SEQ)
        gate_w = set_c["gate_w"].rearrange("p (c n) -> p c n", c=NC)
        forget_w = set_c["forget_w"].rearrange("p (c n) -> p c n", c=NC)
        cmp_w2 = cc(2, 2, 64)
        cmp_w2d = cc(2, P)
        cmp_pos = cc(2, 2, 16)
        forget_b = cc(2)
        kcT, ksT, kwT, vcT = (cc(2, SEQ) for _ in range(4))
        blocks = [cc(16, GROUPS * NCMP) for _ in range(2)]
        blocks_hi, blocks_lo = ([x[:, 4 * kv:4 * kv + 4].rearrange("p c t -> p (c t)")[:, 0:16 * GROUPS * NCMP]
                                 .rearrange("p (l n) -> p l n", l=16) for kv in range(2)] for x in (x_hi, x_lo))
        hid = cc(2 * 2, 64)
        kcmpT = cc(64)
        vcmp = cc(GROUPS, 64)
        gates = cc(NT, 48)
        fz = cc(6, SEQ)
        o_mix_at = cc(2 * P)
        assert cc.at <= ARENA - (NC * T0 + 3 * T0)

        eps = small[:, 0:1]
        lam_sum, lam_exp, neg_lam = small[:, 2:4], small[:, 4:6], small[:, 6:7]
        row_max = small[:, 8:16].rearrange("p (a m) -> p a m", a=2)
        neg_max = small[:, 16:24].rearrange("p (a m) -> p a m", a=2)
        row_sum = small[:, 24:36].rearrange("p (a m) -> p a m", a=3)
        coef = small[:, 36:44].rearrange("p (a m) -> p a m", a=2)
        sub_ss, sub_root, sub_rstd = (small[:, 44 + 16 * i:60 + 16 * i] for i in range(3))
        o_mix = o_mix_at.rearrange("p (a b c) -> p a b c", a=1, b=2)

        chunk_landed = [sem(f"chunk_landed{i}") for i in range(CHUNK_SLOTS)]
        hi_ready, lo_ready = sem("hi_ready"), sem("lo_ready")
        half_used = sem("half_used")
        x_scaled, x_hi_ready = sem("x_scaled"), sem("x_hi_ready")
        subkeys_landed = sem("subkeys_landed")
        early_landed = [sem(f"early_landed{j}") for j in range(4)]
        early_summed, early_act_ready = sem("early_summed"), sem("early_act_ready")
        spill_stored = [sem(f"spill_stored{j}") for j in range(4)]
        spill_landed = [sem(f"spill_landed{j}") for j in range(2)]
        scores_stored = sem("scores_stored")
        meta_rows_ready, meta_turned = sem("meta_rows_ready"), sem("meta_turned")
        gated_hi_ready = sem("gated_hi_ready")
        gated_f32_ready = sem("gated_f32_ready")
        blocks_hi_ready, blocks_split = sem("blocks_hi_ready"), sem("blocks_split")
        inputs_landed = sem("inputs_landed")
        consts_b_landed = sem("consts_b_landed")
        consts_c_landed = sem("consts_c_landed")
        out_stored = sem("out_stored")
        stage_done = sem("stage_done")
        set_up = sem("set_up")
        dve_step = sem("dve_step")
        pool_step = sem("pool_step")
        act_step = sem("act_step")
        squares_ready, sum_ready, root_ready, rstd_ready = (sem(n) for n in (
            "squares_ready", "sum_ready", "root_ready", "rstd_ready"))
        bank_free = sem("bank_free")
        glu_gate_ready, glu_done = sem("glu_gate_ready"), sem("glu_done")
        product_ready = sem("product_ready")
        mean_summed, centred, var_summed, ln_root_ready, ln_scaled = (sem(n) for n in (
            "mean_summed", "centred", "var_summed", "ln_root_ready", "ln_scaled"))
        raw_ready, rot_ready, cos_ready, rope_done = (sem(n) for n in ("raw_ready", "rot_ready", "cos_ready", "rope_done"))
        tile_scores, index_ready, codes_ready, tops_ready, exps_ready, tile_picks, picks_turned, picks_stored = (
            sem(n) for n in ("tile_scores", "index_ready", "codes_ready", "tops_ready", "exps_ready", "tile_picks",
                             "picks_turned", "picks_stored"))
        onehots_ready, spread_summed, spread_stored = (sem(n) for n in (
            "onehots_ready", "spread_summed", "spread_stored"))
        act_ready, gated_ready = sem("act_ready"), sem("gated_ready")
        scores_ready, max_ready, exp_done, turned, turned_stored, av_done, mixed = (sem(n) for n in (
            "scores_ready", "max_ready", "exp_done", "turned", "turned_stored", "av_done", "mixed"))
        out_turned, out_hi_ready = sem("out_turned"), sem("out_hi_ready")
        sub_squared, sub_root_ready = sem("sub_squared"), sem("sub_root_ready")
        lam_exps = sem("lam_exps")
        lam_sums = sem("lam_sums")
        gates_summed = sem("gates_summed")
        cmp_blocks_ready = [sem("cmp_keys_ready"), sem("cmp_values_ready")]
        cmp_hidden_ready, cmp_out_summed = sem("cmp_hidden_ready"), sem("cmp_out_summed")
        forget_summed, forget_parts, forget_abs = sem("forget_summed"), sem("forget_parts"), sem("forget_abs")

        block = ctx.enter_context(nc.Block())

        def vec(name, i, c):
            n = VEC[name] + NC * i + c
            return vecs[:, n:n + 1]

        def slot_of(n):
            return n % CHUNK_SLOTS

        def half_of(n, half):
            return (2 * n + half) % SPLITS

        def raw_half(hn):
            return ring[:, slot_of(hn // 2), (hn % 2) * HALF:(hn % 2 + 1) * HALF]

        def plus(base, i, per):
            return base if i is None else i * per + base

        def split_hi(act, hn, i=None):
            if hn >= 2 * N_CHUNKS:
                return
            n = hn // 2
            act.wait_ge(chunk_landed[slot_of(n)], plus(16 * (n // CHUNK_SLOTS + 1), i, 16 * 8 // CHUNK_SLOTS))
            if hn >= SPLITS:
                act.wait_ge(half_used, plus(hn - SPLITS + 1, i, 16))
            act.activation(w_hi[:, hn % SPLITS], raw_half(hn), ACT.Copy).then_inc(hi_ready, 1)

        def split_lo(dve, hn, i=None):
            if hn >= 2 * N_CHUNKS:
                return
            dve.wait_ge(hi_ready, plus(hn + 1, i, 16))
            dve.tensor_tensor(w_lo[:, hn % SPLITS], raw_half(hn), w_hi[:, hn % SPLITS].bitcast(F32), ALU.subtract)\
               .then_inc(lo_ready, 1)

        def follow(split, eng, n, i=None):
            for half in range(2):
                split(eng, 2 * n + half + SPLITS, i)

        def tok_slice(tokens):
            return slice(T0 - tokens, T0)

        class Steps:

            def __init__(self, eng, sem_):
                self.eng, self.sem, self.n = eng, sem_, 0

            def mark(self, ins):
                ins.then_inc(self.sem, 1)
                self.n += 1
                return self.n

            def join(self, n=None):
                self.eng.wait_ge(self.sem, self.n if n is None else n)

            def link(self, ins):
                self.mark(ins)
                self.join()

        def end_stage(eng, s):
            eng.drain().then_inc(stage_done, 1)
            eng.wait_ge(stage_done, 4 * (s["at"] + 1))

        def stage_at(kind, k):
            return next(s["at"] for s in stages if s["kind"] == kind and s["k"] == k)

        DVE_NORM = 6
        POOL_CONV = (1, 3, 5)
        PRODUCTS = 4

        def pool_conv_step(n):
            return n + 1 + n // (CONV_W - 2)

        DVE_TAPS = [(c, w) for c in range(NC) if c not in POOL_CONV for w in range(CONV_W)]
        POOL_TAPS = [(c, w) for c in POOL_CONV for w in range(CONV_W)]
        DVE_BESIDE, POOL_BESIDE = 5, 4

        def dve_taps_beside(m):
            return DVE_TAPS[DVE_BESIDE * (m - 2):DVE_BESIDE * (m - 1)] if m >= 2 else []

        def pool_taps_beside(m):
            return POOL_TAPS[POOL_BESIDE * (m - 4):POOL_BESIDE * (m - 3)] if m >= 4 else []

        def conv_tap(eng, steps, c, w):
            sums = (conv_y[:, c], conv_odd[:, c])
            src, tap = glu_u[:, c, w:w + T0], taps[:, w * NC + c:w * NC + c + 1]
            o = sums[w % 2]
            if w >= 2:
                steps.join(steps.n - 1)
            if w == 0:
                eng.wait_ge(glu_done, c + 1)
                steps.mark(eng.tensor_scalar(o, src, tap, vec("a_dw_b", 0, c), ALU.mult, ALU.add))
            elif w == 1:
                steps.mark(eng.tensor_scalar(o, src, tap, None, ALU.mult))
            else:
                steps.mark(eng.scalar_tensor_tensor(out=o, in0=src, scalar=tap, in1=o, op0=ALU.mult, op1=ALU.add))
            if w == CONV_W - 1:
                steps.join()
                steps.mark(eng.tensor_tensor(sums[0], sums[0], sums[1], ALU.add))

        def scale_rows(eng, s, c, src):
            tk_ = tok_slice(s["tokens"])
            into = s.get("into")
            dst = mo[:, c] if into == "add" else h[:, c, tk_] if into == "h" else squares[:, c, tk_]
            return eng.scalar_tensor_tensor(out=dst, in0=src, scalar=vec(s["gain"], s["gi"], c), in1=rstd[:, tk_],
                                            op0=ALU.mult, op1=ALU.mult)

        head_sel_ones = ones[0:16, 0:1].broadcast_to([16, SEQ])

        def nsa_rope_dst(m):
            return qT[:, m] if m < 8 else (kcT, ksT, kwT)[(m - 8) // 2][:, m % 2]

        def block_rows(eng, kv):
            src = (kcT, vcT)[kv]
            dst = blocks[kv].rearrange("p l (g c) -> p l g c", g=GROUPS)
            for g in range(GROUPS):
                rows = slice(64 * (g % 2), 64 * (g % 2) + 64)
                tokens = src[rows, g // 2].rearrange("p (c l f) -> p l f c", l=8, f=2)
                for par in range(2):
                    for half in range(2):
                        ins = eng.tensor_tensor(
                            dst[64 * par:64 * par + 64, 8 * half:8 * half + 8, g],
                            tokens[:, :, par, half:half + NCMP],
                            cmp_pos[rows, kv, par, 8 * half:8 * half + 8].unsqueeze(2).broadcast_to([64, 8, NCMP]), ALU.add)
            return ins

        def attention_units(kind):
            units = []

            def map_(u, i, q, k, nk, bank, col, add):
                e = probs[:, u % 2, i * T0:i * T0 + nk]
                return dict(q=q, k=k, nk=nk, bank=bank, col=col, add=add, e=e, i=i)

            if kind == "diff_attn":
                for t in range(NT):
                    for hd in range(HEADS):
                        u = len(units)
                        nk = META + P * (t + 1)
                        maps = [map_(u, c, qT[64 * c:64 * c + 64, hd, t * P:(t + 1) * P], kT[64 * c:64 * c + 64, hd, 0:nk],
                                     nk, c, 0, [(ident, set_b["tri"], nk - P, P)]) for c in range(2)]
                        turns, stores, vals = [], [], [[], []]
                        full = nk // P
                        for c in range(2):
                            for kt in range(full + 1):
                                kn = P if kt < full else META
                                bank, col = (0, (c * full + kt) * P) if kt < full else (1, c * P)
                                turns.append((maps[c]["e"][:, kt * P:kt * P + kn], kn, bank, col))
                                vals[c].append((probsT[0:kn, u % 2, 512 * bank + col:512 * bank + col + P],
                                                v_tok[0:kn, kt, hd * P:(hd + 1) * P]))
                        stores = [(P, 0, 2 * full * P), (META, 1, 2 * P)]
                        units.append(dict(kind=kind, tile=t, maps=maps, turns=turns, stores=stores, values=vals, width=P,
                                          maxes=[(banks[:, 2 * (u % 2):2 * (u % 2) + 2, 0:nk], 0, 2)],
                                          out=o_tok[:, t, hd * P:(hd + 1) * P], nmaps=2))
            elif kind == "fox_attn":
                for t in range(NT):
                    for pr in range(8):
                        u = len(units)
                        nk = P * (t + 1)
                        maps = [map_(u, b, qT[64 * b:64 * b + 64, pr, t * P:(t + 1) * P], kT[64 * b:64 * b + 64, pr, 0:nk],
                                     nk, b, 0,
                                     [(fz[0:16, 4, t * P:(t + 1) * P], head_sel[0:16, 2 * pr + b, 0:nk], 0, nk),
                                      (head_sel[0:16, 2 * pr + b, 0:P], fz[0:16, 5, 0:nk], 0, nk),
                                      (ident, set_c["tri"], nk - P, P)]) for b in range(2)]
                        turns, vals = [], [[], []]
                        for b in range(2):
                            for kt in range(t + 1):
                                col = (b * (t + 1) + kt) * P
                                turns.append((maps[b]["e"][:, kt * P:(kt + 1) * P], P, 0, col))
                                hcol = (2 * pr + b) * 64
                                vals[b].append((probsT[:, u % 2, col:col + P], v_tok[:, kt, hcol:hcol + 64]))
                        sc = banks[:, 2 * (u % 2):2 * (u % 2) + 2, 0:nk]
                        units.append(dict(kind=kind, tile=t, maps=maps, turns=turns, stores=[(P, 0, 2 * (t + 1) * P)],
                                          values=vals, width=64, maxes=[(sc, 0, 2)],
                                          out=o_tok[:, t, pr * P:(pr + 1) * P].rearrange("p (b d) -> p b d", b=2), nmaps=2))
            else:
                for t in range(NT):
                    for pair in range(2):
                        for r in range(4):
                            for b in range(2):
                                u = len(units)
                                nk = P * (t + 1)
                                g, j = 2 * pair + b, 4 * pair + r
                                rows = slice(64 * b, 64 * b + 64)
                                q = qT[rows, j, t * P:(t + 1) * P]
                                tri = (ident, set_c["tri"], nk - P, P)
                                maps = [map_(u, 0, q, kcmpT[rows, g * NCMP:(g + 1) * NCMP], NCMP, 1, 0,
                                             [(ident, set_c["cmp_mask"][:, t * 16:t * 16 + NCMP], 0, NCMP)]),
                                        map_(u, 1, q, ksT[rows, pair, 0:nk], nk, 0, 0, [tri]),
                                        map_(u, 2, q, kwT[rows, pair, 0:nk], nk, 0, SEQ, [tri])]
                                turns = [(maps[0]["e"], NCMP, 1, 0)]
                                vals = [[(probsT[0:NCMP, u % 2, 512:512 + P], vcmp[0:NCMP, g, :])], [], []]
                                for i in (1, 2):
                                    for kt in range(t + 1):
                                        col = ((i - 1) * (t + 1) + kt) * P
                                        turns.append((maps[i]["e"][:, kt * P:(kt + 1) * P], P, 0, col))
                                        vc = (i - 1) * 256 + g * 64
                                        vals[i].append((probsT[:, u % 2, col:col + P], v_tok[:, kt, vc:vc + 64]))
                                sc = banks[:, 2 * (u % 2), :].rearrange("p (m n) -> p m n", m=2)[:, :, 0:nk]
                                cmp_sc = banks[:, 2 * (u % 2) + 1, 0:NCMP].unsqueeze(1)
                                units.append(dict(kind=kind, tile=t, maps=maps, turns=turns,
                                                  stores=[(P, 0, 2 * (t + 1) * P), (NCMP, 1, P)], values=vals, width=64,
                                                  maxes=[(cmp_sc, 0, 1), (sc, 1, 2)], head=4 * g + r, nmaps=3,
                                                  out=o_tok[:, t, j * P + b * 64:j * P + b * 64 + 64]))
            return units

        @block.sync
        def _(sp):
            sp.dma_start(h[:, :, :], dram["x"]).then_inc(inputs_landed, 16)
            sp.dma_start(vecs[:, :], dram["vecs"]).then_inc(inputs_landed, 16)
            sp.dma_start(const_a[:, :], dram["const_a"]).then_inc(inputs_landed, 16)
            sp.dma_start(taps, dram["taps"]).then_inc(inputs_landed, 16)

            def load(n, src):
                if n >= CHUNK_SLOTS:
                    sp.wait_ge(lo_ready, 2 * (n - CHUNK_SLOTS + 1))
                sp.dma_start(ring[:, slot_of(n), :], src).then_inc(chunk_landed[slot_of(n)], 16)

            def dense_stream(s, first, second):
                n0, early = s["n0"], s["early"]
                f0, fused = n0 + early, s["n"] - early

                def chunk(n, i=None):
                    if n < f0:
                        return second(plus(n - n0, i, 8))
                    m = n - f0
                    if m == 0:
                        return first(early)
                    if m == 2 * fused - 1:
                        return second(s["n"] - 1)
                    return (first if m % 2 else second)(plus(early + (m + 1) // 2 - (m % 2 == 0), i, 4))

                def load_in_loop(n, i):
                    sp.wait_ge(lo_ready, plus(2 * (n - CHUNK_SLOTS + 1), i, 16))
                    sp.dma_start(ring[:, slot_of(n), :], chunk(n, i)).then_inc(chunk_landed[slot_of(n)], 16)

                for n in range(n0, n0 + CHUNK_SLOTS):
                    load(n, chunk(n))
                if early:
                    early_stream(s, first)

                    def spilled(k, i=None):
                        if k >= 2 or i is not None:
                            sp.wait_ge(gated_f32_ready, plus(s["d0"] + k - 1, i, 8))
                        sp.dma_start(act_out[:, k % 2, 0:s["tokens"]], spill[bass.ds(plus(k, i, 8), 1), :, 0:s["tokens"]]
                                     .rearrange("a p n -> (a p) n")).then_inc(spill_landed[k % 2], 16)

                    sp.wait_ge(stage_done, 4 * s["at"])
                    spilled(0)
                    spilled(1)
                    for k in range(8):
                        spilled(k + 2)
                        load(n0 + k + 4, chunk(n0 + k + 4))
                    with sp.Fori(1, early // 8 - 1) as i:
                        for k in range(8):
                            spilled(k + 2, i)
                            load_in_loop(n0 + k + 4, i)
                    for k in range(early - 8, early):
                        if k + 2 < early:
                            spilled(k + 2)
                        load(n0 + k + 4, chunk(n0 + k + 4))
                for n in range(f0 + 4, f0 + 9):
                    load(n, chunk(n))
                with sp.Fori(1, fused // 4 - 1) as i:
                    for n in range(f0 + 1, f0 + 9):
                        load_in_loop(n, i)
                for n in range(f0 + 2 * fused - 7, f0 + 2 * fused):
                    load(n, chunk(n))

            def early_stream(s, first):
                e0, early = s["e0"], s["early"]

                def fetch(k, i=None):
                    sp.dma_start(early_ring[:, k % 4], first(plus(k, i, 4))).then_inc(early_landed[k % 4], 16)

                def store(k, i=None):
                    sp.wait_ge(early_act_ready, plus(e0 + k + 1, i, 4))
                    sp.dma_start(spill[bass.ds(plus(k, i, 4), 1), :, 0:s["tokens"]].rearrange("a p n -> (a p) n"),
                                 early_act[:, k % 4, 0:s["tokens"]]).then_inc(spill_stored[k % 4], 16)

                sp.wait_ge(stage_done, 4 * (s["at"] - 2))
                for k in range(4):
                    fetch(k)
                with sp.Fori(0, early // 4 - 1) as i:
                    for k in range(4):
                        store(k, i)
                        fetch(k + 4, i)
                for k in range(early - 4, early):
                    store(k)
                for j in range(4):
                    sp.wait_ge(spill_stored[j], 4 * (e0 + early))

            def row(ap, k):
                return ap[bass.ds(k, 1)].rearrange("a p n -> (a p) n")

            for s in stages:
                kind, n0, k = s["kind"], s["n0"], s["k"]
                if kind == "dense" and s["what"] == "peer":
                    u, v = dram["peer_u"][k], dram["peer_v"][k].rearrange("(a b) d -> b a d", b=KEYS)
                    dense_stream(s, lambda i: row(u, i), lambda i: row(v, i))
                elif kind == "dense":
                    up = dram["mlp_up"][k - 2]
                    down = dram["mlp_down"][k - 2].rearrange("(f p) d -> f p d", p=P)
                    dense_stream(s, lambda i: row(up, i), lambda i: row(down, i))
                elif s.get("chunks"):
                    src = dram[(kind, k)]
                    for m in range(s["chunks"]):
                        load(n0 + m, src[m])
            sp.wait_ge(stage_done, 4 * len(stages))
            sp.dma_start(out, h[:, :, META:T0]).then_inc(out_stored, 16)
            sp.wait_ge(out_stored, 16)

        @block.tensor
        def _(pe):
            def three(out, w_at, xh, xl, start, stop):
                for j, (w, x) in enumerate(((w_hi, xh), (w_hi, xl), (w_lo, xh))):
                    mm = pe.matmul(out, w_at(w), x, start=start and j == 0, stop=stop and j == 2, skip_group_check=True)
                return mm

            def project(n, bank, tokens, i=None):
                tk_ = tok_slice(tokens)
                for half in range(2):
                    pe.wait_ge(lo_ready, plus(2 * n + half + 1, i, 16))
                    for c in range(4):
                        cc_ = 4 * half + c
                        mm = three(banks[:, bank, 0:tokens], lambda w: w[:, half_of(n, half), c * P:(c + 1) * P],
                                   x_hi[:, cc_, tk_], x_lo[:, cc_, tk_], cc_ == 0, cc_ == NC - 1)
                    mm.then_inc(half_used, 1)

            def norm(s):
                tk_ = tok_slice(s["tokens"])
                for half in range(2):
                    pe.wait_ge(squares_ready, 2 * s["k"] + half + 1)
                    for c in range(4 * half, 4 * half + 4):
                        mm = pe.matmul(banks[:, 0, 0:s["tokens"]], ones, squares[:, c, tk_], start=c == 0, stop=c == NC - 1)
                mm.then_inc(sum_ready, 1)

            def conv_in(s):
                for m in range(16):
                    if m >= 4:
                        pe.wait_ge(glu_done, m // 2 - 1)
                    project(s["n0"] + m, m % 4, T0)

            def layernorm(s):
                for c in range(NC):
                    mm = pe.matmul(banks[:, 0, 0:T0], ones, conv_y[:, c], start=c == 0, stop=c == NC - 1)
                mm.then_inc(mean_summed, 1)
                pe.wait_ge(squares_ready, 2 * norm_runs + 1)
                for c in range(NC):
                    mm = pe.matmul(banks[:, 1, 0:T0], ones, squares[:, c], start=c == 0, stop=c == NC - 1)
                mm.then_inc(var_summed, 1)

            def proj(s, tokens):
                for m in range(s["chunks"]):
                    if m >= 4:
                        pe.wait_ge(bank_free, s["bf0"] + m - 3)
                    project(s["n0"] + m, m % 4, tokens)

            def peer_select(s):
                pe.wait_ge(subkeys_landed, 16 * (s["layer"] + 1))
                lo = T0 - s["tokens"]
                tiles = peer_token_tiles(s["tokens"])
                e0, tk_ = s["e0"], tok_slice(s["tokens"])

                def scores(i):
                    t0, n = tiles[i]
                    if s["pt0"] + i:
                        pe.wait_ge(scores_stored, s["pt0"] + i)
                    for m in range(16):
                        mm = pe.matmul(banks[0:n, m // 4, (m % 4) * KEYS:(m % 4 + 1) * KEYS], peer_q[:, m, lo + t0:lo + t0 + n],
                                       subkeys[:, m % 2, :], start=True, stop=True)
                    mm.then_inc(tile_scores, 1)

                def early(k, i=None, part=range(NC)):
                    if part[0] == 0:
                        pe.wait_ge(early_landed[k % 4], plus(16 * ((e0 + k) // 4 + 1), i, 16))
                        if k >= 2 or i is not None:
                            pe.wait_ge(early_act_ready, plus(e0 + k - 1, i, 4))
                    for c in part:
                        mm = pe.matmul(banks[:, 6 + k % 2, 0:s["tokens"]], early_ring[:, k % 4, c * P:(c + 1) * P],
                                       squares[:, c, tk_], start=c == 0, stop=c == NC - 1)
                    if part[-1] == NC - 1:
                        mm.then_inc(early_summed, 1)

                def turn(i):
                    t0, n = tiles[i]
                    pe.wait_ge(tile_picks, s["pt0"] + i + 1)
                    if i:
                        pe.wait_ge(picks_stored, s["pt0"] + i)
                    for j, src in enumerate((tk["k1"], tk["k2"], tk["gate"].rearrange("p a b -> p (a b)"))):
                        mm = pe.transpose(banks[:, 4, j * P:j * P + n], src[0:n, :], ident[0:n, 0:n])
                    mm.then_inc(picks_turned, 1)

                def group(g, i=None):
                    pe.wait_ge(onehots_ready, plus(s["gg0"] + g + 1, i, 32))
                    if g >= 2 or i is not None:
                        pe.wait_ge(spread_stored, plus(s["gg0"] + g - 1, i, 32))
                    for t in range(2):
                        mm = pe.matmul(banks[:, g % 2, t * KEYS:(t + 1) * KEYS], onehot1[:, g % 2, t], onehot2[:, g % 2, t],
                                       start=True, stop=True)
                    mm.then_inc(spread_summed, 1)

                for i in range(len(tiles)):
                    scores(i)
                done = 0
                for t, part in enumerate(s["early_parts"]):
                    if t == 0:
                        for k in range(4):
                            early(k)
                        done += 4
                        part -= 4
                    with pe.Fori(done // 4, (done + part) // 4) as i:
                        for k in range(4):
                            early(k, i)
                    done += part
                    turn(t)

                def both(i=None):
                    for g in range(32):
                        group(g, i)
                        early(done + g // 8, i, [g % 8])

                both()
                with pe.Fori(1, GATE_LOOPS) as i:
                    both(i)
                for g in range(32 * GATE_LOOPS, s["tokens"] // 2):
                    group(g)

            def dense(s):
                n0, d0, tokens, early = s["n0"], s["d0"], s["tokens"], s["early"]
                a0, steps = s["a0"], s["n"] - early
                meta = tokens - SEQ

                def up(b, n, freed, i=None):
                    if freed is not None:
                        pe.wait_ge(act_ready, plus(freed, i, 4))
                    project(n, 6 + b, tokens, i)

                def down(b, n, ready, first, last, i=None, per=4):
                    pe.wait_ge(gated_ready, plus(ready, i, per))
                    for half in range(2):
                        pe.wait_ge(lo_ready, plus(2 * n + half + 1, i, 16))
                        for c4 in range(4):
                            c = 4 * half + c4
                            at_ = lambda w: w[:, half_of(n, half), c4 * P:(c4 + 1) * P]
                            mm = three(banks[:, c // 2, (c % 2) * SEQ:(c % 2 + 1) * SEQ], at_, gated_hi[:, b, meta:tokens],
                                       gated_lo[:, b, meta:tokens], first and c % 2 == 0, last)
                        if meta:
                            for j, (x, w) in enumerate(((gated_hi, w_hi), (gated_lo, w_hi), (gated_hi, w_lo))):
                                mm = pe.matmul(banks[0:meta, 4 + half, :], x[:, b, 0:meta], w[:, half_of(n, half)],
                                               start=first and j == 0, stop=last and j == 2, skip_group_check=True)
                        mm.then_inc(half_used, 1)

                if early:
                    for k in range(8):
                        down(k % 2, n0 + k, d0 + k + 1, k == 0, False)
                    with pe.Fori(1, early // 8) as i:
                        for k in range(8):
                            down(k % 2, n0 + k, d0 + k + 1, False, False, i, 8)
                    n0 += early
                    d0 += early
                up(0, n0, None)
                for k in range(1, 5):
                    up(k % 2, n0 + 2 * k - 1, a0 + k - 1 if k >= 2 else None)
                    down((k - 1) % 2, n0 + 2 * k, d0 + k, k == 1 and not early, False)
                with pe.Fori(1, steps // 4 - 1) as i:
                    for j in range(4):
                        up((j + 1) % 2, n0 + 2 * j + 1, a0 + j, i)
                        down(j % 2, n0 + 2 * j + 2, d0 + j + 1, False, False, i)
                for k in range(steps - 3, steps):
                    up(k % 2, n0 + 2 * k - 1, a0 + k - 1)
                    down((k - 1) % 2, n0 + 2 * k, d0 + k, False, False)
                down((steps - 1) % 2, n0 + 2 * steps - 1, d0 + steps, False, True)
                if meta:
                    pe.wait_ge(meta_rows_ready, 1)
                    for c in range(NC):
                        mm = pe.transpose(banks[:, 6, c * META:(c + 1) * META], meta_rows[0:META, c * P:(c + 1) * P],
                                          ident[0:META, 0:META])
                    mm.then_inc(meta_turned, 1)

            def rope_projections(s, n0, m_count, tokens, mat, r_at=0):
                r0 = s["r0"] + r_at

                def rotate(m):
                    pe.wait_ge(raw_ready, r0 + m + 1)
                    if m >= 2:
                        pe.wait_ge(rope_done, r0 + m - 1)
                    pe.matmul(banks[:, 4 + m % 2, 0:tokens], mat, raw[:, m % 2, 0:tokens],
                              start=True, stop=True).then_inc(rot_ready, 1)

                for m in range(m_count):
                    if m >= 4:
                        pe.wait_ge(raw_ready, r0 + m - 3)
                    project(n0 + m, m % 4, tokens)
                    if m >= 1:
                        rotate(m - 1)
                rotate(m_count - 1)

            def values(n0, per_chunk, width, tiles, first_bank=0):
                halves = width // 512
                for n in range(NC // per_chunk):
                    for half in range(2):
                        pe.wait_ge(lo_ready, 2 * (n0 + n) + half + 1)
                        c = n * per_chunk + (half if per_chunk == 2 else 0)
                        at_ = half_of(n0 + n, half)
                        for i, (t0, m) in enumerate(tiles):
                            o = banks[0:m, first_bank + halves * i + (half if halves == 2 else 0), :]
                            for j, (x, w) in enumerate(((x_hi, w_hi), (x_lo, w_hi), (x_hi, w_lo))):
                                mm = pe.matmul(o, x[:, c, t0:t0 + m], w[:, at_], start=c == 0 and j == 0,
                                               stop=c == NC - 1 and j == 2, skip_group_check=True)
                        mm.then_inc(half_used, 1)

            def kv_proj(s):
                pe.wait_ge(consts_b_landed, 48)
                rope_projections(s, s["n0"], 8, T0, set_b["rope_mat"])
                pe.wait_ge(raw_ready, s["r0"] + 8)
                pe.wait_ge(rope_done, s["r0"] + 8)
                values(s["n0"] + 8, 1, D, [(0, P), (P, P), (2 * P, META)])

            def q_proj(s):
                rope_projections(s, s["n0"], 8, SEQ, set_b["rope_mat"])

            def nsa_proj(s):
                pe.wait_ge(consts_c_landed, 80)
                rope_projections(s, s["n0"], 14, SEQ, set_c["rope_mat"])
                pe.wait_ge(raw_ready, s["r0"] + 14)
                pe.wait_ge(rope_done, s["r0"] + 14)
                for m in range(2):
                    project(s["n0"] + 14 + m, m, SEQ)
                values(s["n0"] + 16, 2, 512, [(META + P * i, P) for i in range(NT)], first_bank=2)
                for i in range(NT):
                    for c in range(NC):
                        mm = pe.matmul(banks[:, 4 + i, 0:48], squares[:, c, META + P * i:META + P * (i + 1)], gate_w[:, c],
                                       start=c == 0, stop=c == NC - 1)
                mm.then_inc(gates_summed, 1)

            def nsa_compress(s):
                for kv in range(2):
                    pe.wait_ge(blocks_split, kv + 1)
                    for q in range(8):
                        n, half = s["n0"] + 4 * kv + q // 2, q % 2
                        pe.wait_ge(lo_ready, 2 * n + half + 1)
                        for j in range(2):
                            lp = 2 * q + j
                            for m in range(2):
                                mm = three(banks[:, 2 * kv + m, 0:GROUPS * NCMP],
                                           lambda w: w[:, half_of(n, half), j * 256 + m * P:j * 256 + (m + 1) * P],
                                           blocks_hi[kv][:, lp], blocks_lo[kv][:, lp], lp == 0, lp == 15)
                        mm.then_inc(half_used, 1)
                pe.wait_ge(cmp_hidden_ready, 1)
                for m in range(2):
                    pe.matmul(banks[:, 4, 0:GROUPS * NCMP], cmp_w2d[:, m], hid[:, m, 0:GROUPS * NCMP],
                              start=m == 0, stop=m == 1)
                for g in range(GROUPS):
                    for m in range(2):
                        mm = pe.matmul(banks[0:NCMP, 5, g * 64:(g + 1) * 64], hid[:, 2 + m, g * NCMP:(g + 1) * NCMP],
                                       cmp_w2[:, 1, m], start=m == 0, stop=m == 1, skip_group_check=True)
                mm.then_inc(cmp_out_summed, 1)

            def attend(s, units):
                u0 = s["u0"]

                def scores(u):
                    if u >= 2:
                        pe.wait_ge(exp_done, u0 + u - 1)
                    for mp in units[u]["maps"]:
                        o = banks[:, 2 * (u % 2) + mp["bank"], mp["col"]:mp["col"] + mp["nk"]]
                        mm = pe.matmul(o, mp["q"], mp["k"], start=True, stop=not mp["add"], skip_group_check=True)
                        for j, (lhsT, rhs, c0, w) in enumerate(mp["add"]):
                            mm = pe.matmul(o[:, c0:c0 + w], lhsT, rhs, start=False, stop=j == len(mp["add"]) - 1,
                                           skip_group_check=True)
                    mm.then_inc(scores_ready, 1)

                def turn(u):
                    pe.wait_ge(exp_done, u0 + u + 1)
                    if u >= 1:
                        pe.wait_ge(turned_stored, u0 + u)
                    for (src, kn, bank, col) in units[u]["turns"]:
                        mm = pe.transpose(banks[0:kn, 4 + bank, col:col + P], src, ident)
                    mm.then_inc(turned, 1)

                def weigh(u):
                    pe.wait_ge(turned_stored, u0 + u + 1)
                    if u >= 2:
                        pe.wait_ge(mixed, u0 + u - 1)
                    for i, parts in enumerate(units[u]["values"]):
                        for j, (lhsT, v) in enumerate(parts):
                            w = units[u]["width"]
                            mm = pe.matmul(banks[:, 6 + u % 2, i * w:(i + 1) * w], lhsT, v, start=j == 0,
                                           stop=j == len(parts) - 1, skip_group_check=True)
                    mm.then_inc(av_done, 1)

                for u in range(len(units) + 2):
                    if u < len(units):
                        scores(u)
                    if 1 <= u <= len(units):
                        turn(u - 1)
                    if u >= 2:
                        weigh(u - 2)

            def turn_out(s):
                for i in range(NT):
                    for half in range(2):
                        for c in range(4 * half, 4 * half + 4):
                            mm = pe.transpose(banks[:, 2 * i + half, (c % 4) * P:(c % 4 + 1) * P],
                                              o_tok[:, i, c * P:(c + 1) * P], ident)
                        mm.then_inc(out_turned, 1)

            def fox_proj(s):
                for m in range(16):
                    if m >= 4:
                        pe.wait_ge(bank_free, s["bf0"] + m - 3)
                    project(s["n0"] + m, m % 4, SEQ)
                for c in range(NC):
                    mm = pe.matmul(banks[0:16, 4, 0:SEQ], forget_w[:, c], squares[:, c, META:T0], start=c == 0, stop=c == NC - 1)
                mm.then_inc(forget_summed, 1)
                pe.wait_ge(bank_free, s["bf0"] + 16)
                values(s["n0"] + 16, 1, D, [(META + P * i, P) for i in range(NT)])

            pe.wait_ge(inputs_landed, 64)
            norm_runs = 0
            for s in stages:
                kind = s["kind"]
                if kind == "norm":
                    norm(dict(s, k=norm_runs))
                    norm_runs += 1
                elif kind == "layernorm":
                    layernorm(s)
                    norm_runs += 1
                elif kind == "conv_in":
                    conv_in(s)
                elif kind == "proj_add":
                    proj(s, s["tokens"])
                elif kind == "proj_keep":
                    proj(s, SEQ)
                elif kind == "peer_query":
                    proj(s, s["tokens"])
                elif kind in ("diff_attn", "nsa_attn", "fox_attn"):
                    attend(s, attention_units(kind))
                else:
                    dict(peer_select=peer_select, dense=dense, kv_proj=kv_proj, q_proj=q_proj,
                         nsa_proj=nsa_proj, nsa_compress=nsa_compress, turn_out=turn_out, fox_proj=fox_proj,
                         subln=lambda s: None, conv_taps=lambda s: None)[kind](s)
                end_stage(pe, s)

        @block.scalar
        def _(act):
            steps = Steps(act, act_step)
            norm_runs = 0

            def norm(s, src):
                tk_ = tok_slice(s["tokens"])
                for half in range(2):
                    act.activation(squares[:, 4 * half:4 * half + 4, tk_], src[:, 4 * half:4 * half + 4], ACT.Square)\
                       .then_inc(squares_ready, 1)
                act.wait_ge(sum_ready, s["k"] - ln_runs + 1)
                act.activation(root[:, tk_], banks[:, 0, 0:s["tokens"]], ACT.Sqrt, bias=eps, scale=1.0 / D)\
                   .then_inc(root_ready, 1)
                if not s.get("into"):
                    for c in range(NC):
                        act.wait_ge(x_scaled, 8 * s["xk"] + c + 1)
                        act.activation(x_hi[:, c, tk_], squares[:, c, tk_], ACT.Copy).then_inc(x_hi_ready, 1)

            def weigh_taps(list_):
                for c, w in list_:
                    if w == 0:
                        act.wait_ge(glu_done, c + 1)
                    n = POOL_CONV.index(c) * (CONV_W - 2) + w - 2
                    dst = (conv_y[:, c], conv_odd[:, c])[w] if w < 2 else products[:, n % PRODUCTS]
                    if w >= 2 and n >= PRODUCTS:
                        act.wait_ge(pool_step, pool_conv_step(n - PRODUCTS))
                    src, tap = glu_u[:, c, w:w + T0], taps[:, w * NC + c:w * NC + c + 1]
                    if w == 0:
                        act.activation(dst, src, ACT.Identity, bias=vec("a_dw_b", 0, c), scale=tap)
                    else:
                        ins = act.activation(dst, src, ACT.Copy, scale=tap)
                        if w >= 2:
                            ins.then_inc(product_ready, 1)

            def conv_in(s):
                for p_ in range(8):
                    for m in (2 * p_, 2 * p_ + 1):
                        follow(split_hi, act, s["n0"] + m)
                        weigh_taps(pool_taps_beside(m))
                    act.wait_ge(half_used, 2 * (s["n0"] + 2 * p_ + 2))
                    if p_ >= 2:
                        act.wait_ge(glu_done, p_ - 1)
                    act.activation(glu_sig[:, p_ % 2], banks[:, (2 * p_ + 1) % 4, 0:T0], ACT.Sigmoid,
                                   bias=vec("a_pw1_b", 1, p_)).then_inc(glu_gate_ready, 1)

            def conv_taps_(s):
                weigh_taps(POOL_TAPS[POOL_BESIDE * 12:])

            def layernorm(s):
                act.wait_ge(centred, 1)
                act.activation(squares[:, :, :], conv_y[:, :, :], ACT.Square).then_inc(squares_ready, 2)
                act.wait_ge(var_summed, 1)
                act.activation(root[:, :], banks[:, 1, 0:T0], ACT.Sqrt, bias=eps, scale=1.0 / D).then_inc(ln_root_ready, 1)
                for c in range(NC):
                    act.wait_ge(ln_scaled, c + 1)
                    steps.mark(act.activation(squares[:, c], squares[:, c], ACT.Silu, bias=vec("a_ln_b", 0, c),
                                              scale=vec("a_ln_g", 0, c)))
                steps.join()
                for c in range(NC):
                    act.activation(x_hi[:, c], squares[:, c], ACT.Copy).then_inc(x_hi_ready, 1)

            def keep(s, dst, tokens):
                for m in range(s["chunks"] if s["kind"] != "fox_proj" else 16):
                    follow(split_hi, act, s["n0"] + m)
                    act.wait_ge(half_used, 2 * (s["n0"] + m + 1))
                    act.activation(dst(m), banks[:, m % 4, 0:tokens], ACT.Copy).then_inc(bank_free, 1)

            def peer_select(s):
                tiles, e0 = peer_token_tiles(s["tokens"]), s["e0"]
                for i, (t0, n) in enumerate(tiles):
                    act.wait_ge(tile_scores, s["pt0"] + i + 1)
                    act.activation(tile_scores_sb[i][0:n].rearrange("p (a m) k -> p a (m k)", a=4), banks[0:n, 0:4, :],
                                   ACT.Copy).then_inc(scores_stored, 1)

                def early(k, i=None):
                    act.wait_ge(early_summed, plus(e0 + k + 1, i, 4))
                    if k >= 4 or i is not None:
                        act.wait_ge(spill_stored[k % 4], plus(16 * ((e0 + k) // 4), i, 16))
                    act.activation(early_act[:, k % 4, 0:s["tokens"]], banks[:, 6 + k % 2, 0:s["tokens"]], ACT.Gelu)\
                       .then_inc(early_act_ready, 1)

                def store(g, i=None):
                    act.wait_ge(spread_summed, plus(s["gg0"] + g + 1, i, 32))
                    at = plus(256 * g, i, 32 * 256)
                    act.activation(arena[:, bass.ds(at, 256)], banks[:, g % 2, 0:256], ACT.Copy).then_inc(spread_stored, 1)

                done = 0
                for t, part in enumerate(s["early_parts"]):
                    if t == 0:
                        for k in range(4):
                            early(k)
                        done += 4
                        part -= 4
                    with act.Fori(done // 4, (done + part - 4) // 4) as i:
                        for k in range(4):
                            early(k, i)
                    done += part
                    t0, n = tiles[t]
                    act.wait_ge(tops_ready, s["pt0"] + t + 1)
                    act.activation(tk["ex"][0:n], tk["ex"][0:n], ACT.Exp).then_inc(exps_ready, 1)
                    for k in range(done - 4, done):
                        early(k)
                    act.wait_ge(picks_turned, s["pt0"] + t + 1)
                    src = banks[:, 4, 0:3 * P].rearrange("p (j t) -> p j t", j=3)[:, :, 0:n]
                    act.activation(pick[:, :, t0:t0 + n], src, ACT.Copy).then_inc(picks_stored, 1)

                with act.Fori(0, GATE_LOOPS) as i:
                    for j in range(4):
                        for g in range(8 * j, 8 * j + 8):
                            store(g, i)
                        early(done + j, i)
                for j in range(4):
                    act.wait_ge(spill_stored[j], 4 * (e0 + done + 4 * GATE_LOOPS))
                for g in range(32 * GATE_LOOPS, s["tokens"] // 2):
                    store(g)

            def dense(s):
                n0, d0, tokens, early = s["n0"], s["d0"], s["tokens"], s["early"]
                steps_ = s["n"] - early
                func = ACT.Gelu if s["what"] == "peer" else ACT.Relu

                def one(b, k, n, freed, i=None):
                    if n > n0 or i is not None:
                        follow(split_hi, act, n, i)
                    act.wait_ge(half_used, plus(2 * n + 2, i, 16))
                    if freed is not None:
                        act.wait_ge(gated_f32_ready, plus(freed, i, 4))
                    act.activation(act_out[:, b, 0:tokens], banks[:, 6 + b, 0:tokens], func).then_inc(act_ready, 1)
                    if n > n0 or i is not None:
                        split_hi(act, 2 * (n + 1) + SPLITS, i)
                    act.wait_ge(gated_f32_ready, plus(d0 + k + 1, i, 4))
                    act.activation(gated_hi[:, b, 0:tokens], act_gated[:, 0:tokens], ACT.Copy).then_inc(gated_hi_ready, 1)
                    if n > n0 or i is not None:
                        split_hi(act, 2 * (n + 1) + 1 + SPLITS, i)

                def early_one(k, i=None):
                    if k >= 2 or i is not None:
                        split_hi(act, 2 * (n0 + k - 2) + SPLITS, i)
                    act.wait_ge(gated_f32_ready, plus(d0 + k + 1, i, 8))
                    if k >= 2 or i is not None:
                        act.wait_ge(half_used, plus(2 * (n0 + k - 1), i, 16))
                    act.activation(gated_hi[:, k % 2, 0:tokens], act_gated[:, 0:tokens], ACT.Copy).then_inc(gated_hi_ready, 1)
                    if k >= 2 or i is not None:
                        split_hi(act, 2 * (n0 + k - 2) + 1 + SPLITS, i)

                if early:
                    for k in range(8):
                        early_one(k)
                    with act.Fori(1, early // 8) as i:
                        for k in range(8):
                            early_one(k, i)
                    n0 += early
                    d0 += early
                    follow(split_hi, act, n0 - 2)
                    follow(split_hi, act, n0 - 1)
                follow(split_hi, act, n0)
                one(0, 0, n0, None)
                for k in range(1, 5):
                    one(k % 2, k, n0 + 2 * k - 1, d0 + k - 1 if k >= 2 else None)
                with act.Fori(1, steps_ // 4 - 1) as i:
                    for k in range(1, 5):
                        one(k % 2, k, n0 + 2 * k - 1, d0 + k - 1, i)
                for k in range(steps_ - 3, steps_):
                    one(k % 2, k, n0 + 2 * k - 1, d0 + k - 1)
                follow(split_hi, act, n0 + 2 * steps_ - 1)

            def rope(s, n0, m_count, tokens, r_at=0):
                r0 = s["r0"] + r_at
                for m in range(m_count):
                    follow(split_hi, act, n0 + m)
                    act.wait_ge(half_used, 2 * (n0 + m + 1))
                    if m >= 2:
                        act.wait_ge(rope_done, r0 + m - 1)
                    act.activation(raw[:, m % 2, 0:tokens], banks[:, m % 4, 0:tokens], ACT.Copy).then_inc(raw_ready, 1)

            def kv_proj(s):
                rope(s, s["n0"], 8, T0)
                for m in range(8, 16):
                    follow(split_hi, act, s["n0"] + m)
                act.wait_ge(half_used, 2 * (s["n0"] + 16))
                for i, m in enumerate((P, P, META)):
                    act.activation(v_tok[0:m, i, 0:512], banks[0:m, 2 * i, :], ACT.Copy)

            def diff_lambda():
                act.wait_ge(lam_sums, 1)
                act.activation(lam_exp, lam_sum, ACT.Exp).then_inc(lam_exps, 1)

            def nsa_proj(s):
                rope(s, s["n0"], 14, SEQ)
                for m in range(2):
                    follow(split_hi, act, s["n0"] + 14 + m)
                    act.wait_ge(half_used, 2 * (s["n0"] + 14 + m + 1))
                    act.activation(vcT[:, m], banks[:, m, 0:SEQ], ACT.Copy)
                for m in range(16, 20):
                    follow(split_hi, act, s["n0"] + m)
                act.wait_ge(gates_summed, 1)
                act.activation(gates[:, :, :], banks[:, 4:6, 0:48], ACT.Sigmoid)

            def nsa_compress(s):
                for kv in range(2):
                    act.wait_ge(cmp_blocks_ready[kv], 1)
                    act.activation(blocks_hi[kv], blocks[kv], ACT.Copy).then_inc(blocks_hi_ready, 1)
                for kv in range(2):
                    for m in range(4):
                        follow(split_hi, act, s["n0"] + 4 * kv + m)
                    act.wait_ge(half_used, 2 * (s["n0"] + 4 * kv + 4))
                    ins = act.activation(hid[:, 2 * kv:2 * kv + 2, 0:GROUPS * NCMP],
                                         banks[:, 2 * kv:2 * kv + 2, 0:GROUPS * NCMP], ACT.Silu)
                ins.then_inc(cmp_hidden_ready, 1)
                act.wait_ge(cmp_out_summed, 1)
                act.activation(kcmpT[:, 0:GROUPS * NCMP], banks[:, 4, 0:GROUPS * NCMP], ACT.Copy)
                act.activation(vcmp[0:NCMP, :, :], banks[0:NCMP, 5, 0:256].rearrange("p (g d) -> p g d", g=GROUPS), ACT.Copy)

            def attend(s, units):
                u0 = s["u0"]

                def store(u):
                    act.wait_ge(turned, u0 + u + 1)
                    if u >= 2:
                        act.wait_ge(av_done, u0 + u - 1)
                    for rows, bank, width in units[u]["stores"]:
                        ins = act.activation(probsT[0:rows, u % 2, 512 * bank:512 * bank + width],
                                             banks[0:rows, 4 + bank, 0:width], ACT.Copy)
                    ins.then_inc(turned_stored, 1)

                for u in range(len(units) + 1):
                    if u < len(units):
                        act.wait_ge(max_ready, u0 + u + 1)
                        if u >= 2:
                            act.wait_ge(turned, u0 + u - 1)
                        if u >= 3:
                            act.wait_ge(mixed, u0 + u - 2)
                        for mp in units[u]["maps"]:
                            i = mp["i"]
                            ins = act.activation(mp["e"], banks[:, 2 * (u % 2) + mp["bank"], mp["col"]:mp["col"] + mp["nk"]],
                                                 ACT.Exp, bias=neg_max[:, u % 2, i:i + 1], scale=SCALE,
                                                 accum_out=row_sum[:, u % 3, i:i + 1])
                        ins.then_inc(exp_done, 1)
                    if u >= 1:
                        store(u - 1)

            def subln(s):
                act.wait_ge(sub_squared, 1)
                act.activation(sub_root, sub_ss, ACT.Sqrt, bias=eps, scale=1.0 / P).then_inc(sub_root_ready, 1)

            def turn_out(s):
                for i in range(NT):
                    for half in range(2):
                        act.wait_ge(out_turned, 4 * s["k"] + 2 * i + half + 1)
                        act.activation(x_hi[:, 4 * half:4 * half + 4, META + i * P:META + (i + 1) * P],
                                       banks[:, 2 * i + half, :].rearrange("p (c t) -> p c t", c=4), ACT.Copy)\
                           .then_inc(out_hi_ready, 1)

            def fox_proj(s):
                keep(s, lambda m: qT[:, m] if m < 8 else kT[:, m - 8, 0:SEQ], SEQ)
                act.wait_ge(forget_parts, 1)
                steps.link(act.activation(fz[0:16, 1], fz[0:16, 0], ACT.Abs))
                steps.link(act.activation(fz[0:16, 1], fz[0:16, 1], ACT.Exp, scale=-1.0))
                act.activation(fz[0:16, 2], fz[0:16, 1], ACT.Ln, bias=1.0).then_inc(forget_abs, 1)
                for m in range(16, 24):
                    follow(split_hi, act, s["n0"] + m)
                act.wait_ge(half_used, 2 * (s["n0"] + 24))
                for i in range(NT):
                    act.activation(v_tok[:, i, 0:512], banks[:, 2 * i, :], ACT.Copy)

            act.wait_ge(inputs_landed, 64)
            act.wait_ge(set_up, 2)
            ln_runs = x_runs = 0
            for hn in range(SPLITS):
                split_hi(act, hn)
            for s in stages:
                kind = s["kind"]
                if kind == "norm":
                    norm(dict(s, k=norm_runs, xk=x_runs), mo if s.get("into") == "add" else h[:, :, tok_slice(s["tokens"])])
                    norm_runs += 1
                    x_runs += not s.get("into")
                elif kind == "layernorm":
                    layernorm(s)
                    norm_runs += 1
                    ln_runs += 1
                elif kind == "proj_add":
                    for m in range(s["chunks"]):
                        follow(split_hi, act, s["n0"] + m)
                elif kind == "proj_keep":
                    keep(s, lambda m: mo[:, m], SEQ)
                elif kind == "peer_query":
                    keep(s, lambda m, s=s: peer_q[:, m, tok_slice(s["tokens"])], s["tokens"])
                elif kind == "q_proj":
                    rope(s, s["n0"], 8, SEQ)
                    diff_lambda()
                elif kind in ("diff_attn", "nsa_attn", "fox_attn"):
                    attend(s, attention_units(kind))
                else:
                    dict(conv_in=conv_in, peer_select=peer_select, dense=dense, kv_proj=kv_proj,
                         nsa_proj=nsa_proj, nsa_compress=nsa_compress, turn_out=turn_out, fox_proj=fox_proj,
                         subln=subln, conv_taps=conv_taps_)[kind](s)
                end_stage(act, s)

        @block.vector
        def _(dve):
            steps = Steps(dve, dve_step)

            def norm(s):
                tk_ = tok_slice(s["tokens"])
                dve.wait_ge(root_ready, s["k"] + 1)
                dve.reciprocal(rstd[:, tk_], root[:, tk_]).then_inc(rstd_ready, 1)
                dve.wait_ge(rstd_ready, s["k"] + 1)
                if not s.get("into"):
                    for c in range(NC):
                        scale_rows(dve, s, c, h[:, c, tk_]).then_inc(x_scaled, 1)
                    return
                for c in range(DVE_NORM):
                    steps.mark(scale_rows(dve, s, c, mo[:, c] if s.get("into") == "add" else h[:, c, tk_]))
                if s.get("into") == "add":
                    steps.join()
                    dve.tensor_tensor(h[:, 0:DVE_NORM, tk_], h[:, 0:DVE_NORM, tk_], mo[:, 0:DVE_NORM], ALU.add)

            def conv_in(s):
                for p_ in range(8):
                    for m in (2 * p_, 2 * p_ + 1):
                        follow(split_lo, dve, s["n0"] + m)
                        for c, w in dve_taps_beside(m):
                            conv_tap(dve, steps, c, w)
                    dve.wait_ge(glu_gate_ready, p_ + 1)
                    dve.scalar_tensor_tensor(out=glu_u[:, p_, CONV_W - 1:], in0=banks[:, (2 * p_) % 4, 0:T0],
                                             scalar=vec("a_pw1_b", 0, p_), in1=glu_sig[:, p_ % 2],
                                             op0=ALU.add, op1=ALU.mult).then_inc(glu_done, 1)

            def layernorm(s):
                dve.wait_ge(mean_summed, 1)
                steps.link(dve.tensor_scalar(mean[:, :], banks[:, 0, 0:T0], 1.0 / D, None, ALU.mult))
                dve.tensor_tensor(conv_y[:, :, :], conv_y[:, :, :], mean.unsqueeze(1).broadcast_to([P, NC, T0]),
                                  ALU.subtract).then_inc(centred, 1)
                dve.wait_ge(ln_root_ready, 1)
                steps.link(dve.reciprocal(rstd[:, :], root[:, :]))
                for c in range(NC):
                    dve.tensor_tensor(squares[:, c], conv_y[:, c], rstd[:, :], ALU.mult).then_inc(ln_scaled, 1)

            def proj_add(s):
                tk_ = tok_slice(s["tokens"])
                for m in range(8):
                    follow(split_lo, dve, s["n0"] + m)
                    dve.wait_ge(half_used, 2 * (s["n0"] + m + 1))
                    src, dst = banks[:, m % 4, 0:s["tokens"]], h[:, m, tk_]
                    if s["bias"]:
                        ins = dve.scalar_tensor_tensor(out=dst, in0=src, scalar=vec("a_pw2_b", 0, m), in1=dst,
                                                       op0=ALU.add, op1=ALU.add)
                    else:
                        ins = dve.tensor_tensor(dst, src, dst, ALU.add)
                    ins.then_inc(bank_free, 1)

            def top16(n, src, vals, idx, rest, count):
                for m in range(count):
                    steps.mark(dve.max(vals[0:n, m, 0:8], src(m)))
                steps.join()
                for m in range(count):
                    steps.mark(dve.max_index(idx[0:n, m, 0:8], vals[0:n, m, 0:8], src(m)))
                    steps.mark(dve.match_replace(rest[0:n, m], vals[0:n, m, 0:8], src(m), LOWEST))
                steps.join()
                for m in range(count):
                    steps.mark(dve.max(vals[0:n, m, 8:16], rest[0:n, m]))
                steps.join()
                for m in range(count):
                    last = dve.max_index(idx[0:n, m, 8:16], vals[0:n, m, 8:16], rest[0:n, m])
                    if m < count - 1:
                        steps.mark(last)
                return last

            def peer_topk(s):
                for i, (t0, n) in enumerate(peer_token_tiles(s["tokens"])):
                    k = s["pt0"] + i
                    dve.wait_ge(scores_stored, k + 1)
                    src = lambda m: tile_scores_sb[i][0:n, m]
                    if i:
                        dve.wait_ge(codes_ready, k)
                    top16(n, src, tk["vals"], tk["idx"], tk["rest"], 16).then_inc(index_ready, 1)
                    at = 0
                    v = tk["vals"][0:n].rearrange("p (h f) r -> p h f r", f=2)
                    for a, na, nb in CAND_ROWS:
                        o = tk["cand"][0:n, :, at:at + na * nb].rearrange("p h (a b) -> p h a b", b=nb)
                        steps.mark(dve.tensor_tensor(o, v[:, :, 0, a:a + na].unsqueeze(3).broadcast_to([n, HEADS, na, nb]),
                                                     v[:, :, 1, 0:nb].unsqueeze(2).broadcast_to([n, HEADS, na, nb]), ALU.add))
                        at += na * nb
                    steps.join()
                    steps.link(top16(n, lambda m: tk["cand"][0:n, m], tk["best"], tk["pos"], tk["cand_rest"], HEADS))
                    best = tk["best"][0:n]
                    dve.tensor_tensor(tk["ex"][0:n], best, best[:, :, 0:1].broadcast_to([n, HEADS, TOPK]), ALU.subtract)\
                       .then_inc(tops_ready, 1)
                    steps.link(dve.tensor_copy(tk["posf"][0:n], tk["pos"][0:n]))
                    hit = tk["hit"][0:n]
                    flat = tk["posf"][0:n].rearrange("p h j -> p (h j)")
                    steps.link(dve.tensor_tensor(hit, iota_cand[0:n].unsqueeze(1).broadcast_to([n, P, NCAND]),
                                                 flat.unsqueeze(2).broadcast_to([n, P, NCAND]), ALU.is_equal))
                    dve.wait_ge(codes_ready, k + 1)
                    hit4 = hit.rearrange("p (h j) c -> p h j c", h=HEADS)
                    steps.link(dve.tensor_tensor(hit4, hit4, tk["code"][0:n].unsqueeze(2).broadcast_to([n, HEADS, TOPK, NCAND]),
                                                 ALU.mult))
                    steps.link(dve.reduce_sum(tk["picked"][0:n], hit, AX_X))
                    steps.link(dve.tensor_copy(tk["pickedi"][0:n], tk["picked"][0:n]))
                    if i:
                        dve.wait_ge(picks_turned, k)
                    steps.mark(dve.tensor_scalar(tk["k1i"][0:n], tk["pickedi"][0:n], 7, None, ALU.logical_shift_right))
                    steps.link(dve.tensor_scalar(tk["k2i"][0:n], tk["pickedi"][0:n], 127, None, ALU.bitwise_and))
                    steps.mark(dve.tensor_copy(tk["k1"][0:n], tk["k1i"][0:n]))
                    steps.mark(dve.tensor_copy(tk["k2"][0:n], tk["k2i"][0:n]))
                    dve.wait_ge(exps_ready, k + 1)
                    steps.link(dve.reduce_sum(tk["tot"][0:n], tk["ex"][0:n], AX_X))
                    steps.link(dve.reciprocal(tk["inv"][0:n], tk["tot"][0:n]))
                    dve.tensor_tensor(tk["gate"][0:n], tk["ex"][0:n],
                                      tk["inv"][0:n].unsqueeze(2).broadcast_to([n, HEADS, TOPK]), ALU.mult)\
                       .then_inc(tile_picks, 1)

            def peer_select(s):
                peer_topk(s)
                dve.wait_ge(picks_stored, s["pt0"] + len(peer_token_tiles(s["tokens"])))

                def groups(i, first=False):
                    for b in range(2):
                        if not first:
                            dve.wait_ge(spread_summed, i * 2 + (b + s["gg0"] - 1))
                        at = i * 4 + 2 * b
                        dve.tensor_tensor(onehot1[:, b], iota.unsqueeze(1).broadcast_to([P, 2, KEYS]),
                                          pick[:, 0, bass.ds(at, 2)].unsqueeze(2).broadcast_to([P, 2, KEYS]), ALU.is_equal)
                        for t in range(2):
                            at = i * 4 + (2 * b + t)
                            ins = dve.tensor_scalar(onehot2[:, b, t], iota, pick[:, 1, bass.ds(at, 1)],
                                                    pick[:, 2, bass.ds(at, 1)], ALU.is_equal, ALU.mult)
                        ins.then_inc(onehots_ready, 1)

                groups(0, first=True)
                with dve.Fori(1, s["tokens"] // 4) as i:
                    groups(i)

            def dense(s):
                n0, d0, tokens, early = s["n0"], s["d0"], s["tokens"], s["early"]
                a0, steps_ = s["a0"], s["n"] - early
                meta = tokens - SEQ

                def gate(b, step):
                    a, o = act_out[:, b, 0:tokens], act_gated[:, 0:tokens]
                    g = spread[:, 0:tokens, bass.ds(step, 1)].rearrange("p t k -> p (t k)") if s["what"] == "peer" else a
                    dve.tensor_tensor(o, a, g, ALU.mult).then_inc(gated_f32_ready, 1)

                def gated_rest(b):
                    dve.tensor_tensor(gated_lo[:, b, 0:tokens], act_gated[:, 0:tokens], gated_hi[:, b, 0:tokens].bitcast(F32),
                                      ALU.subtract).then_inc(gated_ready, 1)

                def early_one(k, i=None):
                    if k >= 2 or i is not None:
                        split_lo(dve, 2 * (n0 + k - 2) + SPLITS, i)
                    dve.wait_ge(spill_landed[k % 2], plus(8 * s["e0"] + 16 * (k // 2 + 1), i, 64))
                    if k >= 1 or i is not None:
                        dve.wait_ge(gated_ready, plus(d0 + k, i, 8))
                    gate(k % 2, plus(k, i, 8))
                    dve.wait_ge(gated_hi_ready, plus(d0 + k + 1, i, 8))
                    gated_rest(k % 2)
                    if k >= 2 or i is not None:
                        split_lo(dve, 2 * (n0 + k - 2) + 1 + SPLITS, i)

                if early:
                    for k in range(8):
                        early_one(k)
                    with dve.Fori(1, early // 8) as i:
                        for k in range(8):
                            early_one(k, i)
                    n0 += early
                    d0 += early
                    follow(split_lo, dve, n0 - 2)
                    follow(split_lo, dve, n0 - 1)

                def one(b, k, n, i=None):
                    if n > n0 or i is not None:
                        follow(split_lo, dve, n, i)
                    dve.wait_ge(act_ready, plus(a0 + k + 1, i, 4))
                    if k >= 1 or early:
                        dve.wait_ge(gated_ready, plus(d0 + k, i, 4))
                    gate(b, plus(early + k, i, 4))
                    if n > n0 or i is not None:
                        split_lo(dve, 2 * (n + 1) + SPLITS, i)
                    dve.wait_ge(gated_hi_ready, plus(d0 + k + 1, i, 4))
                    gated_rest(b)
                    if n > n0 or i is not None:
                        split_lo(dve, 2 * (n + 1) + 1 + SPLITS, i)

                follow(split_lo, dve, n0)
                one(0, 0, n0)
                for k in range(1, 5):
                    one(k % 2, k, n0 + 2 * k - 1)
                with dve.Fori(1, steps_ // 4 - 1) as i:
                    for k in range(1, 5):
                        one(k % 2, k, n0 + 2 * k - 1, i)
                for k in range(steps_ - 3, steps_):
                    one(k % 2, k, n0 + 2 * k - 1)
                follow(split_lo, dve, n0 + 2 * steps_ - 1)
                dve.wait_ge(half_used, 2 * (n0 + 2 * steps_))
                if meta:
                    dve.tensor_copy(meta_rows[0:META, :].rearrange("p (a n) -> p a n", a=2), banks[0:META, 4:6, :])\
                       .then_inc(meta_rows_ready, 1)
                dst = h[:, :, META:T0] if s["what"] == "peer" else mo
                for b in range(4):
                    src = banks[:, b, :].rearrange("p (c t) -> p c t", c=2)
                    if s["what"] == "peer":
                        dve.tensor_tensor(dst[:, 2 * b:2 * b + 2], dst[:, 2 * b:2 * b + 2], src, ALU.add)
                    else:
                        dve.tensor_copy(dst[:, 2 * b:2 * b + 2], src)
                if meta:
                    dve.wait_ge(meta_turned, 1)
                    dve.tensor_tensor(h[:, :, 0:META], h[:, :, 0:META],
                                      banks[:, 6, 0:NC * META].rearrange("p (c t) -> p c t", c=NC), ALU.add)

            def rope(s, m_count, tokens, dst, sin):
                for m in range(m_count):
                    follow(split_lo, dve, s["n0"] + m)
                    dve.wait_ge(rot_ready, s["r0"] + m + 1)
                    steps.link(dve.tensor_tensor(rot[:, m % 2, 0:tokens], banks[:, 4 + m % 2, 0:tokens], sin, ALU.mult))
                    dve.wait_ge(cos_ready, s["r0"] + m + 1)
                    dve.tensor_tensor(dst(m), dst(m), rot[:, m % 2, 0:tokens], ALU.add).then_inc(rope_done, 1)

            def kv_proj(s):
                dve.wait_ge(consts_b_landed, 48)
                rope(s, 8, T0, lambda m: kT[:, m], set_b["rope_sin"])
                for m in range(8, 16):
                    follow(split_lo, dve, s["n0"] + m)
                dve.wait_ge(half_used, 2 * (s["n0"] + 16))
                for i, m in enumerate((P, P, META)):
                    dve.tensor_copy(v_tok[0:m, i, 512:1024], banks[0:m, 2 * i + 1, :])

            def q_proj(s):
                for j in range(2):
                    steps.link(dve.tensor_tensor(lam_tmp[:, j], lam_vecs[:, 2 * j], lam_vecs[:, 2 * j + 1], ALU.mult))
                dve.reduce_sum(lam_sum, lam_tmp, AX_X).then_inc(lam_sums, 1)
                rope(s, 8, SEQ, lambda m: qT[:, m], set_b["rope_sin"][:, META:T0])
                dve.wait_ge(lam_exps, 1)
                steps.link(dve.tensor_tensor(neg_lam, lam_exp[:, 1:2], lam_exp[:, 0:1], ALU.subtract))
                steps.link(dve.tensor_scalar(neg_lam, neg_lam, -LAM_INIT, None, ALU.add))

            def nsa_proj(s):
                dve.wait_ge(consts_c_landed, 80)
                rope(s, 14, SEQ, nsa_rope_dst, set_c["rope_sin"])
                for m in range(14, 20):
                    follow(split_lo, dve, s["n0"] + m)
                dve.wait_ge(half_used, 2 * (s["n0"] + 20))
                for i in range(NT):
                    dve.tensor_copy(v_tok[:, i, 0:512], banks[:, 2 + i, :])

            def nsa_compress(s):
                steps.link(dve.tensor_scalar(gates[:, 0, :].rearrange("p (h i) -> p h i", i=3)[:, :, 0],
                                             gates[:, 0, :].rearrange("p (h i) -> p h i", i=3)[:, :, 0],
                                             set_c["row_ok"][:, 0:1], None, ALU.mult))
                block_rows(dve, 0).then_inc(cmp_blocks_ready[0], 1)
                for kv in range(2):
                    dve.wait_ge(blocks_hi_ready, kv + 1)
                    dve.tensor_tensor(blocks_lo[kv], blocks[kv], blocks_hi[kv].bitcast(F32), ALU.subtract)\
                       .then_inc(blocks_split, 1)
                for m in range(8):
                    follow(split_lo, dve, s["n0"] + m)

            def attend(s, units):
                u0 = s["u0"]

                def mix(u):
                    un = units[u]
                    n, w = un["nmaps"], un["width"]
                    part = lambda i: banks[:, 6 + u % 2, i * w:(i + 1) * w]
                    cf, sums = coef[:, u % 2, 0:n], row_sum[:, u % 3, 0:n]
                    dve.wait_ge(av_done, u0 + u + 1)
                    steps.link(dve.reciprocal(cf, sums))
                    if un["kind"] == "fox_attn":
                        for i in range(2):
                            ins = dve.tensor_scalar(un["out"][:, i], part(i), cf[:, i:i + 1], None, ALU.mult)
                    elif un["kind"] == "diff_attn":
                        steps.link(dve.tensor_tensor(cf[:, 1:2], cf[:, 1:2], neg_lam, ALU.mult))
                        steps.link(dve.tensor_scalar(o_mix[:, 0, 0], part(1), cf[:, 1:2], None, ALU.mult))
                        ins = dve.scalar_tensor_tensor(out=un["out"], in0=part(0), scalar=cf[:, 0:1], in1=o_mix[:, 0, 0],
                                                       op0=ALU.mult, op1=ALU.add)
                    else:
                        hd = un["head"]
                        steps.link(dve.tensor_tensor(cf, cf, gates[:, un["tile"], 3 * hd:3 * hd + 3], ALU.mult))
                        steps.link(dve.tensor_scalar(o_mix[:, 0, 0, 0:w], part(0), cf[:, 0:1], None, ALU.mult))
                        steps.link(dve.scalar_tensor_tensor(out=o_mix[:, 0, 1, 0:w], in0=part(1), scalar=cf[:, 1:2],
                                                            in1=o_mix[:, 0, 0, 0:w], op0=ALU.mult, op1=ALU.add))
                        ins = dve.scalar_tensor_tensor(out=un["out"], in0=part(2), scalar=cf[:, 2:3],
                                                       in1=o_mix[:, 0, 1, 0:w], op0=ALU.mult, op1=ALU.add)
                    ins.then_inc(mixed, 1)

                for u in range(len(units) + 2):
                    if u < len(units):
                        un = units[u]
                        dve.wait_ge(scores_ready, u0 + u + 1)
                        if u >= 2:
                            dve.wait_ge(exp_done, u0 + u - 1)
                        for src, c0, n in un["maxes"]:
                            steps.mark(dve.reduce_max(row_max[:, u % 2, c0:c0 + n], src, AX_X))
                        steps.join()
                        n = un["nmaps"]
                        dve.tensor_scalar(neg_max[:, u % 2, 0:n], row_max[:, u % 2, 0:n], -SCALE, None, ALU.mult)\
                           .then_inc(max_ready, 1)
                    if u >= 2:
                        mix(u - 2)

            def subln(s):
                o3 = o_tok.rearrange("p t (h e) -> p (t h) e", h=HEADS)
                sq3 = o_sq.rearrange("p t (h e) -> p (t h) e", h=HEADS)
                full = [P, NT * HEADS, P]
                steps.link(dve.tensor_tensor(sq3, o3, o3, ALU.mult))
                dve.reduce_sum(sub_ss, sq3, AX_X).then_inc(sub_squared, 1)
                dve.wait_ge(sub_root_ready, 1)
                steps.link(dve.reciprocal(sub_rstd, sub_root))
                steps.link(dve.tensor_scalar(lam_tmp.rearrange("p a b -> p (a b)"), subln_gain, 1.0 - LAM_INIT, None, ALU.mult))
                steps.link(dve.tensor_tensor(o3, o3, sub_rstd.unsqueeze(2).broadcast_to(full), ALU.mult))
                steps.link(dve.tensor_tensor(o3, o3, lam_tmp.rearrange("p a b -> p (a b)").unsqueeze(1).broadcast_to(full), ALU.mult))

            def turn_out(s):
                for i in range(NT):
                    for half in range(2):
                        cs, ts = slice(4 * half, 4 * half + 4), slice(META + i * P, META + (i + 1) * P)
                        dve.wait_ge(out_hi_ready, 4 * s["k"] + 2 * i + half + 1)
                        dve.tensor_tensor(x_lo[:, cs, ts], banks[:, 2 * i + half, :].rearrange("p (c t) -> p c t", c=4),
                                          x_hi[:, cs, ts].bitcast(F32), ALU.subtract)

            def fox_proj(s):
                for m in range(16):
                    follow(split_lo, dve, s["n0"] + m)
                dve.wait_ge(forget_summed, 1)
                steps.link(dve.tensor_scalar(fz[0:16, 0], banks[0:16, 4, 0:SEQ], forget_b[0:16, 0:1], None, ALU.add))
                dve.tensor_scalar(fz[0:16, 3], fz[0:16, 0], 0.0, None, ALU.min).then_inc(forget_parts, 1)
                dve.wait_ge(forget_abs, 1)
                steps.link(dve.tensor_tensor(fz[0:16, 3], fz[0:16, 3], fz[0:16, 2], ALU.subtract))
                steps.link(dve.tensor_tensor_scan(fz[0:16, 2], head_sel_ones, fz[0:16, 3], 0.0, ALU.mult, ALU.add))
                steps.mark(dve.tensor_scalar(fz[0:16, 4], fz[0:16, 2], 1.0 / SCALE, None, ALU.mult))
                steps.mark(dve.tensor_scalar(fz[0:16, 5], fz[0:16, 2], -1.0 / SCALE, None, ALU.mult))
                for m in range(16, 24):
                    follow(split_lo, dve, s["n0"] + m)
                dve.wait_ge(half_used, 2 * (s["n0"] + 24))
                for i in range(NT):
                    dve.tensor_copy(v_tok[:, i, 512:1024], banks[:, 2 * i + 1, :])

            dve.memset(eps, EPS).then_inc(set_up, 1)
            dve.memset(small[:, 95:96], 0.0).then_inc(set_up, 1)
            dve.wait_ge(inputs_landed, 64)
            norm_runs = 0
            for hn in range(SPLITS):
                split_lo(dve, hn)
            for s in stages:
                kind = s["kind"]
                if kind == "norm":
                    norm(dict(s, k=norm_runs))
                    norm_runs += 1
                elif kind in ("diff_attn", "nsa_attn", "fox_attn"):
                    attend(s, attention_units(kind))
                elif kind in ("proj_keep", "peer_query"):
                    for m in range(s["chunks"]):
                        follow(split_lo, dve, s["n0"] + m)
                elif kind == "conv_taps":
                    for c, w in DVE_TAPS[DVE_BESIDE * 14:]:
                        conv_tap(dve, steps, c, w)
                else:
                    dict(conv_in=conv_in, layernorm=layernorm, peer_select=peer_select, dense=dense,
                         kv_proj=kv_proj, q_proj=q_proj, nsa_proj=nsa_proj, nsa_compress=nsa_compress,
                         fox_proj=fox_proj, subln=subln, proj_add=proj_add, turn_out=turn_out)[kind](s)
                end_stage(dve, s)

        @block.gpsimd
        def _(pool):
            steps = Steps(pool, pool_step)

            def remainder(tk_, k):
                for c in range(NC):
                    pool.wait_ge(x_hi_ready, 8 * k + c + 1)
                    pool.tensor_tensor(x_lo[:, c, tk_], squares[:, c, tk_], x_hi[:, c, tk_].bitcast(F32), ALU.subtract)

            def norm(s):
                tk_ = tok_slice(s["tokens"])
                into = s.get("into")
                if not into:
                    remainder(tk_, s["xk"])
                    return
                dst = src = mo if into == "add" else h[:, :, tk_]
                pool.wait_ge(rstd_ready, s["k"] + 1)
                for c in range(DVE_NORM, NC):
                    steps.mark(pool.tensor_scalar(dst[:, c], src[:, c], vec(s["gain"], s["gi"], c), None, ALU.mult))
                steps.join()
                for c in range(DVE_NORM, NC):
                    steps.mark(pool.tensor_tensor(dst[:, c], dst[:, c], rstd[:, tk_], ALU.mult))
                if s.get("into") == "add":
                    steps.join()
                    pool.tensor_tensor(h[:, DVE_NORM:, tk_], h[:, DVE_NORM:, tk_], mo[:, DVE_NORM:], ALU.add)

            def sum_taps(list_):
                for c, w in list_:
                    sums = (conv_y[:, c], conv_odd[:, c])
                    if w >= 2:
                        n = POOL_CONV.index(c) * (CONV_W - 2) + w - 2
                        pool.wait_ge(product_ready, n + 1)
                        if w >= 4:
                            steps.join(steps.n - 1)
                        steps.mark(pool.tensor_tensor(sums[w % 2], sums[w % 2], products[:, n % PRODUCTS], ALU.add))
                    if w == CONV_W - 1:
                        steps.join()
                        steps.mark(pool.tensor_tensor(sums[0], sums[0], sums[1], ALU.add))

            def peer_topk(s):
                for i, (t0, n) in enumerate(peer_token_tiles(s["tokens"])):
                    k = s["pt0"] + i
                    pool.wait_ge(index_ready, k + 1)
                    steps.link(pool.tensor_copy(tk["idxf"][0:n], tk["idx"][0:n]))
                    f = tk["idxf"][0:n].rearrange("p (h f) r -> p h f r", f=2)
                    steps.link(pool.tensor_scalar(f[:, :, 0], f[:, :, 0], float(KEYS), None, ALU.mult))
                    if i:
                        pool.wait_ge(tile_picks, k)
                    at = 0
                    for a, na, nb in CAND_ROWS:
                        o = tk["code"][0:n, :, at:at + na * nb].rearrange("p h (a b) -> p h a b", b=nb)
                        ins = pool.tensor_tensor(o, f[:, :, 0, a:a + na].unsqueeze(3).broadcast_to([n, HEADS, na, nb]),
                                                 f[:, :, 1, 0:nb].unsqueeze(2).broadcast_to([n, HEADS, na, nb]), ALU.add)
                        at += na * nb
                    ins.then_inc(codes_ready, 1)

            def rope(s, m_count, tokens, dst, cos):
                for m in range(m_count):
                    pool.wait_ge(raw_ready, s["r0"] + m + 1)
                    pool.tensor_tensor(dst(m), raw[:, m % 2, 0:tokens], cos, ALU.mult).then_inc(cos_ready, 1)

            pool.wait_ge(inputs_landed, 64)
            pool.memset(glu_u[:, :, 0:CONV_W - 1], 0.0)
            norm_runs = x_runs = 0
            for s in stages:
                kind = s["kind"]
                if kind == "norm" and s["gain"] == "kv_norm_g":
                    pool.dma_start(const_b, dram["const_b"]).then_inc(consts_b_landed, 16)
                    pool.dma_start(lam_vecs, dram["lam_vecs"]).then_inc(consts_b_landed, 16)
                    pool.dma_start(subln_gain, dram["subln_gain"]).then_inc(consts_b_landed, 16)
                if kind == "norm" and s["gain"] == "final_norm_g":
                    pool.dma_start(const_c, dram["const_c"]).then_inc(consts_c_landed, 16)
                    pool.dma_start(cmp_w2, dram["cmp_w2"]).then_inc(consts_c_landed, 16)
                    pool.dma_start(cmp_w2d, dram["cmp_w2d"]).then_inc(consts_c_landed, 16)
                    pool.dma_start(cmp_pos, dram["cmp_pos"]).then_inc(consts_c_landed, 16)
                    pool.dma_start(forget_b[0:16, 0:1], dram["forget_b"]).then_inc(consts_c_landed, 16)
                if kind == "peer_query":
                    pool.dma_start(subkeys, dram["subkeys"][:, 2 * s["layer"]:2 * s["layer"] + 2])\
                        .then_inc(subkeys_landed, 16)
                if kind == "norm":
                    norm(dict(s, k=norm_runs, xk=x_runs))
                    norm_runs += 1
                    x_runs += not s.get("into")
                elif kind == "layernorm":
                    remainder(slice(0, T0), x_runs)
                    x_runs += 1
                elif kind == "conv_taps":
                    sum_taps(POOL_TAPS[POOL_BESIDE * 12:])
                elif kind == "conv_in":
                    sum_taps(POOL_TAPS[:POOL_BESIDE * 12])
                elif kind == "peer_select":
                    peer_topk(s)
                elif kind == "kv_proj":
                    pool.wait_ge(consts_b_landed, 48)
                    rope(s, 8, T0, lambda m: kT[:, m], set_b["rope_cos"])
                elif kind == "q_proj":
                    rope(s, 8, SEQ, lambda m: qT[:, m], set_b["rope_cos"][:, META:T0])
                elif kind == "nsa_proj":
                    pool.wait_ge(consts_c_landed, 80)
                    rope(s, 14, SEQ, nsa_rope_dst, set_c["rope_cos"])
                elif kind == "nsa_compress":
                    block_rows(pool, 1).then_inc(cmp_blocks_ready[1], 1)
                end_stage(pool, s)



def rope_constants(rotated, half, theta, n_tokens, first=0):
    inv = np.float32(theta) ** (-np.arange(0, rotated, 2, dtype=np.float32) / np.float32(rotated))
    ang = np.arange(n_tokens, dtype=np.float32)[:, None] * inv.astype(np.float32)[None, :]
    cos = np.ones((P, n_tokens), np.float32)
    sin = np.zeros((P, n_tokens), np.float32)
    mat = np.zeros((P, P), np.float32)
    for base in (0, 64):
        for f in range(half):
            for p in (base + f, base + half + f):
                cos[p], sin[p] = np.cos(ang[:, f]), np.sin(ang[:, f])
            mat[base + half + f, base + f] = -1.0
            mat[base + f, base + half + f] = 1.0
    return mat, cos, sin


def shape_constants():
    ident = np.eye(P, dtype=np.float32)
    iota = np.broadcast_to(np.arange(P, dtype=np.float32), (P, P))
    q = np.arange(P)
    tri = np.where(q[None, :] <= q[:, None], 0.0, NEG).astype(np.float32)
    a = np.concatenate([ident, np.ones((P, P), np.float32), iota], axis=1)
    m, c, s = rope_constants(16, 8, 500000.0, T0)
    b = np.concatenate([m, c, s, tri], axis=1)
    m, c, s = rope_constants(64, 32, 10000.0, SEQ)
    ends = np.arange(16) * CMP_STEP + CMP_L - 1
    cmp_mask = np.concatenate([np.where(ends[None, :] <= (t * P + q)[:, None], 0.0, NEG) for t in range(NT)], axis=1)
    row_ok = np.repeat((q >= CMP_L - 1).astype(np.float32)[:, None], 2, axis=1)
    sel = np.zeros((P, 16, SEQ), np.float32)
    for i in range(16):
        sel[i, i] = 1.0
    cc = np.concatenate([m, c, s, tri, cmp_mask.astype(np.float32), row_ok, sel.reshape(P, -1)], axis=1)
    return tuple(np.ascontiguousarray(x, dtype=np.float32) for x in (a, b, cc))


def kernel(**inputs):
    import concourse.bacc as _bacc
    from concourse.bass_utils import run_bass_kernel_spmd as _run

    g = {k: np.asarray(v) for k, v in inputs.items()}

    def by_chunk(w):
        m = w.shape[1] // P
        return w.reshape(NC, P, m, P).transpose(2, 1, 0, 3).reshape(m, P, D)

    def feature_major(x):
        return x.T.reshape(NC, P, -1).transpose(1, 0, 2)

    def head_order():
        return [4 * (2 * pair + b) + r for pair in range(2) for r in range(4) for b in range(2)]

    arrays = {}
    arrays["x"] = feature_major(np.concatenate([g["meta_tokens"], g["x"][0]], axis=0))
    arrays["vecs"] = np.concatenate([g[n].reshape(k * NC, P) for n, k in VEC_LIST], axis=0).T
    arrays["taps"] = g["a_dw_w"].reshape(CONV_W * NC, P).T
    arrays["const_a"], arrays["const_b"], arrays["const_c"] = shape_constants()
    arrays["subkeys"] = np.stack([g["f_subkey1"], g["f_subkey2"]], axis=1).reshape(4, KEYS, P).transpose(2, 0, 1)
    nsa, fox = g["nsa_w_in_2"][0], g["fox_w_in_2"][0]
    arrays["const_c"] = np.concatenate([
        arrays["const_c"], nsa[:, 2560:2608].reshape(NC, P, 48).transpose(1, 0, 2).reshape(P, -1),
        fox[:, 3072:3088].reshape(NC, P, 16).transpose(1, 0, 2).reshape(P, -1)], axis=1)
    arrays["forget_b"] = g["fox_b_f_2"].reshape(16, 1)
    lam = np.stack([g[f"b_lambda_{n}"][0] for n in ("q1", "k1", "q2", "k2")])
    arrays["lam_vecs"] = np.repeat(lam[None], P, axis=0)
    arrays["subln_gain"] = np.repeat(g["b_subln_g"], P, axis=0)
    w2 = g["nsa_cmp_w2_2"][0].reshape(2, 2, P, 64)
    arrays["cmp_w2"] = w2.transpose(2, 0, 1, 3)
    arrays["cmp_w2d"] = np.concatenate([w2[0], w2[0]], axis=2).transpose(1, 0, 2)
    pos = g["nsa_cmp_pos_2"][0].reshape(2, 16, 2, 64).transpose(3, 0, 2, 1)
    arrays["cmp_pos"] = np.concatenate([pos, pos], axis=0)
    arrays["peer_u"] = g["f_u"].reshape(2, KEYS, KEYS, NC, P).transpose(0, 2, 4, 3, 1).reshape(2, KEYS, P, D)
    arrays["peer_v"] = g["f_v"]
    arrays["mlp_up"] = np.stack([by_chunk(w) for w in g["mlp_w_up_2"]])
    arrays["mlp_down"] = g["mlp_w_down_2"]

    order = head_order()
    heads = nsa[:, 0:1024].reshape(D, 16, 64)[:, order].reshape(D, D)
    kc, vc, ks, vs, kw, vw = (nsa[:, 1024 + 256 * i:1280 + 256 * i] for i in range(6))
    pw1 = by_chunk(g["a_pw1_w"][0])
    streams = {
        ("conv_in", 0): pw1.reshape(2, NC, P, D).transpose(1, 0, 2, 3).reshape(16, P, D),
        ("proj_add", 0): by_chunk(g["a_pw2_w"][0]),
        ("peer_query", 0): by_chunk(g["f_wq"][0]),
        ("kv_proj", 0): np.concatenate([by_chunk(g["w_kv"][:, 0:D]), g["w_kv"][:, D:].reshape(NC, P, D)]),
        ("q_proj", 0): by_chunk(g["b_wq"][0]),
        ("proj_add", 1): by_chunk(g["b_wo"][0]),
        ("peer_query", 1): by_chunk(g["f_wq"][1]),
        ("nsa_proj", 0): np.concatenate([
            by_chunk(np.concatenate([heads, kc, ks, kw, vc], axis=1)),
            np.concatenate([vs, vw], axis=1).reshape(4, 2, P, 512).transpose(0, 2, 1, 3).reshape(4, P, D)]),
        ("nsa_compress", 0): g["nsa_cmp_w1_2"][0].reshape(2, 4, 4, P, 256).transpose(0, 1, 3, 2, 4).reshape(8, P, D),
        ("proj_keep", 0): by_chunk(g["nsa_w_out_2"][0].reshape(16, 64, D)[order].reshape(D, D)),
        ("fox_proj", 0): np.concatenate([by_chunk(fox[:, 0:2048]), fox[:, 2048:3072].reshape(NC, P, D)]),
        ("proj_keep", 1): by_chunk(g["fox_w_out_2"][0]),
    }

    nc = _bacc.Bacc("TRN2", target_bir_lowering=False, num_devices=1)
    dram, feeds = {}, {}

    def declare(key, name, a):
        a = np.ascontiguousarray(a)
        feeds[name] = a
        dram[key] = nc.dram_tensor(name, a.shape, mybir.dt.from_np(a.dtype), kind="ExternalInput").ap()

    for name, a in arrays.items():
        declare(name, f"in_{name}", a)
    for (kind, k), a in streams.items():
        declare((kind, k), f"w_{kind}_{k}", a)
    out = nc.dram_tensor("out_features", [P, NC, SEQ], F32, kind="ExternalOutput").ap()
    spill = nc.dram_tensor("spill", [max(EARLY), P, T0], F32, kind="Internal").ap()
    build_program(nc, dram, spill, out)
    r = _run(nc, [feeds], core_ids=[0])
    y = r.results[0]["out_features"]
    return np.ascontiguousarray(y.transpose(2, 1, 0).reshape(1, SEQ, D))
```
